# Optimizing a Trainium2 kernel written in Bass

```python
import math
import jax, jax.numpy as jnp
from jax import lax
import numpy as np

D_MODEL = 2048
BATCH = 1
SEQ = 512
DEPTH = 1

D_MIX = D_MODEL
SSM_WIDTH = D_MIX // 2
SSM_GROUP = 16
SSM_GROUPS = SSM_WIDTH // SSM_GROUP
SSM_STATE = 64
SSM_CHUNK = 128
DIFF_WIDTH = D_MIX // 4
DIFF_HEADS = 4
DIFF_HEAD_DIM = DIFF_WIDTH // (2 * DIFF_HEADS)
DIFF_V_DIM = 2 * DIFF_HEAD_DIM
XATTN_WIDTH = D_MIX - SSM_WIDTH - DIFF_WIDTH
XATTN_HEADS = 4
XATTN_HEAD_DIM = XATTN_WIDTH // XATTN_HEADS
MEM_TOKENS = 256
ROPE_THETA = 10000.0
Q_BLOCK = 128
NORM_EPS = 1e-6
MASK_VALUE = -1e30


def rmsnorm(x, g):
    x32 = x.astype(jnp.float32)
    var = jnp.mean(x32 * x32, axis=-1, keepdims=True)
    return (x32 * lax.rsqrt(var + NORM_EPS) * g.astype(jnp.float32)).astype(x.dtype)

def rope_tables(positions, dim):
    inv = ROPE_THETA ** (-jnp.arange(0, dim, 2, dtype=jnp.float32) / dim)
    ang = positions.astype(jnp.float32)[..., None] * inv
    return jnp.cos(ang), jnp.sin(ang)

def apply_rope(x, cos, sin):
    extra = x.ndim - 3
    shp = cos.shape[:2] + (1,) * extra + cos.shape[-1:]
    c, s = cos.reshape(shp), sin.reshape(shp)
    x1, x2 = jnp.split(x.astype(jnp.float32), 2, axis=-1)
    return jnp.concatenate([x1 * c - x2 * s, x2 * c + x1 * s], axis=-1).astype(x.dtype)

def s5_scan(u, a_re, a_im, log_dt, b_re, b_im, c_re, c_im, d_skip):
    f32 = jnp.float32
    bsz, seq = u.shape[0], u.shape[1]
    n_chunks = seq // SSM_CHUNK
    dt = jnp.exp(log_dt.astype(f32))[:, None]
    lr, li = a_re.astype(f32), a_im.astype(f32)
    mag = jnp.exp(lr * dt)
    abar_re, abar_im = mag * jnp.cos(li * dt), mag * jnp.sin(li * dt)
    den = lr * lr + li * li
    nr, ni = abar_re - 1.0, abar_im
    z_re = (nr * lr + ni * li) / den
    z_im = (ni * lr - nr * li) / den
    br, bi = b_re.astype(f32), b_im.astype(f32)
    bbar_re = z_re[..., None] * br - z_im[..., None] * bi
    bbar_im = z_re[..., None] * bi + z_im[..., None] * br
    cr, ci = c_re.astype(f32), c_im.astype(f32)

    uc = u.astype(f32).reshape(bsz, n_chunks, SSM_CHUNK, SSM_GROUPS, SSM_GROUP)
    uc = uc.transpose(1, 2, 0, 3, 4)
    a_el_re = jnp.broadcast_to(abar_re[None, None], (SSM_CHUNK, 1, SSM_GROUPS, SSM_STATE))
    a_el_im = jnp.broadcast_to(abar_im[None, None], (SSM_CHUNK, 1, SSM_GROUPS, SSM_STATE))

    def combine(e1, e2):
        a1r, a1i, b1r, b1i = e1
        a2r, a2i, b2r, b2i = e2
        return (a2r * a1r - a2i * a1i,
                a2r * a1i + a2i * a1r,
                a2r * b1r - a2i * b1i + b2r,
                a2r * b1i + a2i * b1r + b2i)

    def chunk_step(carry, u_t):
        h_re, h_im = carry
        bu_re = jnp.einsum('tbgh,gph->tbgp', u_t, bbar_re)
        bu_im = jnp.einsum('tbgh,gph->tbgp', u_t, bbar_im)
        pa_re, pa_im, s_re, s_im = lax.associative_scan(
            combine, (a_el_re, a_el_im, bu_re, bu_im), axis=0)
        x_re = s_re + pa_re * h_re - pa_im * h_im
        x_im = s_im + pa_re * h_im + pa_im * h_re
        y = jnp.einsum('tbgp,ghp->tbgh', x_re, cr) - jnp.einsum('tbgp,ghp->tbgh', x_im, ci)
        return (x_re[-1], x_im[-1]), y

    h0 = (jnp.zeros((bsz, SSM_GROUPS, SSM_STATE), f32), jnp.zeros((bsz, SSM_GROUPS, SSM_STATE), f32))
    _, ys = lax.scan(chunk_step, h0, uc)
    y = ys.transpose(2, 0, 1, 3, 4).reshape(bsz, seq, SSM_WIDTH)
    y = y + d_skip.astype(f32).reshape(SSM_WIDTH) * u.astype(f32)
    return y.astype(u.dtype)

def diff_attention(q, k, v, lam, lambda_init, subln_g):
    bsz, seq = q.shape[0], q.shape[1]
    n_blocks = seq // Q_BLOCK
    scale = DIFF_HEAD_DIM ** -0.5
    k_pos = jnp.arange(seq)
    qb = q.reshape(bsz, n_blocks, Q_BLOCK, DIFF_HEADS, 2, DIFF_HEAD_DIM).transpose(1, 0, 2, 3, 4, 5)

    def block(args):
        qi, blk = args
        s = jnp.einsum('bqhcd,bkhcd->bhcqk', qi, k).astype(jnp.float32) * scale
        q_pos = blk * Q_BLOCK + jnp.arange(Q_BLOCK)
        mask = k_pos[None, :] <= q_pos[:, None]
        s = jnp.where(mask, s, MASK_VALUE)
        p = jax.nn.softmax(s, axis=-1)
        w = p[:, :, 0] - lam * p[:, :, 1]
        return jnp.einsum('bhqk,bkhd->bqhd', w.astype(v.dtype), v)

    o = lax.map(block, (qb, jnp.arange(n_blocks)))
    o = o.transpose(1, 0, 2, 3, 4).reshape(bsz, seq, DIFF_HEADS, DIFF_V_DIM)
    o = rmsnorm(o, subln_g) * (1.0 - lambda_init)
    return o.reshape(bsz, seq, DIFF_WIDTH)

def memory_attention(q, mem_n, w_mem_kv):
    bsz, seq = q.shape[0], q.shape[1]
    kv = mem_n @ w_mem_kv
    mk, mv = jnp.split(kv, 2, axis=-1)
    mk = mk.reshape(bsz, MEM_TOKENS, XATTN_HEADS, XATTN_HEAD_DIM)
    mv = mv.reshape(bsz, MEM_TOKENS, XATTN_HEADS, XATTN_HEAD_DIM)
    s = jnp.einsum('bqhd,bmhd->bhqm', q, mk).astype(jnp.float32) * (XATTN_HEAD_DIM ** -0.5)
    p = jax.nn.softmax(s, axis=-1).astype(mv.dtype)
    o = jnp.einsum('bhqm,bmhd->bqhd', p, mv)
    return o.reshape(bsz, seq, XATTN_WIDTH)

def first_inputs(seed: int = 0) -> dict:
    key = jax.random.key(seed)
    ks = jax.random.split(key, 24)
    f32 = jnp.float32
    in_cols = 2 * SSM_WIDTH + 4 * DIFF_WIDTH + 2 * XATTN_WIDTH
    nrm = lambda k, shp, s: jax.random.normal(k, shp, f32) * s
    x = jax.random.normal(ks[0], (BATCH, SEQ, D_MODEL), f32)
    mem = jax.random.normal(ks[1], (BATCH, MEM_TOKENS, D_MODEL), f32)
    positions = jnp.broadcast_to(jnp.arange(SEQ, dtype=jnp.int32), (BATCH, SEQ))
    norm_pre = 1.0 + nrm(ks[2], (DEPTH, D_MODEL), 0.02)
    norm_post = 1.0 + nrm(ks[3], (DEPTH, D_MODEL), 0.02)
    norm_mem = 1.0 + nrm(ks[4], (DEPTH, D_MODEL), 0.02)
    w_in = nrm(ks[5], (DEPTH, D_MODEL, in_cols), D_MODEL ** -0.5)
    w_out = nrm(ks[6], (DEPTH, D_MIX, D_MODEL), D_MIX ** -0.5)
    w_mem_kv = nrm(ks[7], (DEPTH, D_MODEL, 2 * XATTN_WIDTH), D_MODEL ** -0.5)
    gp = (DEPTH, SSM_GROUPS, SSM_STATE)
    ssm_a_re = -0.5 + nrm(ks[8], gp, 0.01)
    ssm_a_im = jnp.pi * jnp.arange(SSM_STATE, dtype=f32)[None, None, :] + nrm(ks[9], gp, 0.01)
    ssm_log_dt = jax.random.uniform(ks[10], (DEPTH, SSM_GROUPS), f32, math.log(1e-3), math.log(1e-1))
    ssm_b_re = nrm(ks[11], (DEPTH, SSM_GROUPS, SSM_STATE, SSM_GROUP), (2 * SSM_GROUP) ** -0.5)
    ssm_b_im = nrm(ks[12], (DEPTH, SSM_GROUPS, SSM_STATE, SSM_GROUP), (2 * SSM_GROUP) ** -0.5)
    ssm_c_re = nrm(ks[13], (DEPTH, SSM_GROUPS, SSM_GROUP, SSM_STATE), (2 * SSM_STATE) ** -0.5)
    ssm_c_im = nrm(ks[14], (DEPTH, SSM_GROUPS, SSM_GROUP, SSM_STATE), (2 * SSM_STATE) ** -0.5)
    ssm_d = nrm(ks[15], (DEPTH, SSM_GROUPS, SSM_GROUP), 1.0)
    w_glu = nrm(ks[16], (DEPTH, SSM_WIDTH, SSM_WIDTH), SSM_WIDTH ** -0.5)
    b_glu = nrm(ks[17], (DEPTH, SSM_WIDTH), 0.01)
    diff_lq1 = nrm(ks[18], (DEPTH, DIFF_HEAD_DIM), 0.1)
    diff_lk1 = nrm(ks[19], (DEPTH, DIFF_HEAD_DIM), 0.1)
    diff_lq2 = nrm(ks[20], (DEPTH, DIFF_HEAD_DIM), 0.1)
    diff_lk2 = nrm(ks[21], (DEPTH, DIFF_HEAD_DIM), 0.1)
    diff_subln = 1.0 + nrm(ks[22], (DEPTH, DIFF_V_DIM), 0.02)
    return {"x": x, "mem": mem, "positions": positions,
            "norm_pre": norm_pre, "norm_post": norm_post, "norm_mem": norm_mem,
            "w_in": w_in, "w_out": w_out, "w_mem_kv": w_mem_kv,
            "ssm_a_re": ssm_a_re, "ssm_a_im": ssm_a_im, "ssm_log_dt": ssm_log_dt,
            "ssm_b_re": ssm_b_re, "ssm_b_im": ssm_b_im, "ssm_c_re": ssm_c_re, "ssm_c_im": ssm_c_im,
            "ssm_d": ssm_d, "w_glu": w_glu, "b_glu": b_glu,
            "diff_lq1": diff_lq1, "diff_lk1": diff_lk1, "diff_lq2": diff_lq2, "diff_lk2": diff_lk2,
            "diff_subln": diff_subln}

def first_block(x, mem, positions, norm_pre, norm_post, norm_mem, w_in, w_out, w_mem_kv,
              ssm_a_re, ssm_a_im, ssm_log_dt, ssm_b_re, ssm_b_im, ssm_c_re, ssm_c_im,
              ssm_d, w_glu, b_glu, diff_lq1, diff_lk1, diff_lq2, diff_lk2, diff_subln):
    bsz, seq = x.shape[0], x.shape[1]
    cos, sin = rope_tables(positions, DIFF_HEAD_DIM)
    widths = [SSM_WIDTH, SSM_WIDTH, DIFF_WIDTH, DIFF_WIDTH, DIFF_WIDTH, DIFF_WIDTH,
              XATTN_WIDTH, XATTN_WIDTH]
    split_at = [sum(widths[:i + 1]) for i in range(len(widths) - 1)]
    for l in range(DEPTH):
        lambda_init = 0.8 - 0.6 * math.exp(-0.3 * l)
        h = rmsnorm(x, norm_pre[l])
        proj = h @ w_in[l]
        u_s, g_s, q_d, k_d, v_d, g_d, q_x, g_x = jnp.split(proj, split_at, axis=-1)

        y_s = s5_scan(u_s, ssm_a_re[l], ssm_a_im[l], ssm_log_dt[l], ssm_b_re[l], ssm_b_im[l],
                      ssm_c_re[l], ssm_c_im[l], ssm_d[l])
        y_s = jax.nn.gelu(y_s)
        y_s = y_s * jax.nn.sigmoid(y_s @ w_glu[l] + b_glu[l])
        y_s = y_s * jax.nn.silu(g_s)

        q = apply_rope(q_d.reshape(bsz, seq, DIFF_HEADS, 2, DIFF_HEAD_DIM), cos, sin)
        k = apply_rope(k_d.reshape(bsz, seq, DIFF_HEADS, 2, DIFF_HEAD_DIM), cos, sin)
        v = v_d.reshape(bsz, seq, DIFF_HEADS, DIFF_V_DIM)
        lam = (jnp.exp(jnp.sum(diff_lq1[l].astype(jnp.float32) * diff_lk1[l].astype(jnp.float32)))
               - jnp.exp(jnp.sum(diff_lq2[l].astype(jnp.float32) * diff_lk2[l].astype(jnp.float32)))
               + lambda_init)
        y_d = diff_attention(q, k, v, lam, lambda_init, diff_subln[l]) * jax.nn.silu(g_d)

        mem_n = rmsnorm(mem, norm_mem[l])
        y_x = memory_attention(q_x.reshape(bsz, seq, XATTN_HEADS, XATTN_HEAD_DIM), mem_n, w_mem_kv[l])
        y_x = y_x * jax.nn.silu(g_x)

        mix = jnp.concatenate([y_s, y_d, y_x], axis=-1) @ w_out[l]
        x = x + rmsnorm(mix, norm_post[l])
    return x


_first_inputs = first_inputs


def first_inputs(seed=0):
    import zlib

    import numpy as np

    out = dict(_first_inputs(seed))
    spreads = {}
    factors = {'norm_post': 37.158,
     'norm_mem': 33.115,
     'ssm_a_re': 200.0,
     'ssm_b_re': 126.744,
     'ssm_b_im': 127.024,
     'ssm_c_re': 125.504,
     'ssm_c_im': 127.832,
     'b_glu': 200.0,
     'diff_subln': 117.978,
     'ssm_a_im': 26.104,
     'ssm_log_dt': 28.104,
     'w_glu': 14.215,
     'ssm_d': 3.027}
    for name, (base, spread) in spreads.items():
        noise = np.random.default_rng([zlib.crc32(name.encode()), seed]).standard_normal(out[name].shape)
        drawn = base * np.exp(spread * noise) if base else spread * noise
        out[name] = __import__('jax').numpy.asarray(drawn.astype(out[name].dtype))
    for name, factor in factors.items():
        out[name] = (out[name] * factor).astype(out[name].dtype)
    return out


_narrow_inputs = first_inputs


def first_inputs(seed=0):

    out = dict(_narrow_inputs(seed))
    wider = {'norm_post': 3.31, 'ssm_d': 3.3, 'w_glu': 4.13, 'b_glu': 12.0, 'diff_subln': 4.02}
    for name, times in wider.items():
        mean = out[name].mean()
        out[name] = (mean + times * (out[name] - mean)).astype(out[name].dtype)
    return out


CHUNK = 64
MIX_WIDTH = D_MODEL
CONV_WIDTH = MIX_WIDTH // 2
CONV_GROUPS = 16
CONV_K = 3
GLA_WIDTH = MIX_WIDTH - CONV_WIDTH
GLA_HEADS = 4
GLA_DK = GLA_WIDTH // 2
GLA_HEAD_K = GLA_DK // GLA_HEADS
GLA_HEAD_V = GLA_WIDTH // GLA_HEADS
GLA_RANK = 16
GLA_TAU = 16.0
EPS = 1e-6

SPLIT_SIZES = (CONV_WIDTH, CONV_WIDTH, CONV_WIDTH, CONV_WIDTH,
               GLA_DK, GLA_DK, GLA_WIDTH, GLA_WIDTH, GLA_RANK)
IN_COLS = int(sum(SPLIT_SIZES))
SPLIT_IDX = [int(i) for i in np.cumsum(SPLIT_SIZES)[:-1]]


def rms_norm(x, g):
    xf = x.astype(jnp.float32)
    y = xf * lax.rsqrt(jnp.mean(xf * xf, axis=-1, keepdims=True) + EPS)
    return (y * g.astype(jnp.float32)).astype(x.dtype)

def short_conv_branch(h, bg, cg, z, conv_w, conv_b):
    u = cg * h
    s = u.shape[1]
    up = jnp.pad(u, ((0, 0), (CONV_K - 1, 0), (0, 0)))
    y = conv_b + sum(conv_w[j] * up[:, j:j + s] for j in range(CONV_K))
    return bg * y * jax.nn.silu(z)

def gla_branch(q, k, v, r, g_down, w_up, b_gate, norm_g):
    bsz, s, _ = q.shape
    n = s // CHUNK
    f32 = jnp.float32
    qc = q.astype(f32).reshape(bsz, n, CHUNK, GLA_HEADS, GLA_HEAD_K) * (GLA_HEAD_K ** -0.5)
    kc = k.astype(f32).reshape(bsz, n, CHUNK, GLA_HEADS, GLA_HEAD_K)
    vc = v.astype(f32).reshape(bsz, n, CHUNK, GLA_HEADS, GLA_HEAD_V)
    glog = jax.nn.log_sigmoid(g_down.astype(f32) @ w_up.astype(f32) + b_gate.astype(f32)) / GLA_TAU
    glog = glog.reshape(bsz, n, CHUNK, GLA_HEADS, GLA_HEAD_K)
    bcum = jnp.cumsum(glog, axis=2)
    b_end = bcum[:, :, -1]
    k_dec = kc * jnp.exp(b_end[:, :, None] - bcum)
    u = jnp.einsum('bnchk,bnchv->bnhkv', k_dec, vc)
    decay = jnp.exp(b_end)

    def step(state, inp):
        d, du = inp
        state = d[..., None] * state + du
        return state, state

    init = jnp.zeros((bsz, GLA_HEADS, GLA_HEAD_K, GLA_HEAD_V), f32)
    _, s_all = lax.scan(step, init, (jnp.moveaxis(decay, 1, 0), jnp.moveaxis(u, 1, 0)))
    s_all = jnp.moveaxis(s_all, 0, 1)
    o = jnp.einsum('bnchk,bnhkv->bnchv', qc, s_all).reshape(bsz, s, GLA_HEADS, GLA_HEAD_V)
    o = o * lax.rsqrt(jnp.mean(o * o, axis=-1, keepdims=True) + EPS) * norm_g.astype(f32)
    o = o.reshape(bsz, s, GLA_WIDTH).astype(q.dtype)
    return o * jax.nn.silu(r)

def second_inputs(seed: int = 0) -> dict:
    key = jax.random.key(seed)
    ks = jax.random.split(key, 10)
    f32 = jnp.float32
    x = jax.random.normal(ks[0], (BATCH, SEQ, D_MODEL), f32)
    norm_g = 1.0 + 0.02 * jax.random.normal(ks[1], (DEPTH, D_MODEL), f32)
    w_in = jax.random.normal(ks[2], (DEPTH, D_MODEL, IN_COLS), f32) * D_MODEL ** -0.5
    conv_w = jax.random.normal(ks[3], (DEPTH, CONV_K, CONV_WIDTH), f32) * CONV_K ** -0.5
    conv_b = 0.02 * jax.random.normal(ks[4], (DEPTH, CONV_WIDTH), f32)
    gla_w_up = jax.random.normal(ks[5], (DEPTH, GLA_RANK, GLA_DK), f32) * GLA_RANK ** -0.5
    gla_b_gate = 2.0 + 0.1 * jax.random.normal(ks[6], (DEPTH, GLA_DK), f32)
    gla_norm_g = 1.0 + 0.02 * jax.random.normal(ks[7], (DEPTH, GLA_HEADS, GLA_HEAD_V), f32)
    w_out = jax.random.normal(ks[8], (DEPTH, MIX_WIDTH, D_MODEL), f32) * MIX_WIDTH ** -0.5
    final_g = 1.0 + 0.02 * jax.random.normal(ks[9], (D_MODEL,), f32)
    return {"x": x, "norm_g": norm_g, "w_in": w_in, "conv_w": conv_w, "conv_b": conv_b,
            "gla_w_up": gla_w_up, "gla_b_gate": gla_b_gate, "gla_norm_g": gla_norm_g,
            "w_out": w_out, "final_g": final_g}

def second_block(x, norm_g, w_in, conv_w, conv_b, gla_w_up, gla_b_gate, gla_norm_g, w_out, final_g):
    for l in range(DEPTH):
        h = rms_norm(x, norm_g[l])
        proj = h @ w_in[l]
        ch, cb, cc, cz, gq, gk, gv, gr, gd = jnp.split(proj, SPLIT_IDX, axis=-1)
        y_conv = short_conv_branch(ch, cb, cc, cz, conv_w[l], conv_b[l])
        y_gla = gla_branch(gq, gk, gv, gr, gd, gla_w_up[l], gla_b_gate[l], gla_norm_g[l])
        y = jnp.concatenate([y_conv, y_gla], axis=-1)
        x = x + y @ w_out[l]
    return rms_norm(x, final_g)


_first_inputs_2 = second_inputs


def second_inputs(seed=0):
    import zlib

    import numpy as np

    out = dict(_first_inputs_2(seed))
    spreads = {}
    factors = {}
    for name, (base, spread) in spreads.items():
        noise = np.random.default_rng([zlib.crc32(name.encode()), seed]).standard_normal(out[name].shape)
        drawn = base * np.exp(spread * noise) if base else spread * noise
        out[name] = __import__('jax').numpy.asarray(drawn.astype(out[name].dtype))
    for name, factor in factors.items():
        out[name] = (out[name] * factor).astype(out[name].dtype)
    return out


_narrow_inputs_2 = second_inputs


def second_inputs(seed=0):

    out = dict(_narrow_inputs_2(seed))
    wider = {'conv_b': 8.9, 'gla_b_gate': 3.11, 'gla_norm_g': 8.83, 'final_g': 3.13}
    for name, times in wider.items():
        mean = out[name].mean()
        out[name] = (mean + times * (out[name] - mean)).astype(out[name].dtype)
    return out


D_MIX_3 = D_MODEL
M_WIDTH = D_MIX_3 // 2
M_HEADS = 4
M_HD = M_WIDTH // M_HEADS
M_CHUNK = 64
CONV_K_3 = 4
N_WIDTH = D_MIX_3 - M_WIDTH
N_HEADS = 16
N_HD = N_WIDTH // N_HEADS
N_KV = 4
N_HPG = N_HEADS // N_KV
KV_W = N_KV * N_HD
CMP_LEN = 32
CMP_STRIDE = 16
CMP_HIDDEN = 2 * N_HD
SLC_LEN = 64
SLC_TOPN = 16
WIN = 512
QBLK = 128

IN_SPLITS = (M_WIDTH, M_WIDTH, M_WIDTH, M_WIDTH, M_HEADS, M_HEADS,
             N_WIDTH, KV_W, KV_W, KV_W, KV_W, KV_W, KV_W, 3 * N_HEADS, N_WIDTH)
D_IN = sum(IN_SPLITS)


def rmsnorm_3(x, g):
    x = x.astype(jnp.float32)
    return x * lax.rsqrt(jnp.mean(x * x, axis=-1, keepdims=True) + EPS) * g

def masked_softmax(s, mask, axis):
    s = jnp.where(mask, s.astype(jnp.float32), -jnp.inf)
    m = jnp.max(s, axis=axis, keepdims=True)
    m = jnp.where(jnp.isfinite(m), m, 0.0)
    e = jnp.where(mask, jnp.exp(s - m), 0.0)
    z = jnp.sum(e, axis=axis, keepdims=True)
    return e / jnp.where(z > 0, z, 1.0)

def alibi_slopes():
    return np.array([2.0 ** (-8.0 * (h + 1) / N_HEADS) for h in range(N_HEADS)], np.float32)

def mlstm_chunkwise(q, k, v, i_pre, f_pre):
    B, H, T, D = q.shape
    L = M_CHUNK
    nch = T // L
    k = k * (D ** -0.5)
    logf = jax.nn.log_sigmoid(f_pre)
    to_c = lambda a: jnp.moveaxis(a.reshape(a.shape[:2] + (nch, L) + a.shape[3:]), 2, 0)
    xs = (to_c(q), to_c(k), to_c(v), to_c(i_pre), to_c(logf))
    causal = jnp.tril(jnp.ones((L, L), bool))

    def step(carry, inp):
        C, n, m = carry
        qb, kb, vb, ib, fb = inp
        b = jnp.cumsum(fb, axis=-1)
        Dm = jnp.where(causal, b[..., :, None] - b[..., None, :] + ib[..., None, :], -jnp.inf)
        inter = b + m[..., None]
        m_t = jnp.maximum(inter, jnp.max(Dm, axis=-1))
        w_in = jnp.exp(Dm - m_t[..., None])
        w_st = jnp.exp(inter - m_t)
        s = jnp.einsum('bhld,bhsd->bhls', qb, kb) * w_in
        num = w_st[..., None] * jnp.einsum('bhld,bhde->bhle', qb, C) + jnp.einsum('bhls,bhse->bhle', s, vb)
        den = w_st * jnp.einsum('bhld,bhd->bhl', qb, n) + jnp.sum(s, axis=-1)
        h = num / jnp.maximum(jnp.abs(den), jnp.exp(-m_t))[..., None]
        bL = b[..., -1]
        w_end = bL[..., None] - b + ib
        m_new = jnp.maximum(bL + m, jnp.max(w_end, axis=-1))
        decay = jnp.exp(bL + m - m_new)
        wk = jnp.exp(w_end - m_new[..., None])
        C_new = decay[..., None, None] * C + jnp.einsum('bhs,bhsd,bhse->bhde', wk, kb, vb)
        n_new = decay[..., None] * n + jnp.einsum('bhs,bhsd->bhd', wk, kb)
        return (C_new, n_new, m_new), h

    init = (jnp.zeros((B, H, D, D), jnp.float32), jnp.zeros((B, H, D), jnp.float32),
            jnp.zeros((B, H), jnp.float32))
    _, hs = lax.scan(step, init, xs)
    return jnp.moveaxis(hs, 0, 2).reshape(B, H, T, D)

def mlstm_group(xm, vm, om, zm, im, fm, conv_w, conv_b, wq, wk, norm_w, skip, f_bias):
    B, T, _ = xm.shape
    xpad = jnp.pad(xm, ((0, 0), (CONV_K_3 - 1, 0), (0, 0)))
    xc = conv_b + xpad[:, 0:T] * conv_w[0]
    for j in range(1, CONV_K_3):
        xc = xc + xpad[:, j:j + T] * conv_w[j]
    xc = jax.nn.silu(xc)
    xch = xc.reshape(B, T, M_HEADS, M_HD)
    q = jnp.einsum('bthd,hde->bhte', xch, wq)
    k = jnp.einsum('bthd,hde->bhte', xch, wk)
    v = vm.reshape(B, T, M_HEADS, M_HD).transpose(0, 2, 1, 3)
    h = mlstm_chunkwise(q, k, v, im.transpose(0, 2, 1), (fm + f_bias).transpose(0, 2, 1))
    h = h.transpose(0, 2, 1, 3)
    mu = jnp.mean(h, axis=-1, keepdims=True)
    var = jnp.mean(jnp.square(h - mu), axis=-1, keepdims=True)
    hn = ((h - mu) * lax.rsqrt(var + EPS)).reshape(B, T, M_WIDTH) * norm_w
    out = jax.nn.sigmoid(om) * hn + skip * xc
    return out * jax.nn.silu(zm)

def nsa_group(qn, kc, vc, ks, vs, kw, vw, gl, zn, pos_k, pos_v, w1_k, w2_k, w1_v, w2_v):
    B, T, _ = qn.shape
    G, HPG, dh = N_KV, N_HPG, N_HD
    n_cmp = (T - CMP_LEN) // CMP_STRIDE + 1
    n_slc = T // SLC_LEN
    n_top = min(SLC_TOPN, n_slc)
    n_qb = T // QBLK
    q = qn.reshape(B, T, G, HPG, dh) * (dh ** -0.5)
    kc = kc.reshape(B, T, G, dh); vc = vc.reshape(B, T, G, dh)
    ks = ks.reshape(B, T, G, dh); vs = vs.reshape(B, T, G, dh)
    kw = kw.reshape(B, T, G, dh); vw = vw.reshape(B, T, G, dh)

    cidx = np.arange(n_cmp)[:, None] * CMP_STRIDE + np.arange(CMP_LEN)[None, :]

    def compress(a, pos, w1, w2):
        blk = a[:, cidx] + pos[None, None, :, None, :]
        blk = blk.transpose(0, 1, 3, 2, 4).reshape(B, n_cmp, G, CMP_LEN * dh)
        return jax.nn.gelu(blk @ w1) @ w2

    k_cmp = compress(kc, pos_k, w1_k, w2_k)
    v_cmp = compress(vc, pos_v, w1_v, w2_v)
    cmp_end = jnp.asarray(cidx[:, -1], jnp.int32)
    cmp_mid = jnp.asarray(cidx.mean(-1), jnp.float32)
    s_start = np.arange(n_slc) * SLC_LEN
    overlap = jnp.asarray((cidx[:, 0][:, None] <= s_start[None, :] + SLC_LEN - 1)
                          & (cidx[:, -1][:, None] >= s_start[None, :]), jnp.float32)
    slopes = jnp.asarray(alibi_slopes()).reshape(G, HPG)

    ks_blk = ks.reshape(B, n_slc, SLC_LEN, G, dh).transpose(0, 3, 1, 2, 4)
    vs_blk = vs.reshape(B, n_slc, SLC_LEN, G, dh).transpose(0, 3, 1, 2, 4)
    kw_pad = jnp.pad(kw, ((0, 0), (WIN, 0), (0, 0), (0, 0)))
    vw_pad = jnp.pad(vw, ((0, 0), (WIN, 0), (0, 0), (0, 0)))
    gates = jax.nn.sigmoid(gl).reshape(B, T, G, HPG, 3)
    q_blocks = q.reshape(B, n_qb, QBLK, G, HPG, dh).swapaxes(0, 1)
    g_blocks = gates.reshape(B, n_qb, QBLK, G, HPG, 3).swapaxes(0, 1)
    starts = jnp.arange(n_qb, dtype=jnp.int32) * QBLK
    bi = jnp.arange(B)[:, None, None, None]
    gi = jnp.arange(G)[None, :, None, None]
    sidx = jnp.arange(n_slc, dtype=jnp.int32)

    def block(args):
        qb, gb, start = args
        t = start + jnp.arange(QBLK, dtype=jnp.int32)
        tf = t.astype(jnp.float32)
        s_c = jnp.einsum('bqghd,bjgd->bqghj', qb, k_cmp)
        s_c = s_c - slopes[None, None, :, :, None] * (tf[:, None] - cmp_mid[None, :])[None, :, None, None, :]
        mask_c = (cmp_end[None, :] <= t[:, None])[None, :, None, None, :]
        p_c = masked_softmax(s_c, mask_c, -1)
        o_c = jnp.einsum('bqghj,bjgd->bqghd', p_c, v_cmp)
        imp = jnp.einsum('bqghj,js->bgqs', p_c, overlap)
        cur = t // SLC_LEN
        imp = jnp.where(sidx[None, :] <= cur[:, None], imp, -jnp.inf)
        imp = jnp.where((sidx[None, :] == 0) | (sidx[None, :] == cur[:, None]), jnp.inf, imp)
        top_val, top_idx = lax.top_k(imp, n_top)
        sel_ok = top_val > -jnp.inf
        k_sel = ks_blk[bi, gi, top_idx]
        v_sel = vs_blk[bi, gi, top_idx]
        qg = qb.transpose(0, 2, 1, 3, 4)
        s_s = jnp.einsum('bgqhd,bgqnld->bgqhnl', qg, k_sel)
        pos = top_idx[..., None] * SLC_LEN + jnp.arange(SLC_LEN, dtype=jnp.int32)
        dist_s = (t[None, None, :, None, None] - pos).astype(jnp.float32)
        s_s = s_s - slopes[None, :, None, :, None, None] * dist_s[:, :, :, None]
        mask_s = ((pos <= t[None, None, :, None, None]) & sel_ok[..., None])[:, :, :, None]
        p_s = masked_softmax(s_s, mask_s, (-2, -1))
        o_s = jnp.einsum('bgqhnl,bgqnld->bgqhd', p_s, v_sel).transpose(0, 2, 1, 3, 4)
        k_win = lax.dynamic_slice_in_dim(kw_pad, start, QBLK + WIN, axis=1)
        v_win = lax.dynamic_slice_in_dim(vw_pad, start, QBLK + WIN, axis=1)
        pos_w = start - WIN + jnp.arange(QBLK + WIN, dtype=jnp.int32)
        dw = t[:, None] - pos_w[None, :]
        mask_w = ((dw >= 0) & (dw < WIN) & (pos_w[None, :] >= 0))[None, :, None, None, :]
        s_w = jnp.einsum('bqghd,bkgd->bqghk', qb, k_win)
        s_w = s_w - slopes[None, None, :, :, None] * dw.astype(jnp.float32)[None, :, None, None, :]
        p_w = masked_softmax(s_w, mask_w, -1)
        o_w = jnp.einsum('bqghk,bkgd->bqghd', p_w, v_win)
        return gb[..., 0:1] * o_c + gb[..., 1:2] * o_s + gb[..., 2:3] * o_w

    o = lax.map(block, (q_blocks, g_blocks, starts))
    o = o.swapaxes(0, 1).reshape(B, T, N_WIDTH)
    return o * jax.nn.silu(zn)

def third_inputs(seed: int = 0) -> dict:
    key = jax.random.key(seed)
    k = jax.random.split(key, 24)
    f32 = jnp.float32
    nrm = lambda kk, shape, scale: jax.random.normal(kk, shape, f32) * scale
    L = DEPTH
    return {
        'x': nrm(k[0], (BATCH, SEQ, D_MODEL), 1.0),
        'c': nrm(k[1], (BATCH, D_MODEL), 1.0),
        'ln_g': 1.0 + nrm(k[2], (L, D_MODEL), 0.02),
        'w_ada': nrm(k[3], (L, D_MODEL, 3 * D_MODEL), 0.5 * D_MODEL ** -0.5),
        'b_ada': nrm(k[4], (L, 3 * D_MODEL), 0.02),
        'w_in': nrm(k[5], (L, D_MODEL, D_IN), D_MODEL ** -0.5),
        'b_in': nrm(k[6], (L, D_IN), 0.02),
        'm_conv_w': nrm(k[7], (L, CONV_K_3, M_WIDTH), CONV_K_3 ** -0.5),
        'm_conv_b': nrm(k[8], (L, M_WIDTH), 0.02),
        'm_wq': nrm(k[9], (L, M_HEADS, M_HD, M_HD), M_HD ** -0.5),
        'm_wk': nrm(k[10], (L, M_HEADS, M_HD, M_HD), M_HD ** -0.5),
        'm_norm_w': 1.0 + nrm(k[11], (L, M_WIDTH), 0.02),
        'm_skip': 1.0 + nrm(k[12], (L, M_WIDTH), 0.02),
        'm_f_bias': jnp.linspace(3.0, 6.0, M_HEADS, dtype=f32)[None, :] + nrm(k[13], (L, M_HEADS), 0.02),
        'n_pos_k': nrm(k[14], (L, CMP_LEN, N_HD), 0.5),
        'n_pos_v': nrm(k[15], (L, CMP_LEN, N_HD), 0.5),
        'n_w1_k': nrm(k[16], (L, CMP_LEN * N_HD, CMP_HIDDEN), (CMP_LEN * N_HD) ** -0.5),
        'n_w2_k': nrm(k[17], (L, CMP_HIDDEN, N_HD), CMP_HIDDEN ** -0.5),
        'n_w1_v': nrm(k[18], (L, CMP_LEN * N_HD, CMP_HIDDEN), (CMP_LEN * N_HD) ** -0.5),
        'n_w2_v': nrm(k[19], (L, CMP_HIDDEN, N_HD), CMP_HIDDEN ** -0.5),
        'w_out': nrm(k[20], (L, D_MIX_3, D_MODEL), D_MIX_3 ** -0.5),
        'final_g': 1.0 + nrm(k[21], (D_MODEL,), 0.02),
    }

def third_block(x, c, ln_g, w_ada, b_ada, w_in, b_in, m_conv_w, m_conv_b, m_wq, m_wk, m_norm_w,
              m_skip, m_f_bias, n_pos_k, n_pos_v, n_w1_k, n_w2_k, n_w1_v, n_w2_v, w_out, final_g):
    out_dtype = x.dtype
    h_res = x.astype(jnp.float32)
    cf = c.astype(jnp.float32)
    offsets = [int(o) for o in np.cumsum(IN_SPLITS)[:-1]]
    for l in range(DEPTH):
        mod = jax.nn.silu(cf) @ w_ada[l] + b_ada[l]
        shift, scale, gate = jnp.split(mod, 3, axis=-1)
        h = rmsnorm_3(h_res, ln_g[l]) * (1.0 + scale[:, None]) + shift[:, None]
        p = h @ w_in[l] + b_in[l]
        (m_x, m_v, m_o, m_z, m_i, m_f, n_q, n_kc, n_vc, n_ks, n_vs, n_kw, n_vw, n_g, n_z) = \
            jnp.split(p, offsets, axis=-1)
        y_m = mlstm_group(m_x, m_v, m_o, m_z, m_i, m_f, m_conv_w[l], m_conv_b[l], m_wq[l], m_wk[l],
                          m_norm_w[l], m_skip[l], m_f_bias[l])
        y_n = nsa_group(n_q, n_kc, n_vc, n_ks, n_vs, n_kw, n_vw, n_g, n_z, n_pos_k[l], n_pos_v[l],
                        n_w1_k[l], n_w2_k[l], n_w1_v[l], n_w2_v[l])
        y = jnp.concatenate([y_m, y_n], axis=-1) @ w_out[l]
        h_res = h_res + gate[:, None] * y
    return rmsnorm_3(h_res, final_g).astype(out_dtype)


_first_inputs_3 = third_inputs


def third_inputs(seed=0):
    import zlib

    import numpy as np

    out = dict(_first_inputs_3(seed))
    spreads = {}
    factors = {'ln_g': 8.0,
     'b_ada': 4.805,
     'b_in': 8.0,
     'm_conv_b': 8.0,
     'm_norm_w': 8.0,
     'm_skip': 8.0,
     'n_pos_k': 8.0,
     'n_w1_k': 6.259,
     'n_w2_k': 6.263,
     'final_g': 2.764}
    for name, (base, spread) in spreads.items():
        noise = np.random.default_rng([zlib.crc32(name.encode()), seed]).standard_normal(out[name].shape)
        drawn = base * np.exp(spread * noise) if base else spread * noise
        out[name] = __import__('jax').numpy.asarray(drawn.astype(out[name].dtype))
    for name, factor in factors.items():
        out[name] = (out[name] * factor).astype(out[name].dtype)
    return out


_narrow_inputs_3 = third_inputs


def third_inputs(seed=0):

    out = dict(_narrow_inputs_3(seed))
    wider = {'m_norm_w': 12.0, 'm_skip': 3.46, 'n_pos_v': 12.0, 'final_g': 3.07}
    for name, times in wider.items():
        mean = out[name].mean()
        out[name] = (mean + times * (out[name] - mean)).astype(out[name].dtype)
    return out


def setup_inputs(seed=0):
    out = dict(first_inputs(seed))
    for name, value in second_inputs(seed + 1).items():
        if name != "x":
            out[name + "_2"] = value
    for name, value in third_inputs(seed + 2).items():
        if name != "x":
            out[name + "_3"] = value
    return out


def reference(
    x, mem, positions, norm_pre, norm_post, norm_mem, w_in, w_out, w_mem_kv, ssm_a_re, ssm_a_im,
    ssm_log_dt, ssm_b_re, ssm_b_im, ssm_c_re, ssm_c_im, ssm_d, w_glu, b_glu, diff_lq1, diff_lk1,
    diff_lq2, diff_lk2, diff_subln, norm_g_2, w_in_2, conv_w_2, conv_b_2, gla_w_up_2,
    gla_b_gate_2, gla_norm_g_2, w_out_2, final_g_2, c_3, ln_g_3, w_ada_3, b_ada_3, w_in_3,
    b_in_3, m_conv_w_3, m_conv_b_3, m_wq_3, m_wk_3, m_norm_w_3, m_skip_3, m_f_bias_3, n_pos_k_3,
    n_pos_v_3, n_w1_k_3, n_w2_k_3, n_w1_v_3, n_w2_v_3, w_out_3, final_g_3,
):
    x = first_block(
        x, mem, positions, norm_pre, norm_post, norm_mem, w_in, w_out, w_mem_kv, ssm_a_re,
        ssm_a_im, ssm_log_dt, ssm_b_re, ssm_b_im, ssm_c_re, ssm_c_im, ssm_d, w_glu, b_glu,
        diff_lq1, diff_lk1, diff_lq2, diff_lk2, diff_subln,
    )
    x = second_block(
        x, norm_g_2, w_in_2, conv_w_2, conv_b_2, gla_w_up_2, gla_b_gate_2, gla_norm_g_2,
        w_out_2, final_g_2,
    )
    return third_block(
        x, c_3, ln_g_3, w_ada_3, b_ada_3, w_in_3, b_in_3, m_conv_w_3, m_conv_b_3, m_wq_3,
        m_wk_3, m_norm_w_3, m_skip_3, m_f_bias_3, n_pos_k_3, n_pos_v_3, n_w1_k_3, n_w2_k_3,
        n_w1_v_3, n_w2_v_3, w_out_3, final_g_3,
    )


_drawn_inputs = setup_inputs


def setup_inputs(seed=0):
    import zlib

    import numpy as np

    out = dict(_drawn_inputs(seed))
    spreads = {}
    factors = {'norm_g_2': 8.0,
     'conv_b_2': 8.0,
     'gla_w_up_2': 8.0,
     'gla_b_gate_2': 64.0,
     'gla_norm_g_2': 49.886}
    for name, (base, spread) in spreads.items():
        noise = np.random.default_rng([zlib.crc32(name.encode()), seed]).standard_normal(out[name].shape)
        drawn = base * np.exp(spread * noise) if base else spread * noise
        out[name] = __import__('jax').numpy.asarray(drawn.astype(out[name].dtype))
    for name, factor in factors.items():
        out[name] = (out[name] * factor).astype(out[name].dtype)
    return out
```

```python
import concourse.bass as bass
from concourse import mybir
from contextlib import ExitStack
import math

F32 = mybir.dt.float32
I32 = mybir.dt.int32
ALU = mybir.AluOpType
ACT = mybir.ActivationFunctionType
AX = mybir.AxisListType

P = 128
SEQ = 512
D = 2048
KT = D // P
TT = SEQ // P
NC = 512
EPS = 1e-6
NEG = -1e30
RING = 4
PROJ_BANKS = (0, 1, 2)
SIDE_BANKS = (3, 4, 5, 6, 7)


class Lane:

    def __init__(self, eng, sem):
        self.eng, self.sem, self.n = eng, sem, 0

    def __call__(self, ins):
        ins.then_inc(self.sem, 1)
        self.n += 1

    def settle(self):
        self.eng.wait_ge(self.sem, self.n)


class Banks:

    def __init__(self, full, free):
        self.full, self.free = full, free
        self.uses, self.freed = [0] * 8, [0] * 8
        self.at, self.turn = {}, {"P": 0, "S": 0}

    def plan(self, stage, key, pool, readers=1):
        if pool in self.turn:
            group = PROJ_BANKS if pool == "P" else SIDE_BANKS
            b = group[self.turn[pool] % len(group)]
            self.turn[pool] += 1
        else:
            b = pool
        self.uses[b] += 1
        before = self.freed[b]
        self.freed[b] += readers
        self.at[stage, key] = (b, self.uses[b], before, self.freed[b])

    def bank(self, stage, key=0):
        return self.at[stage, key][0]

    def take(self, pe, stage, key=0):
        b, _, before, _ = self.at[stage, key]
        if before:
            pe.wait_ge(self.free[b], before)

    def filled(self, stage, key=0):
        b, use, _, _ = self.at[stage, key]
        return self.full[b], use

    def full_sem(self, stage, key=0):
        return self.full[self.at[stage, key][0]]

    def free_sem(self, stage, key=0):
        return self.free[self.at[stage, key][0]]

    def released(self, stage, key=0):
        b, _, _, after = self.at[stage, key]
        return self.free[b], after

    def read_once(self, stage, key=0):
        b, _, _, after = self.at[stage, key]
        return self.free[b], after - 1


def spread_steps(tiles, steps):
    out, done = [], 0
    for i, t in enumerate(tiles):
        upto = len(steps) * (i + 1) // len(tiles)
        out += [t] + steps[done:upto]
        done = upto
    return out


def deal(script, steps):
    n, tiles, out, done = 0, sum(st[0] == "tile" for st in script), [], 0
    for st in script:
        out.append(st)
        if st[0] == "tile":
            n += 1
            upto = len(steps) * n // tiles
            out += steps[done:upto]
            done = upto
    return out


S_G, S_H, S_N = 64, 16, 64
S_W = S_G * S_H
S_L = P // S_H
S_B = SEQ // S_L
S_CG = P // S_H
S_C = S_G // S_CG
DF_H, DF_D, DF_V = 4, 64, 128
XA_H, XA_D, MEM = 4, 128, 256
LAMBDA_INIT = 0.8 - 0.6 * math.exp(-0.3 * 0)
MAGIC = 1.5 * 2.0 ** 23
TWO_PI = (6.28125, 1.93500518798828125e-3, 3.01991598196e-7)
PI_DOWN = 3.1415925


def block1(K):
    nc, T, ps, bk = K.nc, K.T, K.ps, K.bk
    hT, yT, X = K.A_kt, K.B_kt, K.X
    Bf, Xf = K.B, X.rearrange("p t d -> p (t d)")
    mem_rows = Bf[:, 0:2 * D].rearrange("p (t d) -> p t d", d=D)
    memT = Bf[:, 2 * D:4 * D].rearrange("p (k m) -> p k m", m=MEM)
    K.mem_rows, K.memT = mem_rows, memT

    norm_pre, norm_mem, b_glu = K.keep(KT), K.keep(KT), K.keep(8)
    subln, nlam, lamp = K.keep(1), K.keep(1), K.keep(2)
    invf = K.keep(1)
    d_skip = K.keep(S_G)
    sgn = K.keep(2)
    K.norm_gain[1] = (norm_pre, None)
    K.norm_gain["mem"] = (norm_mem, None)
    mx, sums, rs = K.keep(2, 2), K.keep(4, 2), K.keep(2, 2)
    oss = K.keep(TT)

    a = K.arena()
    mk, mv = a("mk", XA_H, MEM), a("mv", MEM // P, XA_H * XA_D)
    qr, kr = a("q", 2, SEQ), a("k", 2, SEQ)
    raw = a("raw", 2, SEQ)
    v = a("v", 2, TT, DF_V)
    ropeC, ropeS = a("cos", SEQ), a("sin", SEQ)
    tri, perm = a("tri", SEQ), a("perm", P)
    e_at = a.at[0]
    e = a("e", 2, 2, SEQ)
    pT = a("pT", 2, SEQ)
    obuf = a("o", TT, P)
    pb_at = a.at[0]
    pb_re, pb_im = a("pb_re", S_G, S_L), a("pb_im", S_G, S_L)
    pc_re, pc_im = a("pc_re", S_G, S_L + 1), a("pc_im", S_G, S_L + 1)
    z_re, z_im = a("z_re", S_G), a("z_im", S_G)
    l_re, l_im = a("l_re", S_G), a("l_im", 2, S_G)
    inm = a("inm", S_CG, P)
    krow = a("krow", S_CG, P)
    braw = a("braw", 4, S_CG * S_H)
    craw = a("craw", 2, 3 * S_N)
    t = K.arena(0, Bf)
    ba = t("ba", S_CG * S_L, S_H)
    ca = t("ca", S_CG, (S_L + 1) * S_H)
    tmp = t("tmp", S_CG * (S_L + 1), S_H)
    ublk = t("ublk", S_CG * S_B)
    bst, bsw = t("bst", S_CG, S_H), t("bsw", S_CG, S_H)
    us = Xf[:, 0:2 * SEQ].rearrange("p (a s) -> p a s", s=SEQ)
    vst = Xf[:, :].rearrange("p (s b g) -> p s b g", s=2, b=S_B)
    ych = Xf[:, 0:S_C * SEQ].rearrange("p (c s) -> p c s", s=SEQ)
    sig = Xf[:, S_C * SEQ:(S_C + 2) * SEQ].rearrange("p (c s) -> p c s", s=SEQ)
    w = K.arena(e_at)
    T2 = [ba.rearrange("p a b -> p (a b)"), tmp.rearrange("p a b -> p (a b)")[:, 0:S_CG * P]]
    C2 = [ca.rearrange("p a b -> p (a b)")[:, 0:S_CG * P], krow.rearrange("p a b -> p (a b)")]
    U2 = [ublk, braw.rearrange("p a b -> p (a b)")]
    ybuf = inm.rearrange("p a b -> p (a b)").rearrange("p (a s) -> p a s", s=SEQ)
    scan_t = w("scan_t", 4, S_G)
    rope_t = K.arena(pb_at)("rope_t", 2, SEQ)
    w = K.arena(e_at)
    pos_i = w("pos_i", SEQ).bitcast(I32)
    ang, kk_, half = w("ang", SEQ), w("turns", SEQ), w("half", SEQ)
    w = K.arena(e_at)
    araw = w("araw", 2, 2 * S_N)
    logdt = w("logdt", S_G)
    lqk = w("lqk", 4, DF_D)
    lqk_j = w("lqk_j", DF_D)
    tm = [w(f"tm{i}", S_G) for i in range(14)]
    U_d = nc.dram_tensor("u_blocks", (P, S_G, S_B), F32).ap()
    KD = nc.dram_tensor("taps", (S_H, S_G, 2 * P), F32).ap()
    CA_d = nc.dram_tensor("out_matrices", (S_C, P, S_CG * P), F32).ap()
    Y_d = nc.dram_tensor("y_channels", (S_G, S_H, S_L, S_B), F32).ap()

    col, c0 = {}, 0
    for n, wd in (("us", S_W), ("gs", S_W), ("qd", 512), ("kd", 512), ("vd", 512), ("gd", 512), ("qx", 512), ("gx", 512)):
        col[n] = c0
        c0 += wd
    W, WM, WG = T["w_in"][0], T["w_mem_kv"][0], T["w_glu"][0]

    def tile(name, i):
        st = ("tile", 1, name, i)
        if name == "mk":
            K.tile(st, [(WM, i * P, P)], "T", P, memT, MEM)
        elif name == "mv":
            K.tile(st, [(WM, 512 + i * P, P)], "N", P, memT, MEM)
        elif name == "glu":
            K.tile(st, [(WG, i * P, P)], "T", P, ych, SEQ, kt=8)
        else:
            K.tile(st, [(W, col[name] + i * P, P)], "N" if name == "vd" else "T", P, hT, SEQ,
                   readers=1)
        return st

    script = [("norm", 1, tt) for tt in range(TT)] + [("b1_tables", 0), ("ss_par", 0)]
    ut = [tile("us", i) for i in range(S_C)]
    K.after_norm(ut[0], 1)
    script += ut[0:2] + [("rope_tab", 0)] + ut[2:4] + [("norm", "mem", 0)] + ut[4:6] + [("norm", "mem", 1)] + ut[6:8]
    mt = [t_ for h in range(XA_H) for t_ in (tile("mk", h), tile("mv", h))]
    K.tiles[mt[0]]["after"] += [(("norm", "mem", tt), k4) for tt in range(2) for k4 in range(KT // 4)]
    gates = [tile("gd", h) for h in range(DF_H)] + [tile("gx", h) for h in range(XA_H)]
    steps = []
    for c in range(S_C + 2):
        if 0 <= c - 2 < S_C:
            steps.append(("sp_c", c - 2))
        if 0 <= c - 1 < S_C:
            steps.append(("sp_b", c - 1))
        if c < S_C:
            steps.append(("sp_a", c))
    qt = [[tile(n, h) for n in ("qd", "kd", "vd")] for h in range(DF_H)]
    xt = [tile("qx", h) for h in range(XA_H)]
    script += spread_steps(mt + gates[0:4], steps)
    script += [("scan", 0)] + gates[4:8] + qt[0] + [("rope", 0)]
    units = [("d", h, qb) for h in range(DF_H) for qb in range(TT)] + [("x", h, qb) for h in range(XA_H) for qb in range(TT)]
    at = {u: n for n, u in enumerate(units)}

    def attention_steps(n):
        out = []
        if n < len(units):
            out.append(("at_s", n))
        if 0 <= n - 1 < len(units):
            out.append(("at_t", n - 1))
        if 0 <= n - 2 < len(units):
            out.append(("at_v", n - 2))
            if units[n - 2][2] == TT - 1:
                out.append(("at_o", n - 2))
        return out

    n = 0
    for h in range(DF_H):
        nxt = qt[h + 1] + [("rope", h + 1)] if h + 1 < DF_H else xt[0:2]
        tiles_ = [s for s in nxt if s[0] == "tile"]
        for i, t_ in enumerate(nxt):
            script.append(t_)
            if t_[0] == "tile":
                while n < 4 * h + 4 * (i + 1) // len(tiles_):
                    script += attention_steps(n)
                    n += 1
    gs = [tile("gs", i) for i in range(8)]
    glu = [tile("glu", i) for i in range(8)]
    p2 = [("sp_d", c) for c in range(S_C)]
    script += attention_steps(n)
    n += 1
    left = [attention_steps(m) for m in range(n, len(units) + 2)]
    done = 0
    for i in range(S_C):
        script.append(p2[i])
        upto = len(left) * (i + 1) // S_C
        for m in left[done:upto]:
            script += m
            for h in (2, 3):
                if ("at_s", at["x", h - 2, TT - 1]) in m:
                    script.append(xt[h])
        done = upto
    script += [("y_back", 0)] + gs + [("gelu", 0)] + glu
    script += [("wo", 1, n) for n in range(4)] + [("final", 1, tt) for tt in range(TT)]
    for st in script:
        kind = st[0]
        if kind == "ss_par":
            K.uses[st] = [(0, "S", 1)]
        elif kind == "sp_a":
            K.uses[st] = [("c", "S", 1)]
        elif kind == "sp_b":
            K.uses[st] = [(("i", j), "S", 1) for j in range(2)] + [(("k", j), "S", 1) for j in range(2)]
        elif kind == "sp_c":
            K.uses[st] = [(s, "S", 1) for s in range(2)]
        elif kind == "sp_d":
            K.uses[st] = [(0, "S", 1)]
        elif kind == "rope":
            K.uses[st] = [(j, "S", 1) for j in range(2)]
        elif kind == "at_s":
            K.uses[st] = [(c, "S", 1) for c in range(2)] if units[st[1]][0] == "d" else [(0, "S", 2)]
        elif kind in ("at_t", "at_v", "at_o"):
            K.uses[st] = [(0, "S", 1)]

    s_par, s_tab = K.sem("b1_params"), K.sem("b1_tables")
    s_mem = K.sem("mem_loaded")
    K.s_mem = s_mem
    s_tb = K.sem("setup_loads")
    s_zero, s_zst = K.sem("zero_taps"), K.sem("zero_taps_stored")
    s_sa, s_sv = K.sem("setup_act"), K.sem("setup_vec")
    s_pow = K.sem("powers_ready")
    s_u = [K.sem(f"u_stored{i}") for i in range(4)]
    s_ul = [K.sem(f"u_block_loaded{i}") for i in range(2)]
    s_bc = [K.sem(f"bc_loaded{i}") for i in range(2)]
    s_ba, s_ca = K.sem("b_powers_ready"), K.sem("c_powers_ready")
    s_kr = K.sem("taps_ready")
    s_kst, s_cst = K.sem("taps_stored"), K.sem("out_matrices_stored")
    s_scan, s_scand = K.sem("scan_step"), K.sem("scan_done")
    s_p2 = [K.sem(f"pass2_loaded{i}") for i in range(2)]
    s_yst = [K.sem(f"y_stored{i}") for i in range(2)]
    s_yb = K.sem("y_back")
    s_gelu = K.sem("gelu_ready")
    s_rope = K.sem("roped")
    s_score, s_exp, s_w = K.sem("b1_scores"), K.sem("b1_exps"), K.sem("b1_weights")
    s_o = K.sem("b1_heads")
    s_oss, s_ort = K.sem("b1_head_squares"), K.sem("b1_head_root")
    s_on = K.sem("b1_head_normed")
    s_back, s_fg = K.sem("x_back_1"), K.sem("norm_post_loaded")

    def sp_start(sp):
        for tt in range(MEM // P):
            sp.dma_start(mem_rows[:, tt, :], T["mem"][0, tt * P:(tt + 1) * P, :]).then_inc(s_mem, 16)
    K.sp_start.append(sp_start)

    def pool_params(pool):
        n = 0
        vec_of = lambda ap: ap.rearrange("o (k p) -> p (o k)", p=P)
        with nc.allow_non_contiguous_dma(reason="small per-channel parameters"):
            for dst, src in ((norm_pre, vec_of(T["norm_pre"])), (norm_mem, vec_of(T["norm_mem"])), (b_glu, vec_of(T["b_glu"])),
                             (subln, T["diff_subln"].rearrange("o d -> d o")), (invf, T["c_invf"]), (sgn, T["c_sgn"]),
                             (d_skip[0:S_H, :], T["ssm_d"][0].rearrange("g h -> h g"))):
                pool.dma_start(dst, src).then_inc(s_par, 16)
                n += 16
        K.par_count[1] = n

    def load_bc(pool, c):
        i = c % 2
        g = slice(c * S_CG, (c + 1) * S_CG)
        f = lambda ap: ap[0, g].rearrange("g p h -> p g h")
        b3 = [braw[:, 2 * i + j, :].rearrange("p (g h) -> p g h", h=S_H) for j in range(2)]
        re, im = f(T["ssm_b_re"]), f(T["ssm_b_im"])
        for dst, src in ((b3[0][0:64], re), (b3[0][64:128], im), (b3[1][0:64], im), (b3[1][64:128], re)):
            pool.dma_start(dst, src).then_inc(s_bc[i], 16)
        cre, cim = (T[n][0, g].rearrange("g h p -> (g h) p") for n in ("ssm_c_re", "ssm_c_im"))
        for j, src in enumerate((cre, cim, cre)):
            pool.dma_start(craw[:, i, j * S_N:(j + 1) * S_N], src).then_inc(s_bc[i], 16)

    def pool_tables(pool, st):
        pool.wait_ge(*bk.filled(("norm", 1, TT - 1), KT // 4 - 1))
        for j, n in enumerate(("ssm_a_re", "ssm_a_im")):
            for r in range(2):
                pool.dma_start(araw[0:S_G, j, r * S_N:(r + 1) * S_N], T[n][0]).then_inc(s_tb, 16)
        pool.dma_start(logdt, T["ssm_log_dt"][0].partition_broadcast(P)).then_inc(s_tb, 16)
        for j, n in enumerate(("diff_lq1", "diff_lk1", "diff_lq2", "diff_lk2")):
            pool.dma_start(lqk[:, j, :], T[n][0].partition_broadcast(P)).then_inc(s_tb, 16)
        pool.dma_start(tri, T["c_tri"]).then_inc(s_tab, 16)
        pool.dma_start(perm, T["c_perm"]).then_inc(s_tab, 16)
        nc.gpsimd.memset(krow[0:S_H, :, :], 0.0).then_inc(s_zero, 1)
        pool.wait_ge(s_zero, 1)
        for c in range(S_C):
            pool.dma_start(KD[:, c * S_CG:(c + 1) * S_CG, 0:P], krow[0:S_H, :, :]).then_inc(s_zst, 16)
        load_bc(pool, 0)
        load_bc(pool, 1)

    def pool_rope_tab(pool, st):
        pool.wait_ge(s_pow, 1)
        pool.dma_start(pos_i, T["positions"][0].partition_broadcast(P)).then_inc(s_tab, 16)

    def pool_tile(pool, st):
        _, _, name, i = st
        if name == "us":
            pool.wait_ge(*bk.released(st))
            dst = U_d.rearrange("(j h) g b -> g h j b", h=S_H)
            src = us[:, i % 2, :].rearrange("p (j b) -> p j b", b=S_B)
            for g in range(S_CG):
                pool.dma_start(dst[i * S_CG + g], src[g * S_H:(g + 1) * S_H]).then_inc(s_u[i % 4], 16)

    def pool_sp_a(pool, st):
        c = st[1]
        if c >= 1:
            pool.wait_ge(*bk.filled(("sp_c", c - 1), 1))
        else:
            pool.wait_ge(*bk.filled(("norm", "mem", 1), KT // 4 - 1))
        pool.wait_ge(s_u[c % 4], 16 * S_CG * (c // 4 + 1))
        pool.dma_start(ublk, U_d[:, c * S_CG:(c + 1) * S_CG, :].rearrange("p g b -> p (g b)")).then_inc(s_ul[c % 2], 16)

    def pool_sp_b(pool, st):
        c = st[1]
        pool.wait_ge(s_ca, c + 1)
        pool.dma_start(CA_d[c].rearrange("p (g m) -> p g m", m=P), ca[:, :, S_H:]).then_inc(s_cst, 16)
        pool.wait_ge(s_kr, c + 1)
        if c == 0:
            pool.wait_ge(s_zst, 16 * S_C)
        pool.dma_start(KD[:, c * S_CG:(c + 1) * S_CG, P:2 * P], krow[0:S_H, :, :]).then_inc(s_kst, 16)
        if c + 2 < S_C:
            pool.wait_ge(s_ba, c + 1)
            load_bc(pool, c + 2)

    def load_pass2(pool, c):
        i = c % 2
        t3 = T2[i].rearrange("p (g m) -> p g m", m=P)
        for j in range(S_L):
            pool.dma_start(t3[j * S_H:(j + 1) * S_H],
                           KD[:, c * S_CG:(c + 1) * S_CG, P - j * S_H:2 * P - j * S_H]).then_inc(s_p2[i], 16)
        pool.dma_start(C2[i], CA_d[c]).then_inc(s_p2[i], 16)
        pool.dma_start(U2[i], U_d[:, c * S_CG:(c + 1) * S_CG, :].rearrange("p g b -> p (g b)")).then_inc(s_p2[i], 16)

    def pool_scan(pool, st):
        pool.wait_ge(*bk.released(("sp_c", S_C - 1), 1))
        pool.wait_ge(s_kst, 16 * S_C)
        pool.wait_ge(s_cst, 16 * S_C)
        load_pass2(pool, 0)
        load_pass2(pool, 1)

    def pool_sp_d(pool, st):
        c = st[1]
        pool.wait_ge(*bk.released(st))
        dst = Y_d.rearrange("g o i b -> i o g b")
        for i in range(S_L):
            pool.dma_start(dst[i, :, c * S_CG:(c + 1) * S_CG, :],
                           ybuf[i * S_H:(i + 1) * S_H, c % 2, :].rearrange("p (g b) -> p g b", b=S_B)).then_inc(s_yst[c % 2], 16)
        if c + 2 < S_C:
            load_pass2(pool, c + 2)

    def pool_y_back(pool, st):
        for i in range(2):
            pool.wait_ge(s_yst[i], 16 * S_L * S_C // 2)
        for c in range(S_C):
            pool.dma_start(ych[:, c, :], Y_d[c * S_CG:(c + 1) * S_CG].rearrange("g o i b -> (g o) (i b)")).then_inc(s_yb, 16)

    def pool_wo(pool, st):
        if st[2] == 0:
            pool.wait_ge(K.y_done, K.y_base[1] + KT)
            for tt in range(TT):
                pool.dma_start(X[:, tt, :], T["x"][0, tt * P:(tt + 1) * P, :]).then_inc(s_back, 16)
            pool.dma_start(K.work[:, 2 * D:3 * D], T["norm_post"][0].partition_broadcast(P)).then_inc(s_fg, 16)

    def pe_ss_par(pe, st):
        pe.wait_ge(s_tb, n_tb)
        bk.take(pe, st)
        for j in range(2):
            mm = nc.tensor.transpose(ps(st)[:, j * S_G:(j + 1) * S_G], araw[0:S_G, j, :], K.ident[0:S_G, 0:S_G])
        mm.then_inc(bk.full_sem(st), 1)
    n_tb = 16 * 9

    def pe_sp_a(pe, st):
        c = st[1]
        pe.wait_ge(s_bc[c % 2], 16 * 7 * (c // 2 + 1))
        bk.take(pe, st, "c")
        for j in range(2):
            mm = nc.tensor.transpose(ps(st, "c")[:, j * P:(j + 1) * P], craw[:, c % 2, j * S_N:j * S_N + P], K.ident[:, :])
        mm.then_inc(bk.full_sem(st, "c"), 1)

    def pe_sp_b(pe, st):
        c = st[1]
        pe.wait_ge(s_ba, c + 1)
        for j in range(2):
            bk.take(pe, st, ("i", j))
            for g in range(4 * j, 4 * j + 4):
                mm = nc.tensor.transpose(ps(st, ("i", j))[:, (g % 4) * P:(g % 4 + 1) * P],
                                         ba[:, g * S_L:(g + 1) * S_L, :], K.ident[:, :])
            mm.then_inc(bk.full_sem(st, ("i", j)), 1)
        pe.wait_ge(s_ca, c + 1)
        for j in range(2):
            bk.take(pe, st, ("k", j))
            for g in range(4 * j, 4 * j + 4):
                mm = nc.tensor.matmul(ps(st, ("k", j))[0:S_H, (g % 4) * P:(g % 4 + 1) * P], lhsT=bst[:, g, :],
                                      rhs=ca[:, g, 0:P], start=True, stop=True)
            mm.then_inc(bk.full_sem(st, ("k", j)), 1)

    def pe_sp_c(pe, st):
        c = st[1]
        for j in range(2):
            pe.wait_ge(*bk.released(("sp_b", c), ("i", j)))
        pe.wait_ge(s_ul[c % 2], 16 * (c // 2 + 1))
        for s in range(2):
            bk.take(pe, st, s)
            for g in range(S_CG):
                o, u = ps(st, s)[:, g * S_B:(g + 1) * S_B], ublk[:, g * S_B:(g + 1) * S_B]
                if s == 0:
                    mm = nc.tensor.matmul(o, lhsT=inm[:, g, :], rhs=u, start=True, stop=True)
                else:
                    for r in range(2):
                        mm = nc.tensor.matmul(o[64 * r:64 * r + 64], lhsT=inm[:, g, 64 * (1 - r):64 * (1 - r) + 64], rhs=u,
                                              start=True, stop=True)
            mm.then_inc(bk.full_sem(st, s), 1)

    def pe_sp_d(pe, st):
        c = st[1]
        if c == 0:
            pe.wait_ge(s_scand, 1)
        pe.wait_ge(s_p2[c % 2], 160 * (c // 2 + 1))
        bk.take(pe, st)
        for g in range(S_CG):
            o = ps(st)[:, g * S_B:(g + 1) * S_B]
            nc.tensor.matmul(o, lhsT=T2[c % 2][:, g * P:(g + 1) * P], rhs=U2[c % 2][:, g * S_B:(g + 1) * S_B], start=True,
                             stop=False)
            mm = nc.tensor.matmul(o[:, 1:S_B], lhsT=C2[c % 2][:, g * P:(g + 1) * P], rhs=vst[:, 0, 0:S_B - 1, c * S_CG + g],
                                  start=False, stop=True)
        mm.then_inc(bk.full_sem(st), 1)

    def pe_rope(pe, st):
        h = st[1]
        pe.wait_ge(s_tab, 48)
        for j, n in enumerate(("qd", "kd")):
            pe.wait_ge(*bk.released(("tile", 1, n, h)))
            bk.take(pe, st, j)
            nc.tensor.matmul(ps(st, j), lhsT=perm[:, :], rhs=raw[:, j, :], start=True, stop=True).then_inc(bk.full_sem(st, j), 1)

    def pe_at_s(pe, st):
        u = st[1]
        kind, h, qb = units[u]
        t_ = slice(qb * P, (qb + 1) * P)
        if kind == "d":
            pe.wait_ge(s_rope, h + 1)
            for c in range(2):
                r = slice(64 * c, 64 * c + 64)
                bk.take(pe, st, c)
                nc.tensor.matmul(ps(st, c)[:, 0:(qb + 1) * P], lhsT=qr[r, h % 2, t_], rhs=kr[r, h % 2, 0:(qb + 1) * P],
                                 start=True, stop=True).then_inc(bk.full_sem(st, c), 1)
        else:
            if qb == 0:
                pe.wait_ge(*bk.released(("tile", 1, "qx", h)))
                pe.wait_ge(*bk.released(("tile", 1, "mk", h)))
            bk.take(pe, st)
            nc.tensor.matmul(ps(st)[:, 0:MEM], lhsT=qr[:, h % 2, t_], rhs=mk[:, h, :], start=True,
                             stop=True).then_inc(bk.full_sem(st), 1)

    def pe_at_t(pe, st):
        u = st[1]
        kind, h, qb = units[u]
        if kind == "d":
            pe.wait_ge(s_w, u + 1)
        else:
            pe.wait_ge(s_exp, 32 + u - 15)
        bk.take(pe, st)
        for kt in range(qb + 1 if kind == "d" else MEM // P):
            mm = nc.tensor.transpose(ps(st)[:, kt * P:(kt + 1) * P], e4[u % 2][0][:, kt * P:(kt + 1) * P], K.ident[:, :])
        mm.then_inc(bk.full_sem(st), 1)

    e4 = [[e[:, p, c, :] for c in range(2)] for p in range(2)]

    def pe_at_v(pe, st):
        u = st[1]
        kind, h, qb = units[u]
        pe.wait_ge(*bk.released(("at_t", u)))
        if kind == "d":
            pe.wait_ge(*bk.released(("tile", 1, "vd", h)))
        else:
            pe.wait_ge(*bk.released(("tile", 1, "mv", h)))
        bk.take(pe, st)
        n = qb + 1 if kind == "d" else MEM // P
        for kt in range(n):
            rhs = v[:, h % 2, kt, :] if kind == "d" else mv[:, kt, h * XA_D:(h + 1) * XA_D]
            mm = nc.tensor.matmul(ps(st)[:, 0:P], lhsT=pT[:, u % 2, kt * P:(kt + 1) * P], rhs=rhs, start=(kt == 0),
                                  stop=(kt == n - 1))
        mm.then_inc(bk.full_sem(st), 1)

    def pe_at_o(pe, st):
        i = st[1] // TT
        pe.wait_ge(s_on, i + 1)
        bk.take(pe, st)
        for tt in range(TT):
            mm = nc.tensor.transpose(ps(st)[:, tt * P:(tt + 1) * P], obuf[:, tt, :], K.ident[:, :])
        mm.then_inc(bk.full_sem(st), 1)

    def act_tile(act, L, st):
        _, _, name, i = st
        b = ps(st)
        if name == "glu":
            if i >= 2:
                act.wait_ge(K.y_done, K.y_base[1] + 8 + i - 1)
            act.wait_ge(*bk.filled(st))
            nc.scalar.activation(sig[:, i % 2, :], b, ACT.Sigmoid, bias=b_glu[:, i:i + 1]).then_inc(bk.free_sem(st), 1)
            return
        if name == "us" and i >= 2:
            act.wait_ge(s_u[(i - 2) % 4], 16 * S_CG * ((i - 2) // 4 + 1))
        if name in ("qd", "kd") and i >= 1:
            act.wait_ge(s_rope, i)
        if name == "vd" and i >= 2:
            act.wait_ge(*bk.filled(("at_v", at["d", i - 2, TT - 1])))
        if name == "qx":
            prev = at["d", DF_H - 2 + i, TT - 1] if i < 2 else at["x", i - 2, TT - 1]
            act.wait_ge(*bk.filled(("at_s", prev), 1 if i < 2 else 0))
        if name == "gd" and i == 0:
            act.wait_ge(*bk.filled(mt[-1]))
        if name == "gs" and i == 0:
            act.wait_ge(*bk.filled(("sp_d", S_C - 1)))
        act.wait_ge(*bk.filled(st))
        if name == "us":
            ins = nc.scalar.activation(us[:, i % 2, :].rearrange("p (j b) -> p j b", b=S_B),
                                       b.rearrange("p (b j) -> p j b", j=S_L), ACT.Copy)
        elif name == "mk":
            ins = nc.scalar.activation(mk[:, i, :], b[:, 0:MEM], ACT.Copy)
        elif name == "mv":
            ins = nc.scalar.activation(mv[:, :, i * P:(i + 1) * P], b[:, 0:MEM].rearrange("p (t c) -> p t c", c=P), ACT.Copy)
        elif name == "gd":
            ins = nc.scalar.activation(yT[:, 8 + i, :], b, ACT.Silu)
        elif name == "gx":
            ins = nc.scalar.activation(yT[:, 12 + i, :], b, ACT.Silu)
        elif name == "gs":
            ins = nc.scalar.activation(yT[:, i, :], b, ACT.Silu)
        elif name == "qd":
            ins = nc.scalar.activation(raw[:, 0, :], b, ACT.Copy, scale=DF_D ** -0.5)
        elif name == "kd":
            ins = nc.scalar.activation(raw[:, 1, :], b, ACT.Copy)
        elif name == "vd":
            ins = nc.scalar.activation(v[:, i % 2, :, :], b.rearrange("p (t c) -> p t c", c=P), ACT.Copy)
        elif name == "qx":
            ins = nc.scalar.activation(qr[:, i % 2, :], b, ACT.Copy)
        ins.then_inc(bk.free_sem(st), 1)

    def act_ss_par(act, L, st):
        act.wait_ge(s_tb, n_tb)
        nc.scalar.activation(tm[0], logdt, ACT.Exp).then_inc(s_sa, 1)
        act.wait_ge(s_sv, 1)
        nc.scalar.activation(tm[1], tm[1], ACT.Exp).then_inc(s_sa, 1)
        nc.scalar.activation(lamp, lamp, ACT.Exp).then_inc(s_sa, 1)
        act.wait_ge(s_sv, 2)
        nc.scalar.activation(tm[4], tm[3], ACT.Sin).then_inc(s_sa, 1)
        nc.scalar.activation(tm[5], tm[3], ACT.Sin, scale=0.5).then_inc(s_sa, 1)

    def act_rope_tab(act, L, st):
        act.wait_ge(s_sv, 3)
        nc.scalar.activation(ropeS, ang, ACT.Sin).then_inc(s_sa, 1)
        nc.scalar.activation(half, ang, ACT.Sin, scale=0.5).then_inc(s_sa, 1)

    def act_sp_b(act, L, st):
        c = st[1]
        for j in range(2):
            act.wait_ge(*bk.filled(st, ("i", j)))
            if c >= 1 and j == 0:
                act.wait_ge(*bk.filled(("sp_c", c - 1), 1))
            nc.scalar.activation(inm[:, 4 * j:4 * j + 4, :].rearrange("p g m -> p (g m)"), ps(st, ("i", j)),
                                 ACT.Copy).then_inc(bk.free_sem(st, ("i", j)), 1)
        for j in range(2):
            act.wait_ge(*bk.filled(st, ("k", j)))
            if j == 0:
                act.wait_ge(s_zst, 16 * S_C)
                if c >= 1:
                    act.wait_ge(s_kst, 16 * c)
            nc.scalar.activation(krow[0:S_H, 4 * j:4 * j + 4, :].rearrange("p g m -> p (g m)"), ps(st, ("k", j))[0:S_H, :],
                                 ACT.Copy).then_inc(bk.free_sem(st, ("k", j)), 1)

    def act_sp_c(act, L, st):
        c = st[1]
        if c == 0:
            for i in range(4):
                act.wait_ge(s_u[i], 32 * S_CG)
        act.wait_ge(*bk.filled(st, 0))
        nc.scalar.activation(vst[:, 0, :, c * S_CG:(c + 1) * S_CG].rearrange("p b g -> p g b"),
                             ps(st, 0).rearrange("p (g b) -> p g b", b=S_B), ACT.Copy).then_inc(bk.free_sem(st, 0), 1)

    def act_sp_d(act, L, st):
        c = st[1]
        if c >= 2:
            act.wait_ge(s_yst[c % 2], 16 * S_L * (c // 2))
        act.wait_ge(*bk.filled(st))
        nc.scalar.activation(ybuf[:, c % 2, :], ps(st), ACT.Copy).then_inc(bk.free_sem(st), 1)

    def act_gelu(act, L, st):
        act.wait_ge(s_yb, 16 * S_C)
        for c in range(S_C):
            nc.scalar.activation(ych[:, c, :], ych[:, c, :], ACT.Gelu_apprx_tanh).then_inc(s_gelu, 1)

    def act_at_s(act, L, st):
        u = st[1]
        kind, h, qb = units[u]
        if kind == "d":
            for c in range(2):
                act.wait_ge(s_score, 2 * u + c + 1)
                x = e4[u % 2][c][:, 0:(qb + 1) * P]
                nc.scalar.activation(x, x, ACT.Exp, bias=mx[:, u % 2, c:c + 1],
                                     accum_out=sums[:, u % 4, c:c + 1]).then_inc(s_exp, 1)
        else:
            act.wait_ge(s_score, 32 + u - 15)
            act.wait_ge(*bk.filled(("at_t", u - 2)))
            nc.scalar.activation(e4[u % 2][0][:, 0:MEM], ps(st)[:, 0:MEM], ACT.Exp, bias=mx[:, u % 2, 0:1],
                                 scale=XA_D ** -0.5, accum_out=sums[:, u % 4, 0:1]).then_inc(s_exp, 1)
            act.wait_ge(s_exp, 32 + u - 15)
            act.sem_inc(bk.free_sem(st), 1)

    def act_at_t(act, L, st):
        u = st[1]
        kind, h, qb = units[u]
        n = (qb + 1) * P if kind == "d" else MEM
        if u >= 2:
            act.wait_ge(*bk.filled(("at_v", u - 2)))
        act.wait_ge(*bk.filled(st))
        nc.scalar.activation(pT[:, u % 2, 0:n], ps(st)[:, 0:n], ACT.Copy).then_inc(bk.free_sem(st), 1)

    def act_at_o(act, L, st):
        i = st[1] // TT
        if i < DF_H:
            act.wait_ge(s_oss, i + 1)
            nc.scalar.activation(oss, oss, ACT.Sqrt, scale=1.0 / DF_V, bias=K.eps[:, 0:1]).then_inc(s_ort, 1)

    def act_wo(act, L, st):
        n = st[2]
        mix = K.A.rearrange("p (t d) -> p t d", d=D)
        for tt in range(TT):
            act.wait_ge(*bk.filled(st, tt))
            nc.scalar.activation(mix[:, tt, n * NC:(n + 1) * NC], ps(st, tt), ACT.Copy).then_inc(bk.free_sem(st, tt), 1)

    def act_final(act, L, st):
        tt = st[2]
        mix = K.A.rearrange("p (t d) -> p t d", d=D)
        act.wait_ge(*bk.released(("wo", 1, 3), tt))
        K.act_rstd(act, L, st, mix[:, tt, :], K.hn_junk)
        act.wait_ge(K.s_ss, K.norms[st] + 1)

    def reduce_angle(vec, L, x, turns):
        L(nc.vector.tensor_scalar(turns, x, 1.0 / (2.0 * math.pi), MAGIC, ALU.mult, ALU.add))
        L.settle()
        L(nc.vector.tensor_scalar(turns, turns, MAGIC, None, ALU.subtract))
        L.settle()
        for part in TWO_PI:
            L(nc.vector.scalar_tensor_tensor(x, turns, -part, x, ALU.mult, ALU.add))
            L.settle()
        L(nc.vector.tensor_scalar(x, x, PI_DOWN, -PI_DOWN, ALU.min, ALU.max))
        L.settle()

    def vec_ss_par(vec, L, st):
        def op(fn, *a_):
            L(fn(*a_))
            L.settle()
        tt_ = nc.vector.tensor_tensor
        vec.wait_ge(s_par, K.par_count[1])
        vec.wait_ge(*bk.filled(st))
        lr, li = tm[6], tm[7]
        L(nc.vector.tensor_copy(lr, ps(st)[:, 0:S_G]))
        L(nc.vector.tensor_copy(li, ps(st)[:, S_G:2 * S_G]))
        L.settle()
        vec.sem_inc(bk.free_sem(st), 1)
        for j in range(2):
            L(nc.vector.tensor_tensor_reduce(lqk_j, lqk[:, 2 * j, :], lqk[:, 2 * j + 1, :], 1.0, 0.0, ALU.mult, ALU.add,
                                             lamp[:, j:j + 1]))
            L.settle()
        vec.wait_ge(s_sa, 1)
        op(tt_, tm[3], li, tm[0], ALU.mult)
        nc.vector.tensor_tensor(tm[1], lr, tm[0], ALU.mult).then_inc(s_sv, 1)
        reduce_angle(vec, L, tm[3], tm[8])
        vec.sem_inc(s_sv, 1)
        vec.wait_ge(s_sa, 5)
        op(tt_, nlam, lamp[:, 1:2], lamp[:, 0:1], ALU.subtract)
        op(nc.vector.tensor_scalar, nlam, nlam, LAMBDA_INIT, None, ALU.subtract)
        op(nc.vector.tensor_scalar, subln, subln, 1.0 - LAMBDA_INIT, None, ALU.mult)
        ar, ai, mag = tm[9], tm[10], tm[1]
        op(tt_, tm[5], tm[5], tm[5], ALU.mult)
        op(nc.vector.tensor_scalar, tm[5], tm[5], -2.0, 1.0, ALU.mult, ALU.add)
        op(tt_, ar, mag, tm[5], ALU.mult)
        op(tt_, ai, mag, tm[4], ALU.mult)
        nr, den, x = tm[11], tm[12], tm[13]
        op(nc.vector.tensor_scalar, nr, ar, 1.0, None, ALU.subtract)
        op(tt_, den, lr, lr, ALU.mult)
        op(tt_, x, li, li, ALU.mult)
        op(tt_, den, den, x, ALU.add)
        op(nc.vector.reciprocal, den, den)
        op(tt_, z_re, nr, lr, ALU.mult)
        op(tt_, x, ai, li, ALU.mult)
        op(tt_, z_re, z_re, x, ALU.add)
        op(tt_, z_re, z_re, den, ALU.mult)
        op(tt_, z_im, ai, lr, ALU.mult)
        op(tt_, x, nr, li, ALU.mult)
        op(tt_, z_im, z_im, x, ALU.subtract)
        op(tt_, z_im, z_im, den, ALU.mult)
        op(nc.vector.tensor_scalar, z_im, z_im, sgn[:, 0:1], None, ALU.mult)
        op(nc.vector.memset, pc_re[:, :, 0], 1.0)
        op(nc.vector.memset, pc_im[:, :, 0], 0.0)
        for k in range(1, S_L + 1):
            pr, pi, nr_, ni_ = pc_re[:, :, k - 1], pc_im[:, :, k - 1], pc_re[:, :, k], pc_im[:, :, k]
            op(tt_, nr_, pr, ar, ALU.mult)
            op(tt_, x, pi, ai, ALU.mult)
            op(tt_, nr_, nr_, x, ALU.subtract)
            op(tt_, ni_, pr, ai, ALU.mult)
            op(tt_, x, pi, ar, ALU.mult)
            op(tt_, ni_, ni_, x, ALU.add)
        op(nc.vector.tensor_copy, l_re, pc_re[:, :, S_L])
        op(nc.vector.tensor_scalar, l_im[:, 0, :], pc_im[:, :, S_L], sgn[:, 0:1], None, ALU.mult)
        op(nc.vector.tensor_scalar, l_im[:, 1, :], pc_im[:, :, S_L], sgn[:, 1:2], None, ALU.mult)
        for j in range(S_L):
            op(nc.vector.tensor_copy, pb_re[:, :, j], pc_re[:, :, S_L - 1 - j])
            op(nc.vector.tensor_scalar, pb_im[:, :, j], pc_im[:, :, S_L - 1 - j], sgn[:, 0:1], None, ALU.mult)
        op(nc.vector.tensor_scalar, pc_re, pc_re, sgn[:, 1:2], None, ALU.mult)
        op(nc.vector.tensor_scalar, pc_im, pc_im, -1.0, None, ALU.mult)
        vec.sem_inc(s_pow, 1)

    def vec_rope_tab(vec, L, st):
        vec.wait_ge(s_tab, 48)
        L(nc.vector.tensor_copy(ang, pos_i))
        L.settle()
        L(nc.vector.tensor_scalar(ang, ang, invf[:, 0:1], None, ALU.mult))
        L.settle()
        reduce_angle(vec, L, ang, kk_)
        vec.sem_inc(s_sv, 1)
        vec.wait_ge(s_sa, 7)
        L(nc.vector.tensor_tensor(half, half, half, ALU.mult))
        L.settle()
        L(nc.vector.tensor_scalar(ropeC, half, -2.0, 1.0, ALU.mult, ALU.add))
        L.settle()

    def vec_sp_a(vec, L, st):
        c = st[1]
        g = slice(c * S_CG, (c + 1) * S_CG)
        i = c % 2
        gh = lambda ap: ap[:, g].unsqueeze(2).to_broadcast([P, S_CG, S_H])
        b1, b2 = (braw[:, 2 * i + j, :].rearrange("p (g h) -> p g h", h=S_H) for j in range(2))
        t2 = tmp.rearrange("p a b -> p (a b)")
        x = t2[:, 0:S_CG * S_H].rearrange("p (g h) -> p g h", h=S_H)
        x2 = t2[:, S_CG * S_H:2 * S_CG * S_H].rearrange("p (g h) -> p g h", h=S_H)
        tt_ = nc.vector.tensor_tensor
        vec.wait_ge(s_bc[i], 16 * 7 * (c // 2 + 1))
        if c >= 1:
            vec.wait_ge(*bk.filled(("sp_b", c - 1), ("k", 1)))
        L(tt_(bst, b1, gh(z_re), ALU.mult))
        L(tt_(x, b2, gh(z_im), ALU.mult))
        L(tt_(bsw, b2, gh(z_re), ALU.mult))
        L(tt_(x2, b1, gh(z_im), ALU.mult))
        L.settle()
        L(tt_(bst, bst, x, ALU.add))
        L(tt_(bsw, bsw, x2, ALU.subtract))
        L.settle()
        four = [P, S_CG, S_L, S_H]
        ba4 = ba.rearrange("p (g j) h -> p g j h", j=S_L)
        x4 = t2[:, 0:S_CG * S_L * S_H].rearrange("p (g j h) -> p g j h", j=S_L, h=S_H)
        L(tt_(ba4, pb_re[:, g, :].unsqueeze(3).to_broadcast(four), bst[:, :, :].unsqueeze(2).to_broadcast(four), ALU.mult))
        L(tt_(x4, pb_im[:, g, :].unsqueeze(3).to_broadcast(four), bsw[:, :, :].unsqueeze(2).to_broadcast(four), ALU.mult))
        L.settle()
        nc.vector.tensor_tensor(ba4, ba4, x4, ALU.add).then_inc(s_ba, 1)
        vec.wait_ge(s_ba, c + 1)
        four = [P, S_CG, S_L + 1, S_H]
        ca4 = ca.rearrange("p g (j h) -> p g j h", h=S_H)
        x4 = t2[:, 0:S_CG * (S_L + 1) * S_H].rearrange("p (g j h) -> p g j h", j=S_L + 1, h=S_H)
        cs, cw_ = (ps(("sp_a", c), "c")[:, j * P:(j + 1) * P].rearrange("p (g h) -> p g h", h=S_H) for j in range(2))
        vec.wait_ge(*bk.filled(st, "c"))
        if c >= 1:
            vec.wait_ge(s_cst, 16 * c)
        L(tt_(ca4, pc_re[:, g, :].unsqueeze(3).to_broadcast(four), cs.unsqueeze(2).to_broadcast(four), ALU.mult))
        nc.vector.tensor_tensor(x4, pc_im[:, g, :].unsqueeze(3).to_broadcast(four), cw_.unsqueeze(2).to_broadcast(four),
                                ALU.mult).then_inc(bk.free_sem(st, "c"), 1)
        vec.wait_ge(*bk.released(st, "c"))
        L.settle()
        nc.vector.tensor_tensor(ca4, ca4, x4, ALU.add).then_inc(s_ca, 1)
        vec.wait_ge(s_ca, c + 1)

    def vec_sp_b(vec, L, st):
        c = st[1]
        g = slice(c * S_CG, (c + 1) * S_CG)
        x = tmp.rearrange("p a b -> p (a b)")[0:S_H, 0:S_CG * S_H].rearrange("p (g h) -> p g h", h=S_H)
        three = [S_H, S_CG, S_H]
        L(nc.vector.tensor_tensor(x, d_skip[0:S_H, g].unsqueeze(2).to_broadcast(three),
                                  K.ident[0:S_H, 0:S_H].unsqueeze(1).to_broadcast(three), ALU.mult))
        L.settle()
        for j in range(2):
            vec.wait_ge(*bk.released(st, ("k", j)))
        k0 = krow[0:S_H, :, 0:S_H]
        nc.vector.tensor_tensor(k0, k0, x, ALU.add).then_inc(s_kr, 1)
        vec.wait_ge(s_kr, c + 1)

    def vec_sp_c(vec, L, st):
        c = st[1]
        if c == 0:
            for i in range(4):
                vec.wait_ge(s_u[i], 32 * S_CG)
        vec.wait_ge(*bk.filled(st, 1))
        nc.vector.tensor_copy(vst[:, 1, :, c * S_CG:(c + 1) * S_CG].rearrange("p b g -> p g b"),
                              ps(st, 1).rearrange("p (g b) -> p g b", b=S_B)).then_inc(bk.free_sem(st, 1), 1)

    def vec_scan(vec, L, st):
        vec.wait_ge(*bk.released(("sp_c", S_C - 1), 0))
        vec.wait_ge(*bk.released(("sp_c", S_C - 1), 1))
        t1, t2 = scan_t[:, 0:2, :], scan_t[:, 2:4, :]
        lre2 = l_re.unsqueeze(1).to_broadcast([P, 2, S_G])
        with vec.Fori(0, S_B - 1) as b:
            x0 = vst[:, :, bass.ds(b, 1), :].rearrange("p s o g -> p s (o g)")
            x1 = vst[:, :, bass.ds(b + 1, 1), :].rearrange("p s o g -> p s (o g)")
            nc.vector.tensor_tensor(t1, x0, lre2, ALU.mult).then_inc(s_scan, 1)
            nc.vector.tensor_tensor(t2[:, 0, :], x0[:, 1, :], l_im[:, 0, :], ALU.mult).then_inc(s_scan, 1)
            nc.vector.tensor_tensor(t2[:, 1, :], x0[:, 0, :], l_im[:, 1, :], ALU.mult).then_inc(s_scan, 1)
            vec.wait_ge(s_scan, b * 5 + 3)
            nc.vector.tensor_tensor(t1, t1, t2, ALU.add).then_inc(s_scan, 1)
            vec.wait_ge(s_scan, b * 5 + 4)
            nc.vector.tensor_tensor(x1, x1, t1, ALU.add).then_inc(s_scan, 1)
            vec.wait_ge(s_scan, b * 5 + 5)
        vec.sem_inc(s_scand, 1)

    def vec_rope(vec, L, st):
        h = st[1]
        for j, dst in enumerate((qr, kr)):
            vec.wait_ge(*bk.filled(st, j))
            if h >= 2 and j == 0:
                vec.wait_ge(*bk.filled(("at_s", at["d", h - 2, TT - 1]), 1))
            o, x = dst[:, h % 2, :], rope_t[:, j, :]
            L(nc.vector.tensor_tensor(o, raw[:, j, :], ropeC[:, :], ALU.mult))
            nc.vector.tensor_tensor(x, ps(st, j), ropeS[:, :], ALU.mult).then_inc(bk.free_sem(st, j), 1)
            vec.wait_ge(*bk.released(st, j))
            L.settle()
            L(nc.vector.tensor_tensor(o, o, x, ALU.add))
        L.settle()
        vec.sem_inc(s_rope, 1)

    def vec_tile(vec, L, st):
        _, _, name, i = st
        if name == "glu":
            vec.wait_ge(*bk.released(st))
            s_ = sig[:, i % 2, :]
            L(nc.vector.tensor_tensor(s_, ych[:, i, :], s_, ALU.mult))
            L.settle()
            y = yT[:, i, :].rearrange("p (b j) -> p j b", j=S_L)
            nc.vector.tensor_tensor(y, y, s_.rearrange("p (j b) -> p j b", b=S_B), ALU.mult).then_inc(K.y_done, 1)

    def vec_at_s(vec, L, st):
        u = st[1]
        kind, h, qb = units[u]
        nk = (qb + 1) * P
        if kind == "d":
            if u >= 2:
                vec.wait_ge(*bk.filled(("at_t", u - 2)))
            for c in range(2):
                vec.wait_ge(*bk.filled(st, c))
                m = mx[:, u % 2, c:c + 1]
                nc.vector.tensor_tensor_reduce(e4[u % 2][c][:, 0:nk], ps(st, c)[:, 0:nk], tri[:, SEQ - nk:SEQ], 1.0, -3e38,
                                               ALU.add, ALU.max, m).then_inc(bk.free_sem(st, c), 1)
                vec.wait_ge(*bk.released(st, c))
                nc.vector.tensor_scalar(m, m, -1.0, None, ALU.mult).then_inc(s_score, 1)
        else:
            m = mx[:, u % 2, 0:1]
            vec.wait_ge(s_exp, 32 + u - 17 if u >= 18 else 2 * (u - 1))
            vec.wait_ge(*bk.filled(st))
            nc.vector.tensor_reduce(m, ps(st)[:, 0:MEM], AX.X, ALU.max).then_inc(bk.free_sem(st), 1)
            vec.wait_ge(*bk.read_once(st))
            nc.vector.tensor_scalar(m, m, -XA_D ** -0.5, None, ALU.mult).then_inc(s_score, 1)

    def vec_at_t(vec, L, st):
        u = st[1]
        kind, h, qb = units[u]
        if kind != "d":
            return
        nk = (qb + 1) * P
        vec.wait_ge(s_exp, 2 * u + 2)
        r = rs[:, u % 2, :]
        L(nc.vector.reciprocal(r, sums[:, u % 4, :]))
        L.settle()
        L(nc.vector.tensor_tensor(r[:, 1:2], r[:, 1:2], nlam, ALU.mult))
        e0, e1 = (e4[u % 2][c][:, 0:nk] for c in range(2))
        L(nc.vector.tensor_scalar(e0, e0, r[:, 0:1], None, ALU.mult))
        L.settle()
        nc.vector.scalar_tensor_tensor(e0, e1, r[:, 1:2], e0, ALU.mult, ALU.add).then_inc(s_w, 1)

    def vec_at_v(vec, L, st):
        u = st[1]
        kind, h, qb = units[u]
        if qb == 0 and u >= TT:
            vec.wait_ge(*bk.filled(("at_o", u - 1)))
        vec.wait_ge(*bk.filled(st))
        if kind == "d":
            nc.vector.tensor_copy(obuf[:, qb, :], ps(st)[:, 0:P]).then_inc(bk.free_sem(st), 1)
        else:
            r = rs[:, u % 2, 0:1]
            vec.wait_ge(s_exp, 32 + u - 15)
            L(nc.vector.reciprocal(r, sums[:, u % 4, 0:1]))
            L.settle()
            nc.vector.tensor_scalar(obuf[:, qb, :], ps(st)[:, 0:P], r, None, ALU.mult).then_inc(bk.free_sem(st), 1)
        vec.wait_ge(*bk.released(st))

    def vec_at_o(vec, L, st):
        u = st[1]
        i = u // TT
        if i < DF_H:
            for tt in range(TT):
                L(nc.vector.tensor_tensor_reduce(rope_t[:, 0, 0:P], obuf[:, tt, :], obuf[:, tt, :], 1.0, 0.0, ALU.mult, ALU.add,
                                                 oss[:, tt:tt + 1]))
                L.settle()
            vec.sem_inc(s_oss, 1)
            vec.wait_ge(s_ort, i + 1)
            L(nc.vector.reciprocal(oss, oss))
            L.settle()
            L(nc.vector.tensor_tensor(obuf, obuf, oss.unsqueeze(2).to_broadcast([P, TT, P]), ALU.mult))
            L.settle()
        vec.sem_inc(s_on, 1)
        vec.wait_ge(*bk.filled(st))
        y = yT[:, 8 + i, :]
        gate = ("tile", 1, "gd", i) if i < DF_H else ("tile", 1, "gx", i - DF_H)
        vec.wait_ge(*bk.released(gate))
        if i < DF_H:
            nc.vector.scalar_tensor_tensor(y, ps(st), subln[:, 0:1], y, ALU.mult, ALU.mult).then_inc(bk.free_sem(st), 1)
        else:
            nc.vector.tensor_tensor(y, ps(st), y, ALU.mult).then_inc(bk.free_sem(st), 1)
        vec.wait_ge(*bk.released(st))
        vec.sem_inc(K.y_done, 1)

    def vec_final(vec, L, st):
        tt = st[2]
        mix = K.A.rearrange("p (t d) -> p t d", d=D)[:, tt, :]
        K.vec_rstd(vec, L, st)
        if tt == 0:
            vec.wait_ge(s_fg, 16)
            vec.wait_ge(s_back, 16 * TT)
        L(nc.vector.scalar_tensor_tensor(mix, mix, K.rstd[:, tt:tt + 1], K.work[:, 2 * D:3 * D], ALU.mult, ALU.mult))
        L.settle()
        nc.vector.tensor_tensor(X[:, tt, :], X[:, tt, :], mix, ALU.add).then_inc(K.x_done, 1)

    K.y_base[1] = K.y_count
    K.y_count += KT
    K.wo_src[1] = (T["w_out"][0], yT)
    K.params.append(pool_params)
    K.wait_gain[1] = K.wait_gain["mem"] = lambda vec: vec.wait_ge(s_par, K.par_count[1])
    K.tiles[glu[0]]["wait"] = lambda pe: pe.wait_ge(s_gelu, S_C)
    K.stage("pool", b1_tables=pool_tables, rope_tab=pool_rope_tab, tile1=pool_tile, sp_a=pool_sp_a, sp_b=pool_sp_b,
            scan=pool_scan, sp_d=pool_sp_d, y_back=pool_y_back, wo1=pool_wo)
    K.stage("pe", ss_par=pe_ss_par, sp_a=pe_sp_a, sp_b=pe_sp_b, sp_c=pe_sp_c, sp_d=pe_sp_d, rope=pe_rope,
            at_s=pe_at_s, at_t=pe_at_t, at_v=pe_at_v, at_o=pe_at_o)
    K.stage("act", tile1=act_tile, ss_par=act_ss_par, rope_tab=act_rope_tab, sp_b=act_sp_b, sp_c=act_sp_c, sp_d=act_sp_d,
            gelu=act_gelu, at_s=act_at_s, at_t=act_at_t, at_o=act_at_o, wo1=act_wo, final1=act_final)
    K.stage("vec", tile1=vec_tile, ss_par=vec_ss_par, rope_tab=vec_rope_tab, sp_a=vec_sp_a, sp_b=vec_sp_b, sp_c=vec_sp_c,
            scan=vec_scan, rope=vec_rope, at_s=vec_at_s, at_t=vec_at_t, at_v=vec_at_v, at_o=vec_at_o, final1=vec_final)
    return script


C2_CONV = 1024
C2_DK = 512
C2_V = 1024
GLA_H = 4
GLA_K = C2_DK // GLA_H
GLA_VD = C2_V // GLA_H
GLA_CH = 64
GLA_NC = SEQ // GLA_CH
GLA_TAU = 16.0


def block2(K):
    nc, T, ps, bk = K.nc, K.T, K.ps, K.bk
    hT, yT, X = K.B_kt, K.A_kt, K.X
    a = K.arena()
    tmp_h = a("b2_ch", 2, NC)
    tmp_u = a("b2_u", 2, NC + 2)
    tmp_y = a("b2_y", 2, NC)
    tmp_z = a("b2_z", 2, NC)
    gd = a("b2_gd", NC)
    q = a("b2_q", 2, NC)
    k = a("b2_k", 2, NC)
    v = a("b2_v", 2, TT, GLA_VD)
    r = a("b2_r", 2, 2, NC)
    ab = a("b2_ab", NC)
    mn = a("b2_mn", NC)
    bcum = a("b2_bcum", NC)
    dec = a("b2_dec", GLA_NC)
    kd = a("b2_kd", NC)
    kn = a("b2_kn", TT, P)
    state = a("b2_state", GLA_NC, GLA_VD)
    sq = a("b2_sq", 2, NC)
    rs = a("b2_rs", NC)
    fg = K.work[:, 2 * D:3 * D]
    prm = K.keep(16 + 24 + 8 + 4 + 8)
    norm_g, conv_w, conv_b = prm[:, 0:16], prm[:, 16:40], prm[:, 40:48]
    b_gate, gla_g = prm[:, 48:52], prm[:, 52:60]
    w_up = K.keep(C2_DK)
    K.norm_gain[2] = (norm_g, None)

    col, c0 = {}, 0
    for n, w in (("ch", 1024), ("cb", 1024), ("cc", 1024), ("cz", 1024),
                 ("gq", 512), ("gk", 512), ("gv", 1024), ("gr", 1024), ("gd", 16)):
        col[n] = c0
        c0 += w

    def tile(name, i, mode="T", w=P):
        st = ("tile", 2, name, i)
        K.tile(st, [(T["w_in_2"][0], col[name] + i * P, w)], mode, w, hT, SEQ)
        return st

    script = [("norm", 2, tt) for tt in range(TT)]
    script.append(tile("gd", 0, w=16))
    K.after_norm(script[-1], 2)
    heads = []
    for h in range(GLA_H):
        heads.append([tile("gk", h), tile("gq", h), tile("gv", 2 * h, "N"), tile("gv", 2 * h + 1, "N"),
                      tile("gr", 2 * h), tile("gr", 2 * h + 1)])
    convs = [[tile(n, i) for n in ("ch", "cc", "cb", "cz")] for i in range(8)]
    for h in range(GLA_H):
        t = heads[h]
        script += [t[0], ("gla_gate", h), t[1], ("gla_kt", h), t[2], t[3], ("gla_u", h), t[4], ("gla_o", h), t[5],
                   ("gla_ss", h)]
    for c in convs:
        script += c
    script += [("wo", 2, n) for n in range(4)]
    script += [("final", 2, tt) for tt in range(TT)]
    for st in script:
        if st[0] == "gla_gate":
            K.uses[st] = [("x", "S", 2)]
        elif st[0] == "gla_kt":
            K.uses[st] = [("t", "S", 1)]
        elif st[0] == "gla_u":
            K.uses[st] = [((half, par), "S", 1) for half in range(2) for par in range(2)]
        elif st[0] == "gla_o":
            K.uses[st] = [(0, "S", 2), (1, "S", 2)]
        elif st[0] == "gla_ss":
            K.uses[st] = [("s", "S", 1)]

    s_par = K.sem("b2_params")
    s_fg = K.sem("final_gain_2_loaded")
    s_kd = K.sem("gla_kd_ready")
    s_state = K.sem("gla_state_ready")
    s_sq = K.sem("gla_squares_ready")
    s_act = K.sem("gla_act_ready")
    s_vec = K.sem("gla_vec_ready")
    s_conv = K.sem("conv_vec_done")

    def pool_params(pool):
        n = 0
        with nc.allow_non_contiguous_dma(reason="small per-channel parameters"):
            for dst, src in ((norm_g, T["norm_g_2"].rearrange("o (k p) -> p (o k)", p=P)),
                             (conv_b, T["conv_b_2"].rearrange("o (k p) -> p (o k)", p=P)),
                             (b_gate, T["gla_b_gate_2"].rearrange("o (k p) -> p (o k)", p=P)),
                             (gla_g, T["gla_norm_g_2"].rearrange("o h (j p) -> p (o h j)", p=P)),
                             (conv_w[:, 0:8], T["conv_w_2"][0, 0:1].rearrange("o (k p) -> p (o k)", p=P)),
                             (conv_w[:, 8:16], T["conv_w_2"][0, 1:2].rearrange("o (k p) -> p (o k)", p=P)),
                             (conv_w[:, 16:24], T["conv_w_2"][0, 2:3].rearrange("o (k p) -> p (o k)", p=P)),
                             (w_up[0:16, :], T["gla_w_up_2"][0])):
                pool.dma_start(dst, src).then_inc(s_par, 16)
                n += 16
        K.par_count[2] = n

    def pool_final_gain(pool, st):
        if st[2] == 0:
            pool.wait_ge(*bk.filled(st, 0))
            pool.dma_start(fg, T["final_g_2"].partition_broadcast(P)).then_inc(s_fg, 16)

    def pe_gate(pe, st):
        h = st[1]
        pe.wait_ge(*bk.released(("tile", 2, "gd", 0)))
        if h == 0:
            pe.wait_ge(s_par, K.par_count[2])
        bk.take(pe, st, "x")
        nc.tensor.matmul(ps(st, "x"), lhsT=w_up[0:16, h * P:(h + 1) * P], rhs=gd[0:16, :], start=True,
                         stop=True).then_inc(bk.full_sem(st, "x"), 1)

    def pe_kt(pe, st):
        h = st[1]
        pe.wait_ge(s_kd, h + 1)
        bk.take(pe, st, "t")
        for tt in range(TT):
            mm = nc.tensor.transpose(ps(st, "t")[:, tt * P:(tt + 1) * P], kd[:, tt * P:(tt + 1) * P], K.ident[:, :])
        mm.then_inc(bk.full_sem(st, "t"), 1)

    def pe_u(pe, st):
        h = st[1]
        pe.wait_ge(*bk.released(("gla_kt", h), "t"))
        pe.wait_ge(*bk.released(("tile", 2, "gv", 2 * h)))
        pe.wait_ge(*bk.released(("tile", 2, "gv", 2 * h + 1)))
        for half in range(2):
            for par in range(2):
                bk.take(pe, st, (half, par))
                for j in range(2):
                    tt = 2 * half + j
                    rows = slice(par * GLA_CH, (par + 1) * GLA_CH)
                    mm = nc.tensor.matmul(ps(st, (half, par))[:, j * GLA_VD:(j + 1) * GLA_VD], lhsT=kn[rows, tt, :],
                                          rhs=v[rows, h % 2, tt, :], start=True, stop=True)
                mm.then_inc(bk.full_sem(st, (half, par)), 1)

    def pe_o(pe, st):
        h = st[1]
        pe.wait_ge(s_state, h + 1)
        pe.wait_ge(*bk.released(("tile", 2, "gq", h)))
        for vt in range(2):
            bk.take(pe, st, vt)
            for c in range(GLA_NC):
                mm = nc.tensor.matmul(ps(st, vt)[:, c * GLA_CH:(c + 1) * GLA_CH],
                                      lhsT=state[:, c, vt * P:(vt + 1) * P],
                                      rhs=q[:, h % 2, c * GLA_CH:(c + 1) * GLA_CH], start=True, stop=True)
            mm.then_inc(bk.full_sem(st, vt), 1)

    def pe_ss(pe, st):
        h = st[1]
        pe.wait_ge(s_sq, 2 * h + 2)
        bk.take(pe, st, "s")
        for vt in range(2):
            mm = nc.tensor.matmul(ps(st, "s"), lhsT=K.ones[:, :], rhs=sq[:, vt, :], start=(vt == 0), stop=(vt == 1))
        mm.then_inc(bk.full_sem(st, "s"), 1)

    def act_tile(act, L, st):
        _, _, name, i = st
        b = ps(st)
        if name in ("gd", "gq", "gk", "gv", "gr", "ch", "cz"):
            act.wait_ge(*bk.filled(st))
        if name == "gd":
            ins = nc.scalar.activation(gd[0:16, :], b[0:16, :], ACT.Copy)
        elif name == "gq":
            if i >= 2:
                act.wait_ge(*bk.filled(("gla_o", i - 2), 1))
            ins = nc.scalar.activation(q[:, i % 2, :], b, ACT.Copy, scale=GLA_K ** -0.5)
        elif name == "gk":
            if i >= 2:
                act.wait_ge(s_kd, i - 1)
            ins = nc.scalar.activation(k[:, i % 2, :], b, ACT.Copy)
        elif name == "gv":
            h, j = i // 2, i % 2
            if h >= 2:
                act.wait_ge(*bk.filled(("gla_u", h - 2), (1, 1)))
            ins = nc.scalar.activation(v[:, h % 2, :, j * P:(j + 1) * P], b.rearrange("p (t n) -> p t n", n=P), ACT.Copy)
        elif name == "gr":
            h, j = i // 2, i % 2
            if h >= 2:
                act.wait_ge(K.y_done, K.y_base[2] + 2 * (h - 2) + 2)
            ins = nc.scalar.activation(r[:, h % 2, j, :], b, ACT.Silu)
        elif name == "ch":
            if i >= 2:
                act.wait_ge(s_conv, 2 * (i - 2) + 1)
            ins = nc.scalar.activation(tmp_h[:, i % 2, :], b, ACT.Copy)
        elif name == "cz":
            if i >= 2:
                act.wait_ge(s_conv, 2 * (i - 2) + 2)
            ins = nc.scalar.activation(tmp_z[:, i % 2, :], b, ACT.Silu)
        else:
            return
        ins.then_inc(bk.free_sem(st), 1)

    def act_gate(act, L, st):
        h = st[1]
        if h == 0:
            act.wait_ge(s_par, K.par_count[2])
        act.wait_ge(*bk.filled(st, "x"))
        nc.scalar.activation(ab[:, :], ps(st, "x"), ACT.Abs, bias=b_gate[:, h:h + 1]).then_inc(bk.free_sem(st, "x"), 1)
        act.wait_ge(*bk.read_once(st, "x"))
        L(nc.scalar.activation(ab[:, :], ab[:, :], ACT.Exp, scale=-1.0))
        L.settle()
        nc.scalar.activation(ab[:, :], ab[:, :], ACT.Ln, bias=1.0).then_inc(s_act, 1)
        act.wait_ge(s_vec, h + 1)
        nc.scalar.activation(mn[:, :], mn[:, :], ACT.Exp, scale=1.0 / GLA_TAU).then_inc(s_act, 1)
        nc.scalar.activation(dec[:, :], bcum[:, GLA_CH - 1::GLA_CH], ACT.Exp, scale=1.0 / GLA_TAU).then_inc(s_act, 1)

    def act_kt(act, L, st):
        h = st[1]
        act.wait_ge(*bk.filled(st, "t"))
        if h >= 1:
            act.wait_ge(*bk.filled(("gla_u", h - 1), (1, 1)))
        nc.scalar.activation(kn.rearrange("p t n -> p (t n)"), ps(st, "t"), ACT.Copy).then_inc(bk.free_sem(st, "t"), 1)

    def act_o(act, L, st):
        h = st[1]
        for vt in range(2):
            act.wait_ge(*bk.filled(st, vt))
            if h >= 1 and vt == 0:
                act.wait_ge(*bk.filled(("gla_ss", h - 1), "s"))
                act.wait_ge(K.y_done, K.y_base[2] + 2 * h)
            nc.scalar.activation(sq[:, vt, :], ps(st, vt), ACT.Square).then_inc(s_sq, 1)
            act.wait_ge(s_sq, 2 * h + vt + 1)
            act.sem_inc(bk.free_sem(st, vt), 1)

    def act_ss(act, L, st):
        h = st[1]
        act.wait_ge(*bk.filled(st, "s"))
        if h >= 1:
            act.wait_ge(K.y_done, K.y_base[2] + 2 * h)
        L(nc.scalar.activation(rs[:, :], ps(st, "s"), ACT.Identity, scale=1.0 / GLA_VD, bias=K.eps[:, 0:1]))
        L.settle()
        act.sem_inc(bk.free_sem(st, "s"), 1)
        nc.scalar.activation(rs[:, :], rs[:, :], ACT.Sqrt).then_inc(s_act, 1)

    def vec_tile(vec, L, st):
        _, _, name, i = st
        b = ps(st)
        if name == "cc":
            vec.wait_ge(*bk.filled(st))
            vec.wait_ge(*bk.released(("tile", 2, "ch", i)))
            if i == 0:
                L(nc.vector.memset(tmp_u[:, :, 0:2], 0.0))
                vec.wait_ge(s_par, K.par_count[2])
            u, y = tmp_u[:, i % 2, :], tmp_y[:, i % 2, :]
            nc.vector.tensor_tensor(u[:, 2:NC + 2], b, tmp_h[:, i % 2, :], ALU.mult).then_inc(bk.free_sem(st), 1)
            vec.wait_ge(*bk.released(st))
            L.settle()
            nc.vector.tensor_scalar(y, u[:, 0:NC], conv_w[:, i:i + 1], conv_b[:, i:i + 1], ALU.mult, ALU.add).then_inc(s_conv, 1)
            vec.wait_ge(s_conv, 2 * i + 1)
            for j in (1, 2):
                L(nc.vector.scalar_tensor_tensor(y, u[:, j:NC + j], conv_w[:, 8 * j + i:8 * j + i + 1], y, ALU.mult, ALU.add))
                L.settle()
        elif name == "cb":
            y = tmp_y[:, i % 2, :]
            vec.wait_ge(*bk.filled(st))
            nc.vector.tensor_tensor(y, b, y, ALU.mult).then_inc(bk.free_sem(st), 1)
            vec.wait_ge(*bk.released(st))
        elif name == "cz":
            vec.wait_ge(*bk.released(st))
            y = tmp_y[:, i % 2, :]
            nc.vector.tensor_tensor(yT[:, i, :], y, tmp_z[:, i % 2, :], ALU.mult).then_inc(K.y_done, 1)
            vec.wait_ge(K.y_done, K.y_base[2] + 8 + i + 1)
            vec.sem_inc(s_conv, 1)

    def vec_gate(vec, L, st):
        h = st[1]
        if h == 0:
            vec.wait_ge(s_par, K.par_count[2])
        vec.wait_ge(*bk.read_once(st, "x"))
        L(nc.vector.tensor_scalar(mn[:, :], ps(st, "x"), b_gate[:, h:h + 1], 0.0, ALU.add, ALU.min))
        L.settle()
        vec.sem_inc(bk.free_sem(st, "x"), 1)
        vec.wait_ge(s_act, 4 * h + 1)
        L(nc.vector.tensor_tensor(mn[:, :], mn[:, :], ab[:, :], ALU.subtract))
        L.settle()
        L(nc.vector.tensor_tensor_scan(bcum[:, :], K.reset[:, :], mn[:, :], 0.0, ALU.mult, ALU.add))
        L.settle()
        b3 = bcum.rearrange("p (c l) -> p c l", l=GLA_CH)
        nc.vector.tensor_tensor(mn.rearrange("p (c l) -> p c l", l=GLA_CH),
                                b3[:, :, GLA_CH - 1:GLA_CH].to_broadcast([P, GLA_NC, GLA_CH]), b3,
                                ALU.subtract).then_inc(s_vec, 1)
        vec.wait_ge(s_act, 4 * h + 3)
        vec.wait_ge(*bk.released(("tile", 2, "gk", h)))
        if h >= 1:
            vec.wait_ge(*bk.filled(("gla_kt", h - 1), "t"))
        nc.vector.tensor_tensor(kd[:, :], k[:, h % 2, :], mn[:, :], ALU.mult).then_inc(s_kd, 1)
        vec.wait_ge(s_kd, h + 1)

    def vec_u(vec, L, st):
        h = st[1]
        if h >= 1:
            vec.wait_ge(*bk.filled(("gla_o", h - 1), 1))
        for c in range(GLA_NC):
            tt, par = c // 2, c % 2
            key, j = (tt // 2, par), tt % 2
            u = ps(st, key)[:, j * GLA_VD:(j + 1) * GLA_VD]
            if j == 0:
                vec.wait_ge(*bk.filled(st, key))
            if c == 0:
                L(nc.vector.tensor_copy(state[:, 0, :], u))
            else:
                ins = nc.vector.scalar_tensor_tensor(state[:, c, :], state[:, c - 1, :], dec[:, c:c + 1], u, ALU.mult, ALU.add)
                L(ins)
            L.settle()
            if j == 1:
                vec.sem_inc(bk.free_sem(st, key), 1)
        vec.sem_inc(s_state, 1)

    def vec_ss(vec, L, st):
        h = st[1]
        vec.wait_ge(s_act, 4 * h + 4)
        L(nc.vector.reciprocal(rs[:, :], rs[:, :]))
        L.settle()
        for vt in range(2):
            o = ps(("gla_o", h), vt)
            nc.vector.tensor_tensor(sq[:, vt, :], o, rs[:, :], ALU.mult).then_inc(bk.free_sem(("gla_o", h), vt), 1)
            vec.wait_ge(*bk.released(("gla_o", h), vt))
            vec.wait_ge(*bk.released(("tile", 2, "gr", 2 * h + vt)))
            nc.vector.scalar_tensor_tensor(yT[:, 8 + 2 * h + vt, :], sq[:, vt, :], gla_g[:, 2 * h + vt:2 * h + vt + 1],
                                           r[:, h % 2, vt, :], ALU.mult, ALU.mult).then_inc(K.y_done, 1)

    def vec_wo(vec, L, st):
        n = st[2]
        for tt in range(TT):
            vec.wait_ge(*bk.filled(st, tt))
            xs = X[:, tt, n * NC:(n + 1) * NC]
            nc.vector.tensor_tensor(xs, ps(st, tt), xs, ALU.add).then_inc(bk.free_sem(st, tt), 1)

    def vec_final(vec, L, st):
        tt = st[2]
        K.vec_rstd(vec, L, st)
        vec.wait_ge(s_fg, 16)
        nc.vector.scalar_tensor_tensor(X[:, tt, :], X[:, tt, :], K.rstd[:, tt:tt + 1], fg[:, :], ALU.mult,
                                       ALU.mult).then_inc(K.x_done, 1)

    K.y_base[2] = K.y_count
    K.y_count += 16
    K.params.append(pool_params)
    K.stage("pool", wo2=pool_final_gain)
    K.wait_gain[2] = lambda vec: vec.wait_ge(s_par, K.par_count[2])
    K.stage("pe", gla_gate=pe_gate, gla_kt=pe_kt, gla_u=pe_u, gla_o=pe_o, gla_ss=pe_ss)
    K.stage("act", tile2=act_tile, gla_gate=act_gate, gla_kt=act_kt, gla_o=act_o, gla_ss=act_ss, final2=K.act_rstd_x)
    K.stage("vec", tile2=vec_tile, gla_gate=vec_gate, gla_u=vec_u, gla_ss=vec_ss, wo2=vec_wo, final2=vec_final)
    K.wo_src[2] = (T["w_out_2"][0], yT)
    return script


M_H, M_HD, M_CH, M_TAPS = 4, 256, 64, 4
M_NC = SEQ // M_CH
M_W = M_H * M_HD
N_H, N_G, N_HD = 16, 4, 64
N_HPG = N_H // N_G
C_LEN, C_STEP, C_HID = 32, 16, 128
N_CMP = (SEQ - C_LEN) // C_STEP + 1
ADA_W = 1024
ADA_PARTS = 3 * D // ADA_W
ADA_KP = KT // 2


def ada_stages():
    out = []
    for part in range(ADA_PARTS):
        out += [("ada", part, kp) for kp in range(ADA_KP)] + [("ada_sum", part)]
    return out


def modulation(K):
    nc, T, ps, bk = K.nc, K.T, K.ps, K.bk
    acc = K.sb("ada_acc", ADA_W)
    cT, sc = K.keep(KT), K.keep(KT)
    b_ada, mod = K.keep(3 * KT), K.keep(3 * KT)
    K.mod = mod
    s_c, s_sc = K.sem("c_loaded"), K.sem("silu_c_ready")
    s_used, s_acc = K.sem("ada_slot_used"), K.sem("ada_part_ready")
    K.ada_used = s_used
    K.s_mod = s_mod = K.sem("modulation_ready")

    def pool_params(pool):
        with nc.allow_non_contiguous_dma(reason="small per-channel parameters"):
            pool.dma_start(cT, T["c_3"].rearrange("o (k p) -> p (o k)", p=P)).then_inc(s_c, 16)
            pool.dma_start(b_ada, T["b_ada_3"].rearrange("o (k p) -> p (o k)", p=P)).then_inc(s_c, 16)

    def act_ada(act, L, st):
        if st[1:] == (0, 0):
            act.wait_ge(s_c, 32)
            nc.scalar.activation(sc, cT, ACT.Silu).then_inc(s_sc, 1)

    def vec_ada(vec, L, st):
        _, part, kp = st
        if (part, kp) == (0, 0):
            vec.wait_ge(s_sc, 1)
        if part >= 1 and kp == 0:
            vec.wait_ge(*bk.filled(("ada_sum", part - 1)))
        w = K.slot_ap(st).rearrange("p k c -> p (k c)").rearrange("p (k c) -> p k c", c=ADA_W)
        vec.wait_ge(*K.slot_loaded(st))
        for j in range(2):
            k = 2 * kp + j
            if k == 0:
                ins = nc.vector.tensor_scalar(acc[:, :], w[:, j, :], sc[:, k:k + 1], None, ALU.mult)
            else:
                ins = nc.vector.scalar_tensor_tensor(acc[:, :], w[:, j, :], sc[:, k:k + 1], acc[:, :], ALU.mult, ALU.add)
            if j == 0:
                L(ins)
                L.settle()
        ins.then_inc(s_used, 1)
        vec.wait_ge(s_used, ADA_KP * part + kp + 1)

    def pe_sum(pe, st):
        part = st[1]
        pe.wait_ge(s_used, ADA_KP * (part + 1))
        bk.take(pe, st)
        n = ADA_W // P
        for m in range(n):
            mm = nc.tensor.matmul(ps(st)[:, m:m + 1], lhsT=acc[:, m * P:(m + 1) * P], rhs=K.ones[:, 0:1], start=True, stop=True)
        mm.then_inc(bk.full_sem(st), 1)

    def vec_sum(vec, L, st):
        part, n = st[1], ADA_W // P
        vec.wait_ge(*bk.filled(st))
        if part == 0:
            vec.wait_ge(s_c, 32)
        sl = slice(part * n, (part + 1) * n)
        nc.vector.tensor_tensor(mod[:, sl], ps(st)[:, 0:n], b_ada[:, sl], ALU.add).then_inc(bk.free_sem(st), 1)
        vec.wait_ge(*bk.released(st))

    for st in ada_stages():
        if st[0] == "ada_sum":
            K.uses[st] = [(0, "S", 1)]
    K.params.append(pool_params)
    K.stage("act", ada=act_ada)
    K.stage("vec", ada=vec_ada, ada_sum=vec_sum)
    K.stage("pe", ada_sum=pe_sum)


def block3(K):
    nc, T, ps, bk = K.nc, K.T, K.ps, K.bk
    hT, yT, X = K.A_kt, K.B_kt, K.X
    if not K.modulated:
        modulation(K)
    ln_g, gain = K.keep(KT), K.keep(KT)
    cw, cb, nw, skip = K.keep(M_TAPS * 8), K.keep(8), K.keep(8), K.keep(8)
    fb = K.keep(1)
    bias = {n: K.keep(w) for n, w in (("mx", 8), ("mo", 8), ("mz", 8), ("nq", 8), ("nz", 8), ("ksw", 4), ("kvc", 4))}
    pos = K.keep(C_LEN)
    K.norm_gain[3] = (gain, K.mod[:, 0:KT])
    a = K.arena()
    mv_row, vv_row, g_row = a("mv_row", M_W), a("vv_row", N_G * P), a("g_row", 56)
    negM, wst = a("negM", SEQ), a("wst", SEQ)
    sel = a("sel", M_H, P)
    maskbd = a("maskbd", P)
    gates = a("gates", TT, 56)
    nat = a("nat", 3, TT, M_H)
    decb = a("decb", M_H, M_NC)
    mp = a("m_prev", M_NC + 1)
    mark = a.at[0]
    ndist, cdist = a("ndist", SEQ), a("cdist", TT, N_CMP)
    slope_tab = a("slope_tab", 2, SEQ)
    slope_cmp = a("slope_cmp", 2, TT, N_CMP)
    ksw, kws = a("ksw", 2, SEQ), a("kws", 2, SEQ)
    vv = a("vv", 2, TT, P)
    q = a("q", 2, 2, SEQ)
    kcmp, vcmp = a("kcmp", N_G * N_CMP), a("vcmp", N_G, N_HD)
    w2 = a("w2", 3, N_HD)
    hid = a("hid", 2, N_G * N_CMP)
    hb1 = a("hid_bias", 2)
    obuf = a("obuf", 2, TT, P)
    mx = a("mx", 2, 3)
    sums = a("sums", 4, 3)
    coef = a("coef", 2, 3)
    kv_mark = a.at[0]
    es = a("es", 2, 2, SEQ)
    ec = a("ec", 2, N_CMP)
    pT = a("pT", 2, 2, SEQ)
    cT = a("cT", 2, P)
    a2 = K.arena(kv_mark)
    kvc = a2("kvc", N_G, SEQ)
    Xf = X.rearrange("p t d -> p (t d)")
    x = K.arena(0, Xf)
    xc = x("xc", 4, SEQ)
    so = x("so", 4, SEQ)
    xp = x("xp", 2, SEQ + M_TAPS - 1)
    vx0, vx1 = x("vx0", TT, M_HD + 1), x("vx1", TT, M_HD + 1)
    vx = [vx0, vx1]
    cv = x("cv", 1, SEQ)
    rows = K.arena(0, Xf)
    rf, ra, rb, rM, re, rt = (rows(n, SEQ) for n in ("rf", "ra", "rb", "rM", "re", "rt"))
    s = K.arena(mark)
    mq, mqt, mk = s("mq", 2, SEQ), s("mqt", 2, SEQ), s("mk", 2, SEQ)
    kn = s("kn", TT, M_HD)
    Cst = s("Cst", 2 * (M_NC - 1), M_HD + 1)
    E, Pm = s("E", SEQ), s("Pm", SEQ)
    hbuf = s("hbuf", TT, M_HD)
    st6, mv2, rden = s("st6", TT, 6), s("mv2", TT, 2), s("rden", TT)
    zt = s("zt", 2, SEQ)
    yt = s("yt", SEQ)

    qT, esb, pTb = ([[ap[:, p, i, :] for i in range(2)] for p in range(2)] for ap in (q, es, pT))

    names = (("mx", M_W), ("mv", M_W), ("mo", M_W), ("mz", M_W), ("mi", M_H), ("mf", M_H), ("nq", N_H * N_HD),
             ("kc", 256), ("vc", 256), ("ks", 256), ("vs", 256), ("kw", 256), ("vw", 256), ("ng", 3 * N_H), ("nz", 1024))
    col, c0 = {}, 0
    for n, w in names:
        col[n] = c0
        c0 += w
    W = T["w_in_3"][0]

    def tile(name, i):
        st = ("tile", 3, name, i)
        if name == "gates":
            K.tile(st, [(W, col["mi"], 8), (W, col["ng"], 48)], "N", 56, hT, SEQ, bias=g_row[0:1, :])
        elif name == "ksw":
            K.tile(st, [(W, col["ks"] + i * 64, 64), (W, col["kw"] + i * 64, 64)], "T", P, hT, SEQ)
        elif name == "kvc":
            K.tile(st, [(W, col["kc"] + i * 64, 64), (W, col["vc"] + i * 64, 64)], "T", P, hT, SEQ)
        elif name == "vv":
            K.tile(st, [(W, col["vs"] + i * 64, 64), (W, col["vw"] + i * 64, 64)], "N", P, hT, SEQ,
                   bias=vv_row[0:1, i * P:(i + 1) * P])
        elif name == "mv":
            K.tile(st, [(W, col["mv"] + i * P, P)], "N", P, hT, SEQ, bias=mv_row[0:1, i * P:(i + 1) * P])
        else:
            K.tile(st, [(W, col[name] + i * P, P)], "T", P, hT, SEQ)
        return st

    script = ([] if K.modulated else ada_stages()) + [("norm", 3, tt) for tt in range(TT)]
    script.append(tile("gates", 0))
    K.after_norm(script[-1], 3)
    script += [("mg_rows", 0), tile("kvc", 0), tile("kvc", 1), ("mg_nat", 0), tile("kvc", 2), tile("kvc", 3), ("cmp", 0),
               ("cmp2", 0)]
    G = [[tile("ksw", g), tile("vv", g), tile("nq", 2 * g), tile("nq", 2 * g + 1)] for g in range(N_G)]
    M = [[tile("mx", 2 * h), tile("mx", 2 * h + 1), tile("mo", 2 * h), tile("mo", 2 * h + 1), tile("mv", 2 * h),
          tile("mv", 2 * h + 1)] for h in range(M_H)]
    Z = [tile("nz", i) for i in range(8)] + [tile("mz", i) for i in range(8)]
    units = [(g, j, qb, hh) for g in range(N_G) for j in range(2) for qb in range(TT) for hh in range(2)]
    at = {u: n for n, u in enumerate(units)}

    def attention_steps(n):
        out = []
        if n < len(units):
            out.append(("nsa_s", n))
        if 0 <= n - 1 < len(units):
            out.append(("nsa_t", n - 1))
        if 0 <= n - 2 < len(units):
            out.append(("nsa_v", n - 2))
            if units[n - 2][2:] == (TT - 1, 1):
                out.append(("nsa_o", n - 2))
        return out

    script += G[0]
    tiles = G[1] + M[0][0:2] + G[2] + M[0][2:4] + G[3] + M[0][4:6] + M[1]
    n = 0
    for i, t in enumerate(tiles):
        script.append(t)
        while n < len(units) * (i + 1) // len(tiles):
            script += attention_steps(n)
            n += 1
    script += attention_steps(n) + attention_steps(n + 1)

    head = lambda h: [("ml_qk", h), ("ml_s", h), ("ml_u", h), ("ml_n", h), ("ml_t", h)]
    script += spread_steps(Z[0:5], head(0)) + spread_steps(M[2], head(1)) + spread_steps(M[3], head(2)) + spread_steps(Z[5:12], head(3)) + Z[12:]
    script += [("wo", 3, n) for n in range(4)] + [("final", 3, tt) for tt in range(TT)]

    for st in script:
        kind = st[0]
        if kind == "mg_rows":
            K.uses[st] = [("i", "S", 1), ("f", "S", 2)]
        elif kind == "mg_nat":
            K.uses[st] = [("n", "S", 1), ("d", "S", 1)]
        elif kind == "cmp":
            K.uses[st] = [(0, "S", 1), (1, "S", 1)]
        elif kind == "cmp2":
            K.uses[st] = [("k", "S", 1), ("v", "S", 1)]
        elif kind in ("nsa_s", "nsa_t"):
            K.uses[st] = [(b, "S", 1) for b in range(3)]
        elif kind in ("nsa_v", "nsa_o"):
            K.uses[st] = [(0, "S", 1)]
        elif kind == "ml_qk":
            K.uses[st] = [(("q", e), "S", 1) for e in range(2)] + [(("k", e), "S", 1) for e in range(2)] + \
                         [(("n", e), "S", 1) for e in range(2)]
        elif kind == "ml_s":
            K.uses[st] = [("m", "S", 1), ("w", "S", 1), ("s", "S", 1)]
        elif kind == "ml_u":
            K.uses[st] = [((c, d), "S", 1) for c in range(M_NC - 1) for d in range(2)]
        elif kind == "ml_n":
            K.uses[st] = [(tt, "S", 1) for tt in range(TT)]
        elif kind == "ml_t":
            K.uses[st] = [(j, "S", 1) for j in range(2)]

    s_par = K.sem("b3_params")
    s_tab = K.sem("b3_tables")
    s_keep, s_back = K.sem("x_kept"), K.sem("x_back")
    s_gain = K.sem("gain_ready")
    s_fg = K.sem("final_gain_3_loaded")
    s_gate = K.sem("gate_rows_act")
    s_gatev = K.sem("gate_rows_vec")
    s_bq = K.sem("scaled_bias_ready")
    s_swap = [K.sem(f"keys_swapped{i}") for i in range(2)]
    s_hid = K.sem("hidden_ready")
    s_hbias = K.sem("hidden_bias_ready")
    s_slope = K.sem("slope_tables_ready")
    s_score = K.sem("scores_ready")
    s_exp = K.sem("exps_ready")
    s_comb = K.sem("unit_combined")
    s_conv = K.sem("mconv_ready")
    s_xc = K.sem("xc_ready")
    s_E = K.sem("decay_logits_ready")
    s_Ee = K.sem("decay_weights_ready")
    s_Pm = K.sem("weighted_scores_ready")
    s_qt = K.sem("decayed_q_ready")
    s_C = K.sem("cell_state_ready")
    s_var = K.sem("head_variance_ready")
    s_std = K.sem("head_std_ready")
    s_hn = K.sem("head_normed")
    s_y = K.sem("ungated_tile_ready")
    s_z = K.sem("gate_tile_ready")
    x_keep = nc.dram_tensor("x_keep", (SEQ, D), F32).ap()

    def pool_params(pool):
        n = 0
        t = lambda name: T[name + "_3"]
        vec_of = lambda ap: ap.rearrange("o (k p) -> p (o k)", p=P)
        b_in = t("b_in")
        loads = [(ln_g, vec_of(t("ln_g"))), (cb, vec_of(t("m_conv_b"))), (nw, vec_of(t("m_norm_w"))),
                 (skip, vec_of(t("m_skip"))), (fb[0:M_H, :], t("m_f_bias").rearrange("o h -> h o")),
                 (pos[0:64, :], t("n_pos_k")[0].rearrange("l d -> d l")),
                 (pos[64:128, :], t("n_pos_v")[0].rearrange("l d -> d l"))]
        loads += [(cw[:, 8 * j:8 * j + 8], vec_of(t("m_conv_w")[0, j:j + 1])) for j in range(M_TAPS)]
        loads += [(bias[n], vec_of(b_in[:, col[n]:col[n] + 1024])) for n in ("mx", "mo", "mz", "nq", "nz")]
        for name, lo, hi in (("ksw", "ks", "kw"), ("kvc", "kc", "vc")):
            for r, c in ((0, lo), (64, hi)):
                loads.append((bias[name][r:r + 64, :], b_in[:, col[c]:col[c] + 256].rearrange("o (g d) -> d (o g)", d=64)))
        with nc.allow_non_contiguous_dma(reason="small per-channel parameters"):
            for dst, src in loads:
                pool.dma_start(dst, src).then_inc(s_par, 16)
                n += 16
        K.par_count[3] = n

    def pool_norm(pool, st):
        _, blk, tt = st
        if blk != 3:
            return
        g = K.blocks.index(3)
        if g == 0:
            for s in K.s_x:
                pool.wait_ge(s, 16)
        else:
            pool.wait_ge(K.x_done, g * TT + (tt - TT + 1))
        pool.dma_start(x_keep[tt * P:(tt + 1) * P, :], X[:, tt, :]).then_inc(s_keep, 16)

    def pool_tile(pool, st):
        _, _, name, i = st
        if name == "gates":
            pass
        elif name == "ksw":
            pool.wait_ge(*bk.released(st))
            if i >= 2:
                pool.wait_ge(*bk.filled(("nsa_s", at[(i - 2, 1, TT - 1, 1)]), 2))
            pool.dma_start(kws[0:64, i % 2, :], ksw[64:128, i % 2, :]).then_inc(s_swap[i % 2], 16)
            pool.dma_start(kws[64:128, i % 2, :], ksw[0:64, i % 2, :]).then_inc(s_swap[i % 2], 16)

    b_in = T["b_in_3"]
    tables = [(mv_row[0:1, :], b_in[:, col["mv"]:col["mv"] + M_W]),
              (g_row[0:1, 0:8], b_in[:, col["mi"]:col["mi"] + 8]), (g_row[0:1, 8:56], b_in[:, col["ng"]:col["ng"] + 48]),
              (sel[0:M_H, :, :], T["c_sel"]), (maskbd, T["c_maskbd"]), (ndist, T["c_ndist"]), (cdist, T["c_cdist"]),
              (w2[:, 0, :], T["n_w2_k_3"][0]), (w2[:, 1, :], T["n_w2_k_3"][0]), (w2[:, 2, :], T["n_w2_v_3"][0])]
    vr = vv_row[0:1, :].rearrange("o (g b d) -> o g b d", b=2, d=N_HD)
    for b, c in ((0, "vs"), (1, "vw")):
        tables.append((vr[:, :, b, :], b_in[:, col[c]:col[c] + 256].rearrange("o (g d) -> o g d", d=N_HD)))

    def pool_tables(pool, st):
        pool.wait_ge(*bk.filled(("norm", 3, TT - 1), KT // 4 - 1))
        for dst, src in tables:
            pool.dma_start(dst, src).then_inc(s_tab, 16)
    n_tab = 16 * len(tables)

    def pool_wo(pool, st):
        if st[2] == 0:
            pool.wait_ge(K.y_done, K.y_base[3] + KT)
            pool.wait_ge(s_keep, 16 * TT)
            for tt in range(TT):
                pool.dma_start(X[:, tt, :], x_keep[tt * P:(tt + 1) * P, :]).then_inc(s_back, 16)
            pool.dma_start(K.work[:, 2 * D:3 * D], T["final_g_3"].partition_broadcast(P)).then_inc(s_fg, 16)

    def pe_mg_rows(pe, st):
        pe.wait_ge(*bk.released(("tile", 3, "gates", 0)))
        for key, c in (("i", 0), ("f", M_H)):
            bk.take(pe, st, key)
            for tt in range(TT):
                mm = nc.tensor.transpose(ps(st, key)[0:M_H, tt * P:(tt + 1) * P], gates[:, tt, c:c + M_H], K.ident[:, :])
            mm.then_inc(bk.full_sem(st, key), 1)

    def pe_mg_nat(pe, st):
        pe.wait_ge(s_gate, 5)
        pe.wait_ge(s_gatev, 1)
        bk.take(pe, st, "n")
        for i, r in enumerate((ra, rt, re)):
            for tt in range(TT):
                mm = nc.tensor.transpose(ps(st, "n")[:, (i * TT + tt) * M_H:(i * TT + tt + 1) * M_H],
                                         r[0:M_H, tt * P:(tt + 1) * P], K.ident[0:M_H, 0:M_H])
        mm.then_inc(bk.full_sem(st, "n"), 1)
        bk.take(pe, st, "d")
        for h in range(M_H):
            mm = nc.tensor.matmul(ps(st, "d")[:, h * M_NC:(h + 1) * M_NC], lhsT=sel[0:M_H, h, :],
                                  rhs=wst[0:M_H, M_CH - 1::M_CH], start=True, stop=True)
        mm.then_inc(bk.full_sem(st, "d"), 1)

    def pe_cmp(pe, st):
        for i in range(N_G):
            pe.wait_ge(*bk.released(("tile", 3, "kvc", i)))
        pe.wait_ge(s_par, K.par_count[3])
        n = N_G * N_CMP
        for b in range(2):
            bk.take(pe, st, b)
        w1 = [K.slot_ap(st, b) for b in range(2)]
        for b in range(2):
            pe.wait_ge(*K.slot_loaded(st, b))
        for b in range(2):
            r = slice(64 * b, 64 * b + 64)
            for l in range(C_LEN):
                rhs = kvc[r, :, l:l + C_STEP * (N_CMP - 1) + 1:C_STEP]
                nc.tensor.matmul(ps(st, b)[:, 0:n].rearrange("p (g j) -> p g j", j=N_CMP), lhsT=w1[l // 16][r, l % 16, :], rhs=rhs, start=(l == 0),
                                 stop=(l == C_LEN - 1))
            for l in range(C_LEN):
                mm = nc.tensor.matmul(ps(st, b)[:, n:n + 1], lhsT=w1[l // 16][r, l % 16, :], rhs=pos[r, l:l + 1],
                                      start=(l == 0), stop=(l == C_LEN - 1))
            mm.then_inc(bk.full_sem(st, b), 1)

    def pe_cmp2(pe, st):
        pe.wait_ge(s_hid, 2)
        bk.take(pe, st, "k")
        nc.tensor.matmul(ps(st, "k")[:, 0:N_G * N_CMP], lhsT=w2[:, 0:2, :], rhs=hid[:, 0, :],
                         start=True, stop=True).then_inc(bk.full_sem(st, "k"), 1)
        bk.take(pe, st, "v")
        for g in range(N_G):
            mm = nc.tensor.matmul(ps(st, "v")[0:N_CMP, g * N_HD:(g + 1) * N_HD], lhsT=hid[:, 1, g * N_CMP:(g + 1) * N_CMP],
                                  rhs=w2[:, 2, :], start=True, stop=True)
        mm.then_inc(bk.full_sem(st, "v"), 1)

    def pe_nsa_s(pe, st):
        g, j, qb, hh = units[st[1]]
        r = slice(64 * hh, 64 * hh + 64)
        nk = (qb + 1) * P
        if (j, qb, hh) == (0, 0, 0):
            pe.wait_ge(s_swap[g % 2], 32 * (g // 2 + 1))
            pe.wait_ge(*bk.released(("tile", 3, "ksw", g)))
            pe.wait_ge(*bk.released(("tile", 3, "nq", 2 * g)))
            pe.wait_ge(*bk.released(("tile", 3, "nq", 2 * g + 1)))
            if g == 0:
                pe.wait_ge(*bk.released(("cmp2", 0), "k"))
        lhsT = qT[g % 2][j][r, qb * P:(qb + 1) * P]
        keys = (kcmp[r, g * N_CMP:(g + 1) * N_CMP], (ksw, kws)[hh][r, g % 2, 0:nk], (kws, ksw)[hh][r, g % 2, 0:nk])
        for b, rhs in enumerate(keys):
            bk.take(pe, st, b)
            nc.tensor.matmul(ps(st, b)[:, 0:rhs.shape[1]], lhsT=lhsT, rhs=rhs, start=True,
                             stop=True).then_inc(bk.full_sem(st, b), 1)

    def pe_nsa_t(pe, st):
        u = st[1]
        g, j, qb, hh = units[u]
        for b in range(3):
            pe.wait_ge(s_exp, 3 * u + b + 1)
            bk.take(pe, st, b)
            if b == 0:
                mm = nc.tensor.transpose(ps(st, b)[0:N_CMP, 0:P], ec[:, u % 2, :], K.ident[:, :])
            else:
                for kt in range(qb + 1):
                    mm = nc.tensor.transpose(ps(st, b)[:, kt * P:(kt + 1) * P], esb[u % 2][b - 1][:, kt * P:(kt + 1) * P],
                                             K.ident[:, :])
            mm.then_inc(bk.full_sem(st, b), 1)

    def pe_nsa_v(pe, st):
        u = st[1]
        g, j, qb, hh = units[u]
        if u == 0:
            pe.wait_ge(*bk.released(("cmp2", 0), "v"))
        if (j, qb, hh) == (0, 0, 0):
            pe.wait_ge(*bk.released(("tile", 3, "vv", g)))
        for b in range(3):
            pe.wait_ge(*bk.released(("nsa_t", u), b))
        bk.take(pe, st)
        o = ps(st)
        nc.tensor.matmul(o[:, 0:N_HD], lhsT=cT[0:N_CMP, u % 2, :], rhs=vcmp[0:N_CMP, g, :], start=True, stop=True)
        for b in (1, 2):
            for kt in range(qb + 1):
                mm = nc.tensor.matmul(o[:, b * N_HD:(b + 1) * N_HD], lhsT=pTb[u % 2][b - 1][:, kt * P:(kt + 1) * P],
                                      rhs=vv[:, g % 2, kt, (b - 1) * N_HD:b * N_HD], start=(kt == 0), stop=(kt == qb))
        mm.then_inc(bk.full_sem(st), 1)

    def pe_nsa_o(pe, st):
        u = st[1]
        pe.wait_ge(s_comb, u + 1)
        bk.take(pe, st)
        par = (u // 8) % 2
        for tt in range(TT):
            mm = nc.tensor.transpose(ps(st)[:, tt * P:(tt + 1) * P], obuf[:, par, tt, :], K.ident[:, :])
        mm.then_inc(bk.full_sem(st), 1)

    def pe_ml_qk(pe, st):
        h = st[1]
        pe.wait_ge(s_xc, 2 * h + 2)
        pe.wait_ge(*K.slot_loaded(st))
        if h == 0:
            pe.wait_ge(s_comb, len(units))
        w = K.slot_ap(st).rearrange("p k c -> p (k c)")[:, 0:4 * M_HD].rearrange("p (m k e) -> p m k e", m=2, k=2)
        for m, key in ((0, "q"), (1, "k")):
            for e in range(2):
                bk.take(pe, st, (key, e))
                for d in range(2):
                    mm = nc.tensor.matmul(ps(st, (key, e)), lhsT=w[:, m, d, e * P:(e + 1) * P], rhs=xc[:, 2 * (h % 2) + d, :],
                                          start=(d == 0), stop=(d == 1))
                mm.then_inc(bk.full_sem(st, (key, e)), 1)
        for half in range(2):
            bk.take(pe, st, ("n", half))
            for i in range(2):
                tt = 2 * half + i
                for d in range(2):
                    mm = nc.tensor.matmul(ps(st, ("n", half))[:, i * M_HD:(i + 1) * M_HD],
                                          lhsT=xc[:, 2 * (h % 2) + d, tt * P:(tt + 1) * P], rhs=w[:, 1, d, :],
                                          start=(d == 0), stop=(d == 1))
            mm.then_inc(bk.full_sem(st, ("n", half)), 1)

    def pe_ml_s(pe, st):
        h = st[1]
        for key, r in (("m", negM), ("w", wst)):
            bk.take(pe, st, key)
            nc.tensor.matmul(ps(st, key), lhsT=sel[0:M_H, h, :], rhs=r[0:M_H, :], start=True,
                             stop=True).then_inc(bk.full_sem(st, key), 1)
        for key in ("q", "k"):
            for e in range(2):
                pe.wait_ge(*bk.released(("ml_qk", h), (key, e)))
        bk.take(pe, st, "s")
        for tt in range(TT):
            t = slice(tt * P, (tt + 1) * P)
            for d in range(2):
                mm = nc.tensor.matmul(ps(st, "s")[:, t], lhsT=mk[:, d, t], rhs=mq[:, d, t], start=(d == 0), stop=(d == 1))
        mm.then_inc(bk.full_sem(st, "s"), 1)

    def pe_ml_u(pe, st):
        h = st[1]
        for half in range(2):
            pe.wait_ge(*bk.released(("ml_qk", h), ("n", half)))
        pe.wait_ge(*bk.released(("tile", 3, "mv", 2 * h)))
        pe.wait_ge(*bk.released(("tile", 3, "mv", 2 * h + 1)))
        for c in range(M_NC - 1):
            r = slice((c % 2) * M_CH, (c % 2 + 1) * M_CH)
            for d in range(2):
                bk.take(pe, st, (c, d))
                nc.tensor.matmul(ps(st, (c, d))[:, 0:M_HD + 1], lhsT=kn[r, c // 2, d * P:(d + 1) * P],
                                 rhs=vx[h % 2][r, c // 2, :], start=True, stop=True).then_inc(bk.full_sem(st, (c, d)), 1)

    def pe_ml_n(pe, st):
        h = st[1]
        pe.wait_ge(s_Pm, h + 1)
        pe.wait_ge(s_qt, h + 1)
        for tt in range(TT):
            bk.take(pe, st, tt)
            o = ps(st, tt)[:, 0:M_HD + 1]
            mm = nc.tensor.matmul(o, lhsT=Pm[:, tt * P:(tt + 1) * P], rhs=vx[h % 2][:, tt, :], start=True, stop=False,
                                  skip_group_check=True)
            for c in (2 * tt, 2 * tt + 1):
                if c == 0:
                    continue
                pe.wait_ge(s_C, 14 * h + 2 * c)
                r = slice((c % 2) * M_CH, (c % 2 + 1) * M_CH)
                for d in range(2):
                    mm = nc.tensor.matmul(o[r, :], lhsT=mqt[:, d, c * M_CH:(c + 1) * M_CH], rhs=Cst[:, 2 * (c - 1) + d, :],
                                          start=False, stop=(d == 1), skip_group_check=True)
            mm.then_inc(bk.full_sem(st, tt), 1)

    def pe_ml_t(pe, st):
        h = st[1]
        pe.wait_ge(s_hn, TT * (h + 1))
        for j in range(2):
            bk.take(pe, st, j)
            for tt in range(TT):
                mm = nc.tensor.transpose(ps(st, j)[:, tt * P:(tt + 1) * P], hbuf[:, tt, j * P:(j + 1) * P], K.ident[:, :])
            mm.then_inc(bk.full_sem(st, j), 1)

    def act_tile(act, L, st):
        _, _, name, i = st
        b = ps(st)
        if name == "mx":
            act.wait_ge(s_conv, i + 1)
            nc.scalar.activation(xc[:, i % 4, :], cv[:, 0, :], ACT.Silu).then_inc(s_xc, 1)
            return
        if name == "vv" and i >= 2:
            act.wait_ge(*bk.filled(("nsa_v", at[(i - 2, 1, TT - 1, 1)])))
        if name == "nq" and i >= 4:
            act.wait_ge(*bk.filled(("nsa_s", at[(i // 2 - 2, 1, TT - 1, 1)]), 2))
        if name == "ksw" and i >= 2:
            act.wait_ge(*bk.filled(("nsa_s", at[(i - 2, 1, TT - 1, 1)]), 2))
            act.wait_ge(s_swap[i % 2], 32 * (i // 2))
        if name == "mo" and i >= 4:
            act.wait_ge(s_y, 8 + 2 * (i // 2 - 2) + 2)
        if name == "mv" and i >= 4:
            act.wait_ge(*bk.filled(("ml_n", i // 2 - 2), TT - 1))
        if name in ("gates", "kvc") and i == 0:
            act.wait_ge(s_par, K.par_count[3])
            act.wait_ge(s_bq, 1)
        act.wait_ge(*bk.filled(st))
        if name == "gates":
            b3 = b.rearrange("p (t c) -> p t c", c=P)
            L(nc.scalar.activation(gates[:, :, 0:8], b3[:, :, 0:8], ACT.Copy))
            ins = nc.scalar.activation(gates[:, :, 8:56], b3[:, :, 8:56], ACT.Sigmoid)
        elif name == "kvc":
            ins = nc.scalar.activation(kvc[:, i, :], b, ACT.Identity, bias=bias["kvc"][:, i:i + 1])
        elif name == "ksw":
            ins = nc.scalar.activation(ksw[:, i % 2, :], b, ACT.Identity, bias=bias["ksw"][:, i:i + 1])
        elif name == "vv":
            ins = nc.scalar.activation(vv[:, i % 2, :, :], b.rearrange("p (t c) -> p t c", c=P), ACT.Copy)
        elif name == "nq":
            ins = nc.scalar.activation(qT[(i // 2) % 2][i % 2], b, ACT.Identity, bias=bias["nq"][:, i:i + 1],
                                       scale=N_HD ** -0.5)
        elif name == "mo":
            ins = nc.scalar.activation(so[:, i % 4, :], b, ACT.Sigmoid, bias=bias["mo"][:, i:i + 1])
        elif name == "mv":
            h, j = i // 2, i % 2
            ins = nc.scalar.activation(vx[h % 2][:, :, j * P:(j + 1) * P], b.rearrange("p (t c) -> p t c", c=P), ACT.Copy)
        else:
            n = i if name == "nz" else 8 + i
            if n == 0:
                act.wait_ge(s_comb, len(units))
            if n >= 2:
                act.wait_ge(K.y_done, K.y_base[3] + n - 1)
            ins = nc.scalar.activation(zt[:, n % 2, :], b, ACT.Silu, bias=bias[name][:, i:i + 1])
        ins.then_inc(bk.free_sem(st), 1)

    def act_mg_rows(act, L, st):
        act.wait_ge(*bk.filled(st, "f"))
        act.wait_ge(s_keep, 16 * TT)
        act.wait_ge(s_hn_done, hn_done)
        r = slice(0, M_H)
        nc.scalar.activation(rf[r, :], ps(st, "f")[r, :], ACT.Abs, bias=fb[r, 0:1]).then_inc(bk.free_sem(st, "f"), 1)
        act.wait_ge(*bk.read_once(st, "f"))
        L(nc.scalar.activation(rf[r, :], rf[r, :], ACT.Exp, scale=-1.0))
        L.settle()
        nc.scalar.activation(rf[r, :], rf[r, :], ACT.Ln, bias=1.0).then_inc(s_gate, 1)
        act.wait_ge(s_gatev, 1)
        nc.scalar.activation(wst[r, :], wst[r, :], ACT.Exp).then_inc(s_gate, 1)
        nc.scalar.activation(re[r, :], re[r, :], ACT.Exp, scale=-1.0).then_inc(s_gate, 1)
        nc.scalar.activation(rt[r, :], rt[r, :], ACT.Exp).then_inc(s_gate, 1)
        nc.scalar.activation(negM[r, :], rM[r, :], ACT.Copy, scale=-1.0).then_inc(s_gate, 1)

    def act_cmp(act, L, st):
        n = N_G * N_CMP
        act.wait_ge(s_hbias, 1)
        for b in range(2):
            act.wait_ge(*bk.filled(st, b))
            nc.scalar.activation(hid[:, b, :], ps(st, b)[:, 0:n], ACT.Gelu_apprx_tanh,
                                 bias=hb1[:, b:b + 1]).then_inc(s_hid, 1)
            act.wait_ge(s_hid, b + 1)
            act.sem_inc(bk.free_sem(st, b), 1)

    def act_cmp2(act, L, st):
        act.wait_ge(*bk.filled(st, "k"))
        nc.scalar.activation(kcmp[:, :], ps(st, "k")[:, 0:N_G * N_CMP], ACT.Copy).then_inc(bk.free_sem(st, "k"), 1)
        act.wait_ge(*bk.filled(st, "v"))
        nc.scalar.activation(vcmp[0:N_CMP, :, :], ps(st, "v")[0:N_CMP, 0:N_G * N_HD].rearrange("p (g d) -> p g d", d=N_HD),
                             ACT.Copy).then_inc(bk.free_sem(st, "v"), 1)

    def act_nsa_s(act, L, st):
        u = st[1]
        g, j, qb, hh = units[u]
        nk = (qb + 1) * P
        n = g * N_HPG + 2 * j + hh
        if qb == 0:
            act.wait_ge(s_tab, n_tab)
            if n >= 2:
                act.wait_ge(s_score, 3 * (u - 1))
            slope = 2.0 ** (-8.0 * (n + 1) / N_H)
            nc.scalar.activation(slope_tab[:, hh, :], ndist, ACT.Copy, scale=slope).then_inc(s_slope, 1)
            nc.scalar.activation(slope_cmp[:, hh, :, :], cdist, ACT.Copy, scale=slope).then_inc(s_slope, 1)
        for b in range(3):
            act.wait_ge(s_score, 3 * u + b + 1)
            e = ec[:, u % 2, :] if b == 0 else esb[u % 2][b - 1][:, 0:nk]
            nc.scalar.activation(e, e, ACT.Exp, bias=mx[:, u % 2, b:b + 1],
                                 accum_out=sums[:, u % 4, b:b + 1]).then_inc(s_exp, 1)

    def act_nsa_t(act, L, st):
        u = st[1]
        qb = units[u][2]
        nk = (qb + 1) * P
        if u >= 2:
            act.wait_ge(*bk.filled(("nsa_v", u - 2)))
        act.wait_ge(*bk.filled(st, 1))
        nc.scalar.activation(pTb[u % 2][0][:, 0:nk], ps(st, 1)[:, 0:nk], ACT.Copy).then_inc(bk.free_sem(st, 1), 1)

    def act_ml_qk(act, L, st):
        h = st[1]
        for key, dst, sc in (("q", mq, 1.0), ("k", mk, M_HD ** -0.5)):
            for e in range(2):
                act.wait_ge(*bk.filled(st, (key, e)))
                if h >= 1 and e == 0:
                    act.wait_ge(*bk.filled(("ml_s", h - 1), "s"))
                    act.wait_ge(s_qt, h)
                nc.scalar.activation(dst[:, e, :], ps(st, (key, e)), ACT.Copy, scale=sc).then_inc(bk.free_sem(st, (key, e)), 1)

    def act_ml_s(act, L, st):
        h = st[1]
        act.wait_ge(s_E, h + 1)
        for tt in range(TT):
            t = slice(tt * P, (tt + 1) * P)
            nc.scalar.activation(E[:, t], E[:, t], ACT.Exp, bias=natc(0, tt, h)).then_inc(s_Ee, 1)

    def natc(i, tt, h):
        c = (i * TT + tt) * M_H + h
        return nat2[:, c:c + 1]
    nat2 = nat.rearrange("p a b c -> p (a b c)")

    def act_ml_n(act, L, st):
        h = st[1]
        for tt in range(TT):
            act.wait_ge(s_var, TT * h + tt + 1)
            nc.scalar.activation(mv2[:, tt, 1:2], mv2[:, tt, 1:2], ACT.Sqrt, bias=K.eps[:, 0:1]).then_inc(s_std, 1)

    def wait_gain(vec):
        vec.wait_ge(s_par, K.par_count[3])
        L = K.vlane[0]
        L(nc.vector.scalar_tensor_tensor(gain, K.mod[:, KT:2 * KT], 1.0, ln_g, ALU.add, ALU.mult))
        L.settle()
        nc.vector.tensor_scalar(bias["nq"], bias["nq"], N_HD ** -0.5, None, ALU.mult).then_inc(s_bq, 1)

    def vec_tile(vec, L, st):
        _, _, name, i = st
        b = ps(st)
        if name == "mx":
            vec.wait_ge(*bk.filled(st))
            if i == 0:
                vec.wait_ge(s_gate, 5)
                vec.wait_ge(*bk.filled(("mg_nat", 0), "d"))
                L(nc.vector.memset(xp[:, :, 0:M_TAPS - 1], 0.0))
                for v in vx:
                    L(nc.vector.memset(v[:, :, M_HD:M_HD + 1], 1.0))
            u = xp[:, i % 2, :]
            if i >= 4:
                vec.wait_ge(s_y, 8 + 2 * (i // 2 - 2) + 2)
            nc.vector.tensor_scalar(u[:, M_TAPS - 1:], b, bias["mx"][:, i:i + 1], None, ALU.add).then_inc(bk.free_sem(st), 1)
            vec.wait_ge(*bk.released(st))
            L.settle()
            if i >= 1:
                vec.wait_ge(s_xc, i)
            for k in range(M_TAPS):
                w = cw[:, 8 * k + i:8 * k + i + 1]
                if k == 0:
                    ins = nc.vector.tensor_scalar(cv[:, 0, :], u[:, 0:SEQ], w, cb[:, i:i + 1], ALU.mult, ALU.add)
                else:
                    ins = nc.vector.scalar_tensor_tensor(cv[:, 0, :], u[:, k:k + SEQ], w, cv[:, 0, :], ALU.mult, ALU.add)
                if k < M_TAPS - 1:
                    L(ins)
                    L.settle()
            ins.then_inc(s_conv, 1)
            vec.wait_ge(s_conv, i + 1)
        elif name in ("nz", "mz"):
            n = i if name == "nz" else 8 + i
            vec.wait_ge(*bk.released(st))
            slot = 8 + i if name == "nz" else i
            vec.wait_ge(s_y, n + 1)
            nc.vector.tensor_tensor(yT[:, slot, :], yT[:, slot, :], zt[:, n % 2, :], ALU.mult).then_inc(K.y_done, 1)

    def vec_mg_rows(vec, L, st):
        r = slice(0, M_H)
        vec.wait_ge(*bk.read_once(st, "f"))
        vec.wait_ge(s_keep, 16 * TT)
        vec.wait_ge(s_hn_done, hn_done)
        L(nc.vector.tensor_scalar(rb[r, :], ps(st, "f")[r, :], fb[r, 0:1], 0.0, ALU.add, ALU.min))
        L(nc.vector.memset(mp[r, 0:1], 0.0))
        L.settle()
        vec.sem_inc(bk.free_sem(st, "f"), 1)
        vec.wait_ge(s_gate, 1)
        L(nc.vector.tensor_tensor(ra[r, :], rb[r, :], rf[r, :], ALU.subtract))
        L.settle()
        L(nc.vector.tensor_tensor_scan(rb[r, :], K.reset[r, :], ra[r, :], 0.0, ALU.mult, ALU.add))
        L.settle()
        vec.wait_ge(*bk.filled(st, "i"))
        nc.vector.tensor_tensor(ra[r, :], ps(st, "i")[r, :], rb[r, :], ALU.subtract).then_inc(bk.free_sem(st, "i"), 1)
        vec.wait_ge(*bk.released(st, "i"))
        for c in range(M_NC):
            t, e = slice(c * M_CH, (c + 1) * M_CH), slice((c + 1) * M_CH - 1, (c + 1) * M_CH)
            L(nc.vector.tensor_tensor_scan(rM[r, t], ra[r, t], ra[r, t], mp[r, c:c + 1], ALU.max, ALU.max))
            L.settle()
            L(nc.vector.tensor_tensor(mp[r, c + 1:c + 2], rb[r, e], rM[r, e], ALU.add))
            L.settle()
        c3 = lambda ap: ap[r, :].rearrange("p (c l) -> p c l", l=M_CH)
        whole = [M_H, M_NC, M_CH]
        L(nc.vector.tensor_tensor(c3(wst), mp[r, 0:M_NC].unsqueeze(2).to_broadcast(whole), c3(rM), ALU.subtract))
        L(nc.vector.tensor_tensor(re[r, :], rb[r, :], rM[r, :], ALU.add))
        L(nc.vector.tensor_tensor(c3(rt), c3(ra), c3(rM)[:, :, M_CH - 1:M_CH].to_broadcast(whole), ALU.subtract))
        L.settle()
        vec.sem_inc(s_gatev, 1)

    def vec_mg_nat(vec, L, st):
        vec.wait_ge(*bk.filled(st, "n"))
        nc.vector.tensor_copy(nat2, ps(st, "n")[:, 0:3 * TT * M_H]).then_inc(bk.free_sem(st, "n"), 1)
        vec.wait_ge(*bk.filled(st, "d"))
        nc.vector.tensor_copy(decb.rearrange("p h c -> p (h c)"), ps(st, "d")[:, 0:M_H * M_NC]).then_inc(bk.free_sem(st, "d"), 1)

    def vec_cmp(vec, L, st):
        n = N_G * N_CMP
        for b in range(2):
            vec.wait_ge(*bk.filled(st, b))
            L(nc.vector.tensor_copy(hb1[:, b:b + 1], ps(st, b)[:, n:n + 1]))
        L.settle()
        vec.sem_inc(s_hbias, 1)

    def vec_nsa_s(vec, L, st):
        u = st[1]
        g, j, qb, hh = units[u]
        nk = (qb + 1) * P
        n = g * N_HPG + 2 * j + hh
        if u >= 2:
            for b in range(3):
                vec.wait_ge(*bk.filled(("nsa_t", u - 2), b))
        vec.wait_ge(s_slope, 2 * (n + 1))
        for b in range(3):
            vec.wait_ge(*bk.filled(st, b))
            width = N_CMP if b == 0 else nk
            e = ec[:, u % 2, :] if b == 0 else esb[u % 2][b - 1][:, 0:nk]
            table = slope_cmp[:, hh, qb, :] if b == 0 else slope_tab[:, hh, SEQ - nk:SEQ]
            m = mx[:, u % 2, b:b + 1]
            nc.vector.tensor_tensor_reduce(e, ps(st, b)[:, 0:width], table, 1.0, -3e38, ALU.add, ALU.max,
                                           m).then_inc(bk.free_sem(st, b), 1)
            vec.wait_ge(*bk.released(st, b))
            if b == 0:
                nc.vector.tensor_scalar(m, m, -1.0, 1e20, ALU.mult, ALU.min).then_inc(s_score, 1)
            else:
                nc.vector.tensor_scalar(m, m, -1.0, None, ALU.mult).then_inc(s_score, 1)

    def vec_nsa_t(vec, L, st):
        u = st[1]
        nk = (units[u][2] + 1) * P
        if u >= 2:
            vec.wait_ge(*bk.filled(("nsa_v", u - 2)))
        vec.wait_ge(*bk.filled(st, 0))
        nc.vector.tensor_copy(cT[0:N_CMP, u % 2, :], ps(st, 0)[0:N_CMP, 0:P]).then_inc(bk.free_sem(st, 0), 1)
        vec.wait_ge(*bk.filled(st, 2))
        nc.vector.tensor_copy(pTb[u % 2][1][:, 0:nk], ps(st, 2)[:, 0:nk]).then_inc(bk.free_sem(st, 2), 1)

    def vec_nsa_v(vec, L, st):
        u = st[1]
        g, j, qb, hh = units[u]
        n = g * N_HPG + 2 * j + hh
        par = (u // 8) % 2
        if u >= 16 and u % 8 == 0:
            vec.wait_ge(*bk.filled(("nsa_o", u - 9)))
        vec.wait_ge(s_exp, 3 * u + 3)
        c = coef[:, u % 2, :]
        L(nc.vector.tensor_scalar(c, sums[:, u % 4, :], 1e-30, None, ALU.max))
        L.settle()
        L(nc.vector.reciprocal(c, c))
        L.settle()
        L(nc.vector.tensor_tensor(c, c, gates[:, qb, 8 + 3 * n:8 + 3 * n + 3], ALU.mult))
        L.settle()
        vec.wait_ge(*bk.filled(st))
        o = obuf[:, par, qb, hh * N_HD:(hh + 1) * N_HD]
        p = ps(st)
        L(nc.vector.tensor_scalar(o, p[:, 0:N_HD], c[:, 0:1], None, ALU.mult))
        L.settle()
        L(nc.vector.scalar_tensor_tensor(o, p[:, N_HD:2 * N_HD], c[:, 1:2], o, ALU.mult, ALU.add))
        L.settle()
        nc.vector.scalar_tensor_tensor(o, p[:, 2 * N_HD:3 * N_HD], c[:, 2:3], o, ALU.mult, ALU.add).then_inc(bk.free_sem(st), 1)
        vec.wait_ge(*bk.released(st))
        vec.sem_inc(s_comb, 1)

    def vec_nsa_o(vec, L, st):
        u = st[1]
        vec.wait_ge(*bk.filled(st))
        nc.vector.tensor_copy(yT[:, 8 + u // 8, :], ps(st)).then_inc(bk.free_sem(st), 1)
        vec.wait_ge(*bk.released(st))
        vec.sem_inc(s_y, 1)

    def vec_ml_qk(vec, L, st):
        h = st[1]
        if h >= 1:
            vec.wait_ge(*bk.filled(("ml_u", h - 1), (M_NC - 2, 1)))
        for half in range(2):
            vec.wait_ge(*bk.filled(st, ("n", half)))
            for i in range(2):
                tt = 2 * half + i
                ins = nc.vector.tensor_scalar(kn[:, tt, :], ps(st, ("n", half))[:, i * M_HD:(i + 1) * M_HD], natc(1, tt, h),
                                              M_HD ** -0.5, ALU.mult, ALU.mult)
                if i == 0:
                    L(ins)
            ins.then_inc(bk.free_sem(st, ("n", half)), 1)

    def vec_ml_s(vec, L, st):
        h = st[1]
        vec.wait_ge(*bk.filled(st, "m"))
        if h == 0:
            vec.wait_ge(s_tab, n_tab)
        L(nc.vector.tensor_tensor(E[:, :].rearrange("p (t l) -> p t l", l=P), ps(st, "m").rearrange("p (t l) -> p t l", l=P),
                                  maskbd[:, :].unsqueeze(1).to_broadcast([P, TT, P]), ALU.add))
        L.settle()
        vec.sem_inc(bk.free_sem(st, "m"), 1)
        vec.sem_inc(s_E, 1)
        vec.wait_ge(*bk.filled(st, "w"))
        for e in range(2):
            vec.wait_ge(*bk.released(("ml_qk", h), ("q", e)))
        if h >= 1:
            vec.wait_ge(*bk.filled(("ml_n", h - 1), TT - 1))
        for e in range(2):
            L(nc.vector.tensor_tensor(mqt[:, e, :], mq[:, e, :], ps(st, "w"), ALU.mult))
        L.settle()
        vec.sem_inc(bk.free_sem(st, "w"), 1)
        vec.sem_inc(s_qt, 1)
        vec.wait_ge(s_Ee, TT * (h + 1))
        vec.wait_ge(*bk.filled(st, "s"))
        nc.vector.tensor_tensor(Pm[:, :], ps(st, "s"), E[:, :], ALU.mult).then_inc(bk.free_sem(st, "s"), 1)
        vec.wait_ge(*bk.released(st, "s"))
        vec.sem_inc(s_Pm, 1)

    def vec_ml_u(vec, L, st):
        h = st[1]
        if h >= 1:
            vec.wait_ge(*bk.filled(("ml_n", h - 1), TT - 1))
        for c in range(M_NC - 1):
            for d in range(2):
                vec.wait_ge(*bk.filled(st, (c, d)))
                u = ps(st, (c, d))[:, 0:M_HD + 1]
                if c == 0:
                    ins = nc.vector.tensor_copy(Cst[:, d, :], u)
                else:
                    vec.wait_ge(s_C, 14 * h + 2 * (c - 1) + d + 1)
                    ins = nc.vector.scalar_tensor_tensor(Cst[:, 2 * c + d, :], Cst[:, 2 * (c - 1) + d, :], decb[:, h, c:c + 1], u,
                                                         ALU.mult, ALU.add)
                ins.then_inc(s_C, 1)
                vec.wait_ge(s_C, 14 * h + 2 * c + d + 1)
                vec.sem_inc(bk.free_sem(st, (c, d)), 1)

    def vec_ml_n(vec, L, st):
        h = st[1]
        if h >= 1:
            vec.wait_ge(*bk.filled(("ml_t", h - 1), 1))
        for tt in range(TT):
            vec.wait_ge(*bk.filled(st, tt))
            o = ps(st, tt)
            r1 = rden[:, tt:tt + 1]
            L(nc.vector.tensor_scalar(r1, o[:, M_HD:M_HD + 1], -1.0, natc(2, tt, h), ALU.mult, ALU.max))
            L.settle()
            L(nc.vector.tensor_tensor(r1, o[:, M_HD:M_HD + 1], r1, ALU.max))
            L.settle()
            L(nc.vector.reciprocal(r1, r1))
            L.settle()
            nc.vector.tensor_scalar(hbuf[:, tt, :], o[:, 0:M_HD], r1, None, ALU.mult).then_inc(bk.free_sem(st, tt), 1)
            vec.wait_ge(*bk.released(st, tt))
            L(nc.vector.bn_stats(st6[:, tt, :], hbuf[:, tt, :]))
            L.settle()
            nc.vector.bn_aggr(mv2[:, tt, :], st6[:, tt, :]).then_inc(s_var, 1)
            vec.wait_ge(s_var, TT * h + tt + 1)
        for tt in range(TT):
            vec.wait_ge(s_std, TT * h + tt + 1)
            L(nc.vector.reciprocal(mv2[:, tt, 1:2], mv2[:, tt, 1:2]))
            L.settle()
            nc.vector.tensor_scalar(hbuf[:, tt, :], hbuf[:, tt, :], mv2[:, tt, 0:1], mv2[:, tt, 1:2], ALU.subtract,
                                    ALU.mult).then_inc(s_hn, 1)
        vec.wait_ge(s_hn, TT * (h + 1))

    def vec_ml_t(vec, L, st):
        h = st[1]
        for j in range(2):
            i = 2 * h + j
            vec.wait_ge(*bk.filled(st, j))
            vec.wait_ge(*bk.released(("tile", 3, "mo", i)))
            y = yt[:, :]
            nc.vector.scalar_tensor_tensor(y, ps(st, j), nw[:, i:i + 1], so[:, i % 4, :], ALU.mult, ALU.mult).then_inc(bk.free_sem(st, j), 1)
            vec.wait_ge(*bk.released(st, j))
            nc.vector.scalar_tensor_tensor(yT[:, i, :], xc[:, i % 4, :], skip[:, i:i + 1], y, ALU.mult, ALU.add).then_inc(s_y, 1)
            vec.wait_ge(s_y, 8 + i + 1)

    def pe_wo_gate(pe, st):
        n = st[2]
        bk.take(pe, st, "g")
        for j in range(4):
            c = 2 * KT + 4 * n + j
            mm = nc.tensor.matmul(ps(st, "g")[:, j * P:(j + 1) * P], lhsT=K.mod[:, c:c + 1].to_broadcast([P, P]),
                                  rhs=K.ident[:, :], start=True, stop=True)
        mm.then_inc(bk.full_sem(st, "g"), 1)

    gate_sb = K.work[:, 3 * D:4 * D]
    s_gsb = K.sem("gate_row_ready")

    def act_wo_gate(act, L, st):
        n = st[2]
        act.wait_ge(*bk.filled(st, "g"))
        if n == 0:
            act.wait_ge(K.y_done, K.y_base[3] + KT)
        nc.scalar.activation(gate_sb[:, n * NC:(n + 1) * NC], ps(st, "g"), ACT.Copy).then_inc(bk.free_sem(st, "g"), 1)

    def vec_wo(vec, L, st):
        n = st[2]
        if n == 0:
            vec.wait_ge(s_back, 16 * TT)
        vec.wait_ge(*bk.released(("wo_gate", 3, n), "g"))
        for tt in range(TT):
            vec.wait_ge(*bk.filled(st, tt))
            xs = X[:, tt, n * NC:(n + 1) * NC]
            t = K.work[:, tt * NC:(tt + 1) * NC]
            L(nc.vector.tensor_tensor(t, ps(st, tt), gate_sb[:, n * NC:(n + 1) * NC], ALU.mult))
            L.settle()
            nc.vector.tensor_tensor(xs, xs, t, ALU.add).then_inc(bk.free_sem(st, tt), 1)

    def vec_final(vec, L, st):
        tt = st[2]
        K.vec_rstd(vec, L, st)
        vec.wait_ge(s_fg, 16)
        nc.vector.scalar_tensor_tensor(X[:, tt, :], X[:, tt, :], K.rstd[:, tt:tt + 1], K.work[:, 2 * D:3 * D], ALU.mult,
                                       ALU.mult).then_inc(K.x_done, 1)

    s_hn_done, hn_done = K.s_hn, TT * (K.blocks.index(3) + 1) + (MEM // P if 1 in K.blocks else 0)
    gi = [n for n, st in enumerate(script) if st[0] == "wo"][0]
    for n in range(4):
        script.insert(gi, ("wo_gate", 3, 3 - n))
    for n in range(4):
        K.uses[("wo_gate", 3, n)] = [("g", "S", 1)]
    script.insert(script.index(("norm", 3, TT - 1)) + 1, ("b3_tables", 0))
    w1 = [T[f"n_w1_{c}_3"][0].rearrange("(l d) h -> d l h", d=N_HD) for c in "kv"]
    K.slot_src["cmp"] = lambda st, sub, ap: [(ap[64 * b:64 * b + 64, :, :], w1[b][:, 16 * sub:16 * sub + 16, :]) for b in range(2)]
    K.slot_src["ml_qk"] = lambda st, sub, ap: [
        (ap.rearrange("p k c -> p (k c)")[:, 512 * m:512 * m + 512].rearrange("p (k e) -> p k e", e=M_HD),
         T[n][0, st[1]].rearrange("(k p) e -> p k e", p=P)) for m, n in enumerate(("m_wq_3", "m_wk_3"))]
    K.slot_count["cmp"], K.slot_count["ml_qk"] = 2, 1
    K.slot_used["cmp"] = lambda st, sub: bk.filled(st, 1)
    K.slot_used["ml_qk"] = lambda st, sub: bk.filled(st, ("n", 1))
    K.wo_src[3] = (T["w_out_3"][0], yT)
    K.y_base[3] = K.y_count
    K.y_count += KT
    K.params.append(pool_params)
    K.wait_gain[3] = wait_gain
    for st in script:
        if st[0] == "tile" and st[2] == "gates":
            K.tiles[st]["wait"] = lambda pe: pe.wait_ge(s_tab, n_tab)
    K.stage("pool", norm3=pool_norm, tile3=pool_tile, b3_tables=pool_tables, wo3=pool_wo)
    K.stage("pe", mg_rows=pe_mg_rows, mg_nat=pe_mg_nat, cmp=pe_cmp, cmp2=pe_cmp2, nsa_s=pe_nsa_s, nsa_t=pe_nsa_t,
            nsa_v=pe_nsa_v, nsa_o=pe_nsa_o, ml_qk=pe_ml_qk, ml_s=pe_ml_s, ml_u=pe_ml_u, ml_n=pe_ml_n, ml_t=pe_ml_t,
            wo_gate=pe_wo_gate)
    K.stage("act", tile3=act_tile, mg_rows=act_mg_rows, cmp=act_cmp, cmp2=act_cmp2, nsa_s=act_nsa_s, nsa_t=act_nsa_t,
            ml_qk=act_ml_qk, ml_s=act_ml_s, ml_n=act_ml_n, wo_gate=act_wo_gate, final3=K.act_rstd_x)
    K.stage("vec", tile3=vec_tile, mg_rows=vec_mg_rows, mg_nat=vec_mg_nat, cmp=vec_cmp, nsa_s=vec_nsa_s, nsa_t=vec_nsa_t,
            nsa_v=vec_nsa_v, nsa_o=vec_nsa_o, ml_qk=vec_ml_qk, ml_s=vec_ml_s, ml_u=vec_ml_u, ml_n=vec_ml_n, ml_t=vec_ml_t,
            wo3=vec_wo, final3=vec_final)
    return script


BLOCKS = {1: block1, 2: block2, 3: block3}
WORK = 16912
PAR = 1152


class Kit:

    def __init__(self, nc, ctx, T):
        self.nc, self.ctx, self.T = nc, ctx, T
        self.at = {"pe": {}, "act": {}, "vec": {}, "pool": {}}
        self.uses, self.tiles, self.params = {}, {}, []
        self.norm_gain, self.par_count, self.wo_src = {}, {}, {}
        self.y_base, self.y_count = {}, 0
        self.slot_src, self.slot_count, self.slot_used = {}, {"tile": 1, "wo": 4, "ada": 1}, {}
        self.const_loads, self.wait_gain, self.par_at = [], {}, 0
        self.sp_start = []

    def keep(self, *dims):
        n = math.prod(dims)
        ap = self.par[:, self.par_at:self.par_at + n]
        self.par_at += n
        assert self.par_at <= PAR
        return ap.rearrange("p (a b) -> p a b", b=dims[1]) if len(dims) == 2 else ap

    def sb(self, name, *dims, dt=F32):
        return self.ctx.enter_context(self.nc.sbuf_tensor(name, [P, *dims], dt))

    def sem(self, name):
        return self.ctx.enter_context(self.nc.semaphore(name))

    def arena(self, start=0, base=None):
        at = [start]
        region = self.work if base is None else base

        def take(name, *dims):
            n = math.prod(dims)
            ap = region[:, at[0]:at[0] + n]
            at[0] += n
            assert at[0] <= region.shape[1], (name, at[0])
            if len(dims) == 2:
                ap = ap.rearrange("p (a b) -> p a b", b=dims[1])
            elif len(dims) == 3:
                ap = ap.rearrange("p (a b c) -> p a b c", b=dims[1], c=dims[2])
            return ap
        take.at = at
        return take

    def stage(self, eng, **fns):
        self.at[eng].update(fns)

    def tile(self, st, srcs, mode, w, act, n, kt=KT, bias=None, after=(), readers=1):
        self.tiles[st] = dict(srcs=srcs, mode=mode, w=w, act=act, n=n, kt=kt, bias=bias, after=list(after),
                              readers=readers)

    def after_norm(self, st, blk, rows=TT):
        self.tiles[st]["after"] += [(("norm", blk, tt), k4) for tt in range(rows) for k4 in range(KT // 4)]


def build(nc, T, out, blocks):
    with ExitStack() as ctx:
        K = Kit(nc, ctx, T)
        A, B = K.sb("A", KT * SEQ), K.sb("B", KT * SEQ)
        K.A, K.B = A, B
        K.A_kt = A.rearrange("p (k t) -> p k t", t=SEQ)
        K.B_kt = B.rearrange("p (k t) -> p k t", t=SEQ)
        K.memT = None
        K.X = X = K.sb("X", TT, D)
        ring = K.sb("ring", RING, KT, P)
        K.work = K.sb("work", WORK)
        K.ident = K.sb("ident", P)
        K.ones = K.sb("ones", P)
        K.reset = K.sb("reset", SEQ)
        K.eps = K.sb("eps", 1)
        K.rstd = K.sb("rstd", TT)
        K.blocks, K.modulated = list(blocks), False
        K.par = K.sb("par", PAR)
        K.hn = K.work[:, 0:2 * D].rearrange("p (a d) -> p a d", d=D)
        K.hn_junk = K.hn[:, 1, :]
        banks = [ctx.enter_context(nc.psum_tensor(f"bank{i}", [P, NC], F32)) for i in range(8)]

        full = [K.sem(f"bank{i}_full") for i in range(8)]
        free = [K.sem(f"bank{i}_free") for i in range(8)]
        K.bk = bk = Banks(full, free)
        loaded = [K.sem(f"slot{i}_loaded") for i in range(RING)]
        wo_used = K.sem("wo_slot_used")
        K.s_const = K.sem("constants_ready")
        s_made = K.sem("constants_made")
        K.s_x = s_x = [K.sem(f"x_rows{tt}_loaded") for tt in range(TT)]
        K.s_hn = s_hn = K.sem("normed_rows_ready")
        K.s_ss = s_ss = K.sem("square_sums_ready")
        K.s_ms = s_ms = K.sem("mean_squares_ready")
        K.s_rt = s_rt = K.sem("root_ready")
        K.s_rstd = s_rstd = K.sem("rstd_ready")
        K.y_done = K.sem("mixed_tile_done")
        K.x_done = K.sem("x_rows_done")
        s_out = K.sem("rows_stored")
        act_step, vec_step = K.sem("act_step"), K.sem("vec_step")
        K.act_step, K.vec_step = act_step, vec_step
        K.ps = lambda st, key=0: banks[bk.bank(st, key)][:, :]

        norms = {}
        K.norms = norms

        def act_rstd(act, L, st, src, junk):
            i = norms[st]
            nc.scalar.activation(junk, src, ACT.Square, accum_out=K.rstd[:, st[2]:st[2] + 1]).then_inc(s_ss, 1)
            act.wait_ge(s_ms, i + 1)
            tt = st[2]
            nc.scalar.activation(K.rstd[:, tt:tt + 1], K.rstd[:, tt:tt + 1], ACT.Sqrt).then_inc(s_rt, 1)

        def vec_rstd(vec, L, st):
            i, tt = norms[st], st[2]
            vec.wait_ge(s_ss, i + 1)
            r1 = K.rstd[:, tt:tt + 1]
            nc.vector.tensor_scalar(r1, r1, 1.0 / D, EPS, ALU.mult, ALU.add).then_inc(s_ms, 1)
            vec.wait_ge(s_rt, i + 1)
            nc.vector.reciprocal(r1, r1).then_inc(s_rstd, 1)
            vec.wait_ge(s_rstd, i + 1)
        K.vec_rstd = vec_rstd

        def act_rstd_x(act, L, st):
            _, blk, tt = st
            if tt == 0:
                act.wait_ge(*bk.filled(("wo", blk, 3), 3))
            act.wait_ge(*bk.released(("wo", blk, 3), tt))
            act_rstd(act, L, st, X[:, tt, :], K.hn_junk)
            act.wait_ge(s_ss, norms[st] + 1)
        K.act_rstd, K.act_rstd_x = act_rstd, act_rstd_x

        block_of = BLOCKS
        script = []
        for b in blocks:
            part = block_of[b](K)
            if b == 2 and 3 in blocks:
                modulation(K)
                K.modulated = True
                part = deal(part, ada_stages())
            script += part
        for st in script:
            if st[0] in ("norm", "final"):
                norms[st] = len(norms)
        normed = [st for st in script if st[0] == "norm"]
        hn_at = {st: n for n, st in enumerate(normed)}
        slots = []
        for st in script:
            if st[0] == "norm":
                for k4 in range(KT // 4):
                    bk.plan(st, k4, "S")
            elif st[0] == "tile":
                bk.plan(st, 0, "P", K.tiles[st].get("readers", 1))
            elif st[0] == "wo":
                for tt in range(TT):
                    bk.plan(st, tt, (st[2] % 2) * 4 + tt)
            slots += [(st, sub) for sub in range(K.slot_count.get(st[0], 0))]
            for key, pool, readers in K.uses.get(st, []):
                bk.plan(st, key, pool, readers)
        slot_of, slot_value, count, loads = {}, {}, [0] * RING, []
        wo_count = 0
        for n, (st, sub) in enumerate(slots):
            i = n % RING
            if st[0] == "tile":
                t = K.tiles[st]
                dmas, at = [], 0
                for w, c0, width in t["srcs"]:
                    dmas.append((ring[:, i, 0:t["kt"], at:at + width],
                                 w[:, c0:c0 + width].rearrange("(k p) c -> p k c", p=P)))
                    at += width
                used = bk.filled(st)
            elif st[0] == "ada":
                dmas = [(ring[:, i, :, :].rearrange("p k c -> p (k c)").rearrange("p (k c) -> p k c", c=ADA_W),
                         T["w_ada_3"][0][2 * st[2] * P:(2 * st[2] + 2) * P, st[1] * ADA_W:(st[1] + 1) * ADA_W]
                         .rearrange("(k p) c -> p k c", p=P))]
                used = (K.ada_used, ADA_KP * st[1] + st[2] + 1)
            elif st[0] in K.slot_src:
                dmas = K.slot_src[st[0]](st, sub, ring[:, i, :, :])
                used = K.slot_used[st[0]](st, sub)
            else:
                w = K.wo_src[st[1]][0]
                dmas = [(ring[:, i, :, :].rearrange("p k c -> p (k c)").rearrange("p (k c) -> p k c", c=NC),
                         w[sub * 4 * P:(sub + 1) * 4 * P, st[2] * NC:(st[2] + 1) * NC].rearrange("(k p) c -> p k c", p=P))]
                if sub < 3:
                    wo_count += 1
                    used = (wo_used, wo_count)
                else:
                    used = bk.filled(st, 3)
            count[i] += 16 * len(dmas)
            slot_of[st, sub], slot_value[st, sub] = i, count[i]
            loads.append((i, dmas, used))
        K.slot_ap = lambda st, sub=0: ring[:, slot_of[st, sub], :, :]
        K.slot_loaded = lambda st, sub=0: (loaded[slot_of[st, sub]], slot_value[st, sub])
        x_after = {blk: (g + 1) * TT for g, blk in enumerate(blocks)}
        x_total = TT * len(blocks)

        def by_block(st):
            return st[0] + str(st[1]) if st[0] in ("norm", "tile", "final", "wo") else st[0]

        block = ctx.enter_context(nc.Block())

        @block.sync
        def _(sp):
            for tt in range(TT):
                sp.dma_start(X[:, tt, :], T["x"][0, tt * P:(tt + 1) * P, :]).then_inc(s_x[tt], 16)
            for fn in K.sp_start:
                fn(sp)
            for n, (i, dmas, _) in enumerate(loads):
                if n >= RING:
                    sp.wait_ge(*loads[n - RING][2])
                for dst, src in dmas:
                    sp.dma_start(dst, src).then_inc(loaded[i], 16)
            for tt in range(TT):
                sp.wait_ge(K.x_done, x_total - TT + tt + 1)
                sp.dma_start(out[0, tt * P:(tt + 1) * P, :], X[:, tt, :]).then_inc(s_out, 16)
            sp.wait_ge(s_out, 16 * TT)

        @block.gpsimd
        def _(pool):
            pool.dma_start(K.ident[:, :], T["c_ident"]).then_inc(K.s_const, 16)
            pool.dma_start(K.reset[:, :], T["c_reset"].partition_broadcast(P)).then_inc(K.s_const, 16)
            for extra in K.const_loads:
                pool.dma_start(*extra).then_inc(K.s_const, 16)
            nc.gpsimd.memset(K.ones[:, :], 1.0).then_inc(s_made, 1)
            nc.gpsimd.memset(K.eps[:, :], EPS).then_inc(s_made, 1)
            for fn in K.params:
                fn(pool)
            for st in script:
                if by_block(st) in K.at["pool"]:
                    K.at["pool"][by_block(st)](pool, st)

        const_total = 16 * (2 + len(K.const_loads))

        @block.tensor
        def _(pe):
            pe.wait_ge(K.s_const, const_total)
            pe.wait_ge(s_made, 2)
            for st in script:
                if st[0] == "norm":
                    pe.wait_ge(s_hn, hn_at[st] + 1)
                    for k4 in range(KT // 4):
                        bk.take(pe, st, k4)
                        for j in range(4):
                            kk = 4 * k4 + j
                            mm = nc.tensor.transpose(K.ps(st, k4)[:, j * P:(j + 1) * P],
                                                     K.hn[:, hn_at[st] % 2, kk * P:(kk + 1) * P], K.ident[:, :])
                        mm.then_inc(bk.full_sem(st, k4), 1)
                elif st[0] == "tile":
                    t = K.tiles[st]
                    i, w = slot_of[st, 0], t["w"]
                    if t.get("wait"):
                        t["wait"](pe)
                    for dep in t["after"]:
                        pe.wait_ge(*bk.released(*dep))
                    pe.wait_ge(loaded[i], slot_value[st, 0])
                    bk.take(pe, st)
                    b = K.ps(st)
                    if t["mode"] == "T":
                        for kk in range(t["kt"]):
                            mm = nc.tensor.matmul(b[0:w, 0:t["n"]], lhsT=ring[:, i, kk, 0:w], rhs=t["act"][:, kk, :],
                                                  start=(kk == 0), stop=(kk == t["kt"] - 1))
                    else:
                        for tt in range(t["n"] // P):
                            o = b[:, tt * P:tt * P + w]
                            if t["bias"] is not None:
                                nc.tensor.matmul(o, lhsT=K.ones[0:1, :], rhs=t["bias"], start=True, stop=False)
                            for kk in range(t["kt"]):
                                mm = nc.tensor.matmul(o, lhsT=t["act"][:, kk, tt * P:(tt + 1) * P], rhs=ring[:, i, kk, 0:w],
                                                      start=(kk == 0 and t["bias"] is None), stop=(kk == t["kt"] - 1))
                    mm.then_inc(bk.full_sem(st), 1)
                elif st[0] == "wo":
                    _, blk, n = st
                    yT = K.wo_src[blk][1]
                    pe.wait_ge(K.y_done, K.y_base[blk] + KT)
                    for tt in range(TT):
                        bk.take(pe, st, tt)
                    for kq in range(4):
                        i = slot_of[st, kq]
                        pe.wait_ge(loaded[i], slot_value[st, kq])
                        w = ring[:, i, :, :].rearrange("p k c -> p (k c)").rearrange("p (k c) -> p k c", c=NC)
                        for j in range(4):
                            for tt in range(TT):
                                kk = 4 * kq + j
                                mm = nc.tensor.matmul(K.ps(st, tt), lhsT=yT[:, kk, tt * P:(tt + 1) * P], rhs=w[:, j, :],
                                                      start=(kk == 0), stop=(kk == KT - 1), skip_group_check=True)
                                if kk == KT - 1:
                                    mm.then_inc(bk.full_sem(st, tt), 1)
                        if kq < 3:
                            mm.then_inc(wo_used, 1)
                elif st[0] in K.at["pe"]:
                    K.at["pe"][st[0]](pe, st)

        @block.scalar
        def _(act):
            L = Lane(act, act_step)
            act.wait_ge(K.s_const, const_total)
            act.wait_ge(s_made, 2)
            for st in script:
                if st[0] == "norm":
                    _, blk, tt = st
                    rows = K.mem_rows[:, tt, :] if blk == "mem" else X[:, tt, :]
                    if blk == "mem":
                        act.wait_ge(K.s_mem, 16 * (MEM // P))
                    elif blk == blocks[0]:
                        act.wait_ge(s_x[tt], 16)
                    else:
                        act.wait_ge(K.x_done, x_after[blk - 1] - TT + tt + 1)
                    n = hn_at[st]
                    if n >= 2:
                        act.wait_ge(*bk.filled(normed[n - 2], KT // 4 - 1))
                    act_rstd(act, L, st, rows, K.hn[:, n % 2, :])
                    act.wait_ge(s_rstd, norms[st] + 1)
                    nc.scalar.activation(K.hn[:, n % 2, :], rows, ACT.Copy, scale=K.rstd[:, tt:tt + 1]).then_inc(s_hn, 1)
                elif by_block(st) in K.at["act"]:
                    K.at["act"][by_block(st)](act, L, st)

        @block.vector
        def _(vec):
            L = Lane(vec, vec_step)
            K.vlane = [L]
            vec.wait_ge(K.s_const, const_total)
            vec.wait_ge(s_made, 2)
            for st in script:
                if st[0] == "norm":
                    _, blk, tt = st
                    vec_rstd(vec, L, st)
                    gain, shift = K.norm_gain[blk]
                    dst = {"mem": K.memT, 2: K.B_kt}.get(blk, K.A_kt)
                    if tt == 0:
                        K.wait_gain[blk](vec)
                    for k4 in range(KT // 4):
                        vec.wait_ge(*bk.filled(st, k4))
                        o = dst[:, 4 * k4:4 * k4 + 4, tt * P:(tt + 1) * P]
                        g4 = gain[:, 4 * k4:4 * k4 + 4].unsqueeze(2).to_broadcast([P, 4, P])
                        b = K.ps(st, k4).rearrange("p (k t) -> p k t", t=P)
                        if shift is None:
                            nc.vector.tensor_tensor(o, b, g4, ALU.mult).then_inc(bk.free_sem(st, k4), 1)
                        else:
                            L(nc.vector.tensor_tensor(o, b, g4, ALU.mult))
                            L.settle()
                            s4 = shift[:, 4 * k4:4 * k4 + 4].unsqueeze(2).to_broadcast([P, 4, P])
                            nc.vector.tensor_tensor(o, o, s4, ALU.add).then_inc(bk.free_sem(st, k4), 1)
                elif by_block(st) in K.at["vec"]:
                    K.at["vec"][by_block(st)](vec, L, st)


def constants():
    import numpy as np
    c = {"c_ident": np.eye(P, dtype=np.float32)}
    h, q, j = np.arange(4), np.arange(P)[:, None], np.arange(SEQ)[None, :]
    c["c_sel"] = np.ascontiguousarray(np.broadcast_to(np.eye(4, dtype=np.float32)[:, :, None], (4, 4, P)))
    c["c_ndist"] = np.where(j - (SEQ - P) <= q, j - (SEQ - P) - q, NEG).astype(np.float32)
    s, l = np.arange(P)[:, None], np.arange(P)[None, :]
    c["c_maskbd"] = np.where((s // 64 == l // 64) & (s <= l), 0.0, NEG).astype(np.float32)
    n = np.arange((SEQ - 32) // 16 + 1)
    t = np.arange(TT)[None, :, None] * P + np.arange(P)[:, None, None]
    mid, end = n * 16 + 15.5, n * 16 + 31
    c["c_cdist"] = np.where(end <= t, -(t.astype(np.float32) - mid.astype(np.float32)), NEG).astype(np.float32)
    p = np.arange(P)
    c["c_invf"] = (np.float32(10000.0) ** (-(2 * (p % 32)).astype(np.float32) / np.float32(64)))[:, None].astype(np.float32)
    perm = np.zeros((P, P), np.float32)
    for m in p:
        perm[m + 32 if m % 64 < 32 else m - 32, m] = -1.0 if m % 64 < 32 else 1.0
    c["c_perm"] = perm
    c["c_sgn"] = np.where((p < 64)[:, None], [[-1.0, 1.0]], [[1.0, -1.0]]).astype(np.float32)
    c["c_tri"] = np.where(np.arange(SEQ)[None, :] - (SEQ - P) <= p[:, None], 0.0, NEG).astype(np.float32)
    c["c_reset"] = (np.arange(SEQ) % 64 != 0).astype(np.float32)
    return c


def kernel(**inputs):
    import numpy as np
    import concourse.bacc as bacc
    from concourse.bass_utils import run_bass_kernel_spmd as run

    nc = bacc.Bacc("TRN2", target_bir_lowering=False, num_devices=1)
    arrays, T = {}, {}
    for name, a in {**inputs, **constants()}.items():
        a = np.ascontiguousarray(a)
        arrays[f"in_{name}"] = a
        T[name] = nc.dram_tensor(f"in_{name}", a.shape, mybir.dt.from_np(a.dtype), kind="ExternalInput").ap()
    out = nc.dram_tensor("out_x", (1, SEQ, D), F32, kind="ExternalOutput").ap()
    build(nc, T, out, [b for b, name in ((1, "w_in"), (2, "w_in_2"), (3, "w_in_3")) if name in inputs])
    return run(nc, [arrays], core_ids=[0]).results[0]["out_x"]
```

```python
import concourse.bass as bass
from concourse import mybir
from contextlib import ExitStack
import math

F32 = mybir.dt.float32
F32R = mybir.dt.float32r
I32 = mybir.dt.int32
ALU = mybir.AluOpType
ACT = mybir.ActivationFunctionType
AX = mybir.AxisListType

P = 128
SEQ = 512
D = 2048
KT = D // P
TT = SEQ // P
NC = 512
EPS = 1e-6
NEG = -1e30
RING = 4
SLOT = 1024
PROJ_BANKS = (0, 1, 2)
SIDE_BANKS = (3, 4, 5, 6, 7)


class Lane:

    def __init__(self, eng, sem):
        self.eng, self.sem, self.n = eng, sem, 0

    def __call__(self, ins):
        ins.then_inc(self.sem, 1)
        self.n += 1

    def settle(self):
        self.eng.wait_ge(self.sem, self.n)


class Banks:

    def __init__(self, full, free):
        self.full, self.free = full, free
        self.uses, self.freed = [0] * 8, [0] * 8
        self.at, self.turn = {}, {"P": 0, "S": 0}

    def plan(self, stage, key, pool, readers=1):
        if pool in self.turn:
            group = PROJ_BANKS if pool == "P" else SIDE_BANKS
            b = group[self.turn[pool] % len(group)]
            self.turn[pool] += 1
        else:
            b = pool
        self.uses[b] += 1
        before = self.freed[b]
        self.freed[b] += readers
        self.at[stage, key] = (b, self.uses[b], before, self.freed[b])

    def bank(self, stage, key=0):
        return self.at[stage, key][0]

    def take(self, pe, stage, key=0):
        b, _, before, _ = self.at[stage, key]
        if before:
            pe.wait_ge(self.free[b], before)

    def filled(self, stage, key=0):
        b, use, _, _ = self.at[stage, key]
        return self.full[b], use

    def full_sem(self, stage, key=0):
        return self.full[self.at[stage, key][0]]

    def free_sem(self, stage, key=0):
        return self.free[self.at[stage, key][0]]

    def released(self, stage, key=0):
        b, _, _, after = self.at[stage, key]
        return self.free[b], after

    def read_once(self, stage, key=0):
        b, _, _, after = self.at[stage, key]
        return self.free[b], after - 1


def spread_steps(tiles, steps):
    out, done = [], 0
    for i, t in enumerate(tiles):
        upto = len(steps) * (i + 1) // len(tiles)
        out += [t] + steps[done:upto]
        done = upto
    return out


def deal(script, steps):
    n, tiles, out, done = 0, sum(st[0] == "tile" for st in script), [], 0
    for st in script:
        out.append(st)
        if st[0] == "tile":
            n += 1
            upto = len(steps) * n // tiles
            out += steps[done:upto]
            done = upto
    return out


S_G, S_H, S_N = 64, 16, 64
S_W = S_G * S_H
S_L = P // S_H
S_B = SEQ // S_L
S_CG = P // S_H
S_C = S_G // S_CG
DF_H, DF_D, DF_V = 4, 64, 128
XA_H, XA_D, MEM = 4, 128, 256
LAMBDA_INIT = 0.8 - 0.6 * math.exp(-0.3 * 0)
MAGIC = 1.5 * 2.0 ** 23
TWO_PI = (6.28125, 1.93500518798828125e-3, 3.01991598196e-7)
PI_DOWN = 3.1415925


def block1(K):
    nc, T, ps, bk = K.nc, K.T, K.ps, K.bk
    hT, yT, X = K.A_kt, K.B_kt, K.X
    Bf, Xf = K.B, X.rearrange("p t d -> p (t d)")
    mem_rows = Bf[:, 0:2 * D].rearrange("p (t d) -> p t d", d=D)
    memT = Bf[:, 2 * D:4 * D].rearrange("p (k m) -> p k m", m=MEM)
    K.mem_rows, K.memT = mem_rows, memT

    norm_pre, norm_mem, b_glu = K.keep(KT), K.keep(KT), K.keep(8)
    subln, nlam, lamp = K.keep(1), K.keep(1), K.keep(2)
    invf = K.keep(1)
    d_skip = K.keep(S_G)
    sgn = K.keep(2)
    K.norm_gain[1] = (norm_pre, None)
    K.norm_gain["mem"] = (norm_mem, None)
    mx, sums, rs = K.keep(2, 2), K.keep(4, 2), K.keep(2, 2)
    oss = K.keep(TT)

    a = K.arena()
    mk, mv = a("mk", XA_H, MEM), a("mv", MEM // P, XA_H * XA_D)
    qr, kr = a("q", 2, SEQ), a("k", 2, SEQ)
    raw = a("raw", 2, SEQ)
    v = a("v", 2, TT, DF_V)
    ropeC, ropeS = a("cos", SEQ), a("sin", SEQ)
    tri, perm = a("tri", SEQ), a("perm", P)
    e_at = a.at[0]
    e = a("e", 2, 2, SEQ)
    pT = a("pT", 2, SEQ)
    obuf = a("o", TT, P)
    pb_at = a.at[0]
    pb_re, pb_im = a("pb_re", S_G, S_L), a("pb_im", S_G, S_L)
    pc_re, pc_im = a("pc_re", S_G, S_L + 1), a("pc_im", S_G, S_L + 1)
    z_re, z_im = a("z_re", S_G), a("z_im", S_G)
    l_re, l_im = a("l_re", S_G), a("l_im", 2, S_G)
    inm = a("inm", S_CG, P)
    krow = a("krow", S_CG, P)
    braw = a("braw", 4, S_CG * S_H)
    craw = a("craw", 2, 3 * S_N)
    t = K.arena(0, Bf)
    ba = t("ba", S_CG * S_L, S_H)
    ca = t("ca", S_CG, (S_L + 1) * S_H)
    tmp = t("tmp", S_CG * (S_L + 1), S_H)
    ublk = t("ublk", S_CG * S_B)
    bst, bsw = t("bst", S_CG, S_H), t("bsw", S_CG, S_H)
    us = Xf[:, 0:2 * SEQ].rearrange("p (a s) -> p a s", s=SEQ)
    vst = Xf[:, :].rearrange("p (s b g) -> p s b g", s=2, b=S_B)
    ych = Xf[:, 0:S_C * SEQ].rearrange("p (c s) -> p c s", s=SEQ)
    sig = Xf[:, S_C * SEQ:(S_C + 2) * SEQ].rearrange("p (c s) -> p c s", s=SEQ)
    w = K.arena(e_at)
    T2 = [ba.rearrange("p a b -> p (a b)"), tmp.rearrange("p a b -> p (a b)")[:, 0:S_CG * P]]
    C2 = [ca.rearrange("p a b -> p (a b)")[:, 0:S_CG * P], krow.rearrange("p a b -> p (a b)")]
    U2 = [ublk, braw.rearrange("p a b -> p (a b)")]
    ybuf = inm.rearrange("p a b -> p (a b)").rearrange("p (a s) -> p a s", s=SEQ)
    scan_t = w("scan_t", 4, S_G)
    rope_t = K.arena(pb_at)("rope_t", 2, SEQ)
    w = K.arena(e_at)
    pos_i = w("pos_i", SEQ).bitcast(I32)
    ang, kk_, half = w("ang", SEQ), w("turns", SEQ), w("half", SEQ)
    w = K.arena(e_at)
    araw = w("araw", 2, 2 * S_N)
    logdt = w("logdt", S_G)
    lqk = w("lqk", 4, DF_D)
    lqk_j = w("lqk_j", DF_D)
    tm = [w(f"tm{i}", S_G) for i in range(14)]
    w = K.arena()
    mix, gain_post, junk = w("mix", TT, D), w("gain_post", D), w("junk", D)
    U_d = nc.dram_tensor("u_blocks", (P, S_G, S_B), F32).ap()
    KD = nc.dram_tensor("taps", (S_H, S_G, 2 * P), F32).ap()
    CA_d = nc.dram_tensor("out_matrices", (S_C, P, S_CG * P), F32).ap()
    Y_d = nc.dram_tensor("y_channels", (S_G, S_H, S_L, S_B), F32).ap()

    col, c0 = {}, 0
    for n, wd in (("us", S_W), ("gs", S_W), ("qd", 512), ("kd", 512), ("vd", 512), ("gd", 512), ("qx", 512), ("gx", 512)):
        col[n] = c0
        c0 += wd
    W, WM, WG = T["w_in"][0], T["w_mem_kv"][0], T["w_glu"][0]

    def tile(name, i):
        st = ("tile", 1, name, i)
        if name == "mk":
            K.tile(st, [(WM, i * P, P)], "T", P, memT, MEM)
        elif name == "mv":
            K.tile(st, [(WM, 512 + i * P, P)], "N", P, memT, MEM)
        elif name == "glu":
            K.tile(st, [(WG, i * P, P)], "T", P, ych, SEQ, kt=8)
        else:
            K.tile(st, [(W, col[name] + i * P, P)], "N" if name == "vd" else "T", P, hT, SEQ,
                   readers=1)
        return st

    script = [("norm", 1, tt) for tt in range(TT)] + [("b1_tables", 0), ("ss_par", 0)]
    ut = [tile("us", i) for i in range(S_C)]
    K.after_norm(ut[0], 1)
    script += ut[0:2] + [("rope_tab", 0)] + ut[2:4] + [("norm", "mem", 0)] + ut[4:6] + [("norm", "mem", 1)] + ut[6:8]
    mt = [t_ for h in range(XA_H) for t_ in (tile("mk", h), tile("mv", h))]
    K.tiles[mt[0]]["after"] += [(("norm", "mem", tt), k4) for tt in range(2) for k4 in range(KT // 4)]
    gates = [tile("gd", h) for h in range(DF_H)] + [tile("gx", h) for h in range(XA_H)]
    steps = []
    for c in range(S_C + 2):
        if 0 <= c - 2 < S_C:
            steps.append(("sp_c", c - 2))
        if 0 <= c - 1 < S_C:
            steps.append(("sp_b", c - 1))
        if c < S_C:
            steps.append(("sp_a", c))
    qt = [[tile(n, h) for n in ("qd", "kd", "vd")] for h in range(DF_H)]
    xt = [tile("qx", h) for h in range(XA_H)]
    script += spread_steps(mt + gates[0:4], steps)
    script += [("scan", 0)] + gates[4:8] + qt[0] + [("rope", 0)]
    units = [("d", h, qb) for h in range(DF_H) for qb in range(TT)] + [("x", h, qb) for h in range(XA_H) for qb in range(TT)]
    at = {u: n for n, u in enumerate(units)}

    def attention_steps(n):
        out = []
        if n < len(units):
            out.append(("at_s", n))
        if 0 <= n - 1 < len(units):
            out.append(("at_t", n - 1))
        if 0 <= n - 2 < len(units):
            out.append(("at_v", n - 2))
            if units[n - 2][2] == TT - 1:
                out.append(("at_o", n - 2))
        return out

    n = 0
    for h in range(DF_H):
        nxt = qt[h + 1] + [("rope", h + 1)] if h + 1 < DF_H else xt[0:2]
        tiles_ = [s for s in nxt if s[0] == "tile"]
        for i, t_ in enumerate(nxt):
            script.append(t_)
            if t_[0] == "tile":
                while n < 4 * h + 4 * (i + 1) // len(tiles_):
                    script += attention_steps(n)
                    n += 1
    gs = [tile("gs", i) for i in range(8)]
    glu = [tile("glu", i) for i in range(8)]
    p2 = [("sp_d", c) for c in range(S_C)]
    script += attention_steps(n)
    n += 1
    left = [attention_steps(m) for m in range(n, len(units) + 2)]
    done = 0
    for i in range(S_C):
        script.append(p2[i])
        upto = len(left) * (i + 1) // S_C
        for m in left[done:upto]:
            script += m
            for h in (2, 3):
                if ("at_s", at["x", h - 2, TT - 1]) in m:
                    script.append(xt[h])
        done = upto
    script += [("y_back", 0)] + gs + [("gelu", 0)] + glu
    script += [("wo", 1, n) for n in range(4)] + [("final", 1, tt) for tt in range(TT)]
    for st in script:
        kind = st[0]
        if kind == "ss_par":
            K.uses[st] = [(0, "S", 1)]
        elif kind == "sp_a":
            K.uses[st] = [("c", "S", 1)]
        elif kind == "sp_b":
            K.uses[st] = [(("i", j), "S", 1) for j in range(2)] + [(("k", j), "S", 1) for j in range(2)]
        elif kind == "sp_c":
            K.uses[st] = [(s, "S", 1) for s in range(2)]
        elif kind == "sp_d":
            K.uses[st] = [(0, "S", 1)]
        elif kind == "rope":
            K.uses[st] = [(j, "S", 1) for j in range(2)]
        elif kind == "at_s":
            K.uses[st] = [(c, "S", 1) for c in range(2)] if units[st[1]][0] == "d" else [(0, "S", 2)]
        elif kind in ("at_t", "at_v", "at_o"):
            K.uses[st] = [(0, "S", 1)]

    s_par, s_tab = K.sem("b1_params"), K.sem("b1_tables")
    s_mem = K.sem("mem_loaded")
    K.s_mem = s_mem
    s_tb = K.sem("setup_loads")
    s_zero, s_zst = K.sem("zero_taps"), K.sem("zero_taps_stored")
    s_sa, s_sv = K.sem("setup_act"), K.sem("setup_vec")
    s_pow = K.sem("powers_ready")
    s_u = [K.sem(f"u_stored{i}") for i in range(4)]
    s_ul = [K.sem(f"u_block_loaded{i}") for i in range(2)]
    s_bc = [K.sem(f"bc_loaded{i}") for i in range(2)]
    s_ba, s_ca = K.sem("b_powers_ready"), K.sem("c_powers_ready")
    s_kr = K.sem("taps_ready")
    s_kst, s_cst = K.sem("taps_stored"), K.sem("out_matrices_stored")
    s_scan, s_scand = K.sem("scan_step"), K.sem("scan_done")
    s_p2 = [K.sem(f"pass2_loaded{i}") for i in range(2)]
    s_yst = [K.sem(f"y_stored{i}") for i in range(2)]
    s_yb = K.sem("y_back")
    s_gelu = K.sem("gelu_ready")
    s_rope = K.sem("roped")
    s_score, s_exp, s_w = K.sem("b1_scores"), K.sem("b1_exps"), K.sem("b1_weights")
    s_o = K.sem("b1_heads")
    s_oss, s_ort = K.sem("b1_head_squares"), K.sem("b1_head_root")
    s_on = K.sem("b1_head_normed")
    s_back, s_fg = K.sem("x_back_1"), K.sem("norm_post_loaded")

    def sp_start(sp):
        for tt in range(MEM // P):
            sp.dma_start(mem_rows[:, tt, :], T["mem"][0, tt * P:(tt + 1) * P, :]).then_inc(s_mem, 16)
    K.sp_start.append(sp_start)

    def pool_params(pool):
        n = 0
        vec_of = lambda ap: ap.rearrange("o (k p) -> p (o k)", p=P)
        with nc.allow_non_contiguous_dma(reason="small per-channel parameters"):
            for dst, src in ((norm_pre, vec_of(T["norm_pre"])), (norm_mem, vec_of(T["norm_mem"])), (b_glu, vec_of(T["b_glu"])),
                             (subln, T["diff_subln"].rearrange("o d -> d o")), (invf, T["c_invf"]), (sgn, T["c_sgn"]),
                             (d_skip[0:S_H, :], T["ssm_d"][0].rearrange("g h -> h g"))):
                pool.dma_start(dst, src).then_inc(s_par, 16)
                n += 16
        K.par_count[1] = n

    def load_bc(pool, c):
        i = c % 2
        g = slice(c * S_CG, (c + 1) * S_CG)
        f = lambda ap: ap[0, g].rearrange("g p h -> p g h")
        b3 = [braw[:, 2 * i + j, :].rearrange("p (g h) -> p g h", h=S_H) for j in range(2)]
        re, im = f(T["ssm_b_re"]), f(T["ssm_b_im"])
        for dst, src in ((b3[0][0:64], re), (b3[0][64:128], im), (b3[1][0:64], im), (b3[1][64:128], re)):
            pool.dma_start(dst, src).then_inc(s_bc[i], 16)
        cre, cim = (T[n][0, g].rearrange("g h p -> (g h) p") for n in ("ssm_c_re", "ssm_c_im"))
        for j, src in enumerate((cre, cim, cre)):
            pool.dma_start(craw[:, i, j * S_N:(j + 1) * S_N], src).then_inc(s_bc[i], 16)

    def pool_tables(pool, st):
        pool.wait_ge(*bk.filled(("norm", 1, TT - 1), KT // 4 - 1))
        for j, n in enumerate(("ssm_a_re", "ssm_a_im")):
            for r in range(2):
                pool.dma_start(araw[0:S_G, j, r * S_N:(r + 1) * S_N], T[n][0]).then_inc(s_tb, 16)
        pool.dma_start(logdt, T["ssm_log_dt"][0].partition_broadcast(P)).then_inc(s_tb, 16)
        for j, n in enumerate(("diff_lq1", "diff_lk1", "diff_lq2", "diff_lk2")):
            pool.dma_start(lqk[:, j, :], T[n][0].partition_broadcast(P)).then_inc(s_tb, 16)
        pool.dma_start(tri, T["c_tri"]).then_inc(s_tab, 16)
        pool.dma_start(perm, T["c_perm"]).then_inc(s_tab, 16)
        nc.gpsimd.memset(krow[0:S_H, :, :], 0.0).then_inc(s_zero, 1)
        pool.wait_ge(s_zero, 1)
        for c in range(S_C):
            pool.dma_start(KD[:, c * S_CG:(c + 1) * S_CG, 0:P], krow[0:S_H, :, :]).then_inc(s_zst, 16)
        load_bc(pool, 0)
        load_bc(pool, 1)

    def pool_rope_tab(pool, st):
        pool.wait_ge(s_pow, 1)
        pool.dma_start(pos_i, T["positions"][0].partition_broadcast(P)).then_inc(s_tab, 16)

    def pool_tile(pool, st):
        _, _, name, i = st
        if name == "us":
            pool.wait_ge(*bk.released(st))
            dst = U_d.rearrange("(j h) g b -> g h j b", h=S_H)
            src = us[:, i % 2, :].rearrange("p (j b) -> p j b", b=S_B)
            for g in range(S_CG):
                pool.dma_start(dst[i * S_CG + g], src[g * S_H:(g + 1) * S_H]).then_inc(s_u[i % 4], 16)

    def pool_sp_a(pool, st):
        c = st[1]
        if c >= 1:
            pool.wait_ge(*bk.filled(("sp_c", c - 1), 1))
        else:
            pool.wait_ge(*bk.filled(("norm", "mem", 1), KT // 4 - 1))
        pool.wait_ge(s_u[c % 4], 16 * S_CG * (c // 4 + 1))
        pool.dma_start(ublk, U_d[:, c * S_CG:(c + 1) * S_CG, :].rearrange("p g b -> p (g b)")).then_inc(s_ul[c % 2], 16)

    def pool_sp_b(pool, st):
        c = st[1]
        pool.wait_ge(s_ca, c + 1)
        pool.dma_start(CA_d[c].rearrange("p (g m) -> p g m", m=P), ca[:, :, S_H:]).then_inc(s_cst, 16)
        pool.wait_ge(s_kr, c + 1)
        if c == 0:
            pool.wait_ge(s_zst, 16 * S_C)
        pool.dma_start(KD[:, c * S_CG:(c + 1) * S_CG, P:2 * P], krow[0:S_H, :, :]).then_inc(s_kst, 16)
        if c + 2 < S_C:
            pool.wait_ge(s_ba, c + 1)
            load_bc(pool, c + 2)

    def load_pass2(pool, c):
        i = c % 2
        t3 = T2[i].rearrange("p (g m) -> p g m", m=P)
        for j in range(S_L):
            pool.dma_start(t3[j * S_H:(j + 1) * S_H],
                           KD[:, c * S_CG:(c + 1) * S_CG, P - j * S_H:2 * P - j * S_H]).then_inc(s_p2[i], 16)
        pool.dma_start(C2[i], CA_d[c]).then_inc(s_p2[i], 16)
        pool.dma_start(U2[i], U_d[:, c * S_CG:(c + 1) * S_CG, :].rearrange("p g b -> p (g b)")).then_inc(s_p2[i], 16)

    def pool_scan(pool, st):
        pool.wait_ge(*bk.released(("sp_c", S_C - 1), 1))
        pool.wait_ge(s_kst, 16 * S_C)
        pool.wait_ge(s_cst, 16 * S_C)
        load_pass2(pool, 0)
        load_pass2(pool, 1)

    def pool_sp_d(pool, st):
        c = st[1]
        pool.wait_ge(*bk.released(st))
        dst = Y_d.rearrange("g o i b -> i o g b")
        for i in range(S_L):
            pool.dma_start(dst[i, :, c * S_CG:(c + 1) * S_CG, :],
                           ybuf[i * S_H:(i + 1) * S_H, c % 2, :].rearrange("p (g b) -> p g b", b=S_B)).then_inc(s_yst[c % 2], 16)
        if c + 2 < S_C:
            load_pass2(pool, c + 2)

    def pool_y_back(pool, st):
        for i in range(2):
            pool.wait_ge(s_yst[i], 16 * S_L * S_C // 2)
        for c in range(S_C):
            pool.dma_start(ych[:, c, :], Y_d[c * S_CG:(c + 1) * S_CG].rearrange("g o i b -> (g o) (i b)")).then_inc(s_yb, 16)

    def pool_wo(pool, st):
        if st[2] == 0:
            pool.wait_ge(K.y_done, K.y_base[1] + KT)
            for tt in range(TT):
                pool.dma_start(X[:, tt, :], T["x"][0, tt * P:(tt + 1) * P, :]).then_inc(s_back, 16)
            pool.dma_start(gain_post, T["norm_post"][0].partition_broadcast(P)).then_inc(s_fg, 16)

    def pe_ss_par(pe, st):
        pe.wait_ge(s_tb, n_tb)
        bk.take(pe, st)
        for j in range(2):
            mm = nc.tensor.transpose(ps(st)[:, j * S_G:(j + 1) * S_G], araw[0:S_G, j, :], K.ident[0:S_G, 0:S_G])
        mm.then_inc(bk.full_sem(st), 1)
    n_tb = 16 * 9

    def pe_sp_a(pe, st):
        c = st[1]
        pe.wait_ge(s_bc[c % 2], 16 * 7 * (c // 2 + 1))
        bk.take(pe, st, "c")
        for j in range(2):
            mm = nc.tensor.transpose(ps(st, "c")[:, j * P:(j + 1) * P], craw[:, c % 2, j * S_N:j * S_N + P], K.ident[:, :])
        mm.then_inc(bk.full_sem(st, "c"), 1)

    def pe_sp_b(pe, st):
        c = st[1]
        pe.wait_ge(s_ba, c + 1)
        for j in range(2):
            bk.take(pe, st, ("i", j))
            for g in range(4 * j, 4 * j + 4):
                mm = nc.tensor.transpose(ps(st, ("i", j))[:, (g % 4) * P:(g % 4 + 1) * P],
                                         ba[:, g * S_L:(g + 1) * S_L, :], K.ident[:, :])
            mm.then_inc(bk.full_sem(st, ("i", j)), 1)
        pe.wait_ge(s_ca, c + 1)
        for j in range(2):
            bk.take(pe, st, ("k", j))
            for g in range(4 * j, 4 * j + 4):
                mm = nc.tensor.matmul(ps(st, ("k", j))[0:S_H, (g % 4) * P:(g % 4 + 1) * P], lhsT=bst[:, g, :],
                                      rhs=ca[:, g, 0:P], start=True, stop=True)
            mm.then_inc(bk.full_sem(st, ("k", j)), 1)

    def pe_sp_c(pe, st):
        c = st[1]
        for j in range(2):
            pe.wait_ge(*bk.released(("sp_b", c), ("i", j)))
        pe.wait_ge(s_ul[c % 2], 16 * (c // 2 + 1))
        for s in range(2):
            bk.take(pe, st, s)
            for g in range(S_CG):
                o, u = ps(st, s)[:, g * S_B:(g + 1) * S_B], ublk[:, g * S_B:(g + 1) * S_B]
                if s == 0:
                    mm = nc.tensor.matmul(o, lhsT=inm[:, g, :], rhs=u, start=True, stop=True)
                else:
                    for r in range(2):
                        mm = nc.tensor.matmul(o[64 * r:64 * r + 64], lhsT=inm[:, g, 64 * (1 - r):64 * (1 - r) + 64], rhs=u,
                                              start=True, stop=True)
            mm.then_inc(bk.full_sem(st, s), 1)

    def pe_sp_d(pe, st):
        c = st[1]
        if c == 0:
            pe.wait_ge(s_scand, 1)
        pe.wait_ge(s_p2[c % 2], 160 * (c // 2 + 1))
        bk.take(pe, st)
        for g in range(S_CG):
            o = ps(st)[:, g * S_B:(g + 1) * S_B]
            nc.tensor.matmul(o, lhsT=T2[c % 2][:, g * P:(g + 1) * P], rhs=U2[c % 2][:, g * S_B:(g + 1) * S_B], start=True,
                             stop=False)
            mm = nc.tensor.matmul(o[:, 1:S_B], lhsT=C2[c % 2][:, g * P:(g + 1) * P], rhs=vst[:, 0, 0:S_B - 1, c * S_CG + g],
                                  start=False, stop=True)
        mm.then_inc(bk.full_sem(st), 1)

    def pe_rope(pe, st):
        h = st[1]
        pe.wait_ge(s_tab, 48)
        for j, n in enumerate(("qd", "kd")):
            pe.wait_ge(*bk.released(("tile", 1, n, h)))
            bk.take(pe, st, j)
            nc.tensor.matmul(ps(st, j), lhsT=perm[:, :], rhs=raw[:, j, :], start=True, stop=True).then_inc(bk.full_sem(st, j), 1)

    def pe_at_s(pe, st):
        u = st[1]
        kind, h, qb = units[u]
        t_ = slice(qb * P, (qb + 1) * P)
        if kind == "d":
            pe.wait_ge(s_rope, h + 1)
            for c in range(2):
                r = slice(64 * c, 64 * c + 64)
                bk.take(pe, st, c)
                nc.tensor.matmul(ps(st, c)[:, 0:(qb + 1) * P], lhsT=qr[r, h % 2, t_], rhs=kr[r, h % 2, 0:(qb + 1) * P],
                                 start=True, stop=True).then_inc(bk.full_sem(st, c), 1)
        else:
            if qb == 0:
                pe.wait_ge(*bk.released(("tile", 1, "qx", h)))
                pe.wait_ge(*bk.released(("tile", 1, "mk", h)))
            bk.take(pe, st)
            nc.tensor.matmul(ps(st)[:, 0:MEM], lhsT=qr[:, h % 2, t_], rhs=mk[:, h, :], start=True,
                             stop=True).then_inc(bk.full_sem(st), 1)

    def pe_at_t(pe, st):
        u = st[1]
        kind, h, qb = units[u]
        if kind == "d":
            pe.wait_ge(s_w, u + 1)
        else:
            pe.wait_ge(s_exp, 32 + u - 15)
        bk.take(pe, st)
        for kt in range(qb + 1 if kind == "d" else MEM // P):
            mm = nc.tensor.transpose(ps(st)[:, kt * P:(kt + 1) * P], e4[u % 2][0][:, kt * P:(kt + 1) * P], K.ident[:, :])
        mm.then_inc(bk.full_sem(st), 1)

    e4 = [[e[:, p, c, :] for c in range(2)] for p in range(2)]

    def pe_at_v(pe, st):
        u = st[1]
        kind, h, qb = units[u]
        pe.wait_ge(*bk.released(("at_t", u)))
        if kind == "d":
            pe.wait_ge(*bk.released(("tile", 1, "vd", h)))
        else:
            pe.wait_ge(*bk.released(("tile", 1, "mv", h)))
        bk.take(pe, st)
        n = qb + 1 if kind == "d" else MEM // P
        for kt in range(n):
            rhs = v[:, h % 2, kt, :] if kind == "d" else mv[:, kt, h * XA_D:(h + 1) * XA_D]
            mm = nc.tensor.matmul(ps(st)[:, 0:P], lhsT=pT[:, u % 2, kt * P:(kt + 1) * P], rhs=rhs, start=(kt == 0),
                                  stop=(kt == n - 1))
        mm.then_inc(bk.full_sem(st), 1)

    def pe_at_o(pe, st):
        i = st[1] // TT
        pe.wait_ge(s_on, i + 1)
        bk.take(pe, st)
        for tt in range(TT):
            mm = nc.tensor.transpose(ps(st)[:, tt * P:(tt + 1) * P], obuf[:, tt, :], K.ident[:, :])
        mm.then_inc(bk.full_sem(st), 1)

    def act_tile(act, L, st):
        _, _, name, i = st
        b = ps(st)
        if name == "glu":
            if i >= 2:
                act.wait_ge(K.y_done, K.y_base[1] + 8 + i - 1)
            act.wait_ge(*bk.filled(st))
            nc.scalar.activation(sig[:, i % 2, :], b, ACT.Sigmoid, bias=b_glu[:, i:i + 1]).then_inc(bk.free_sem(st), 1)
            return
        if name == "us" and i >= 2:
            act.wait_ge(s_u[(i - 2) % 4], 16 * S_CG * ((i - 2) // 4 + 1))
        if name in ("qd", "kd") and i >= 1:
            act.wait_ge(s_rope, i)
        if name == "vd" and i >= 2:
            act.wait_ge(*bk.filled(("at_v", at["d", i - 2, TT - 1])))
        if name == "qx":
            prev = at["d", DF_H - 2 + i, TT - 1] if i < 2 else at["x", i - 2, TT - 1]
            act.wait_ge(*bk.filled(("at_s", prev), 1 if i < 2 else 0))
        if name == "gd" and i == 0:
            act.wait_ge(*bk.filled(mt[-1]))
        if name == "gs" and i == 0:
            act.wait_ge(*bk.filled(("sp_d", S_C - 1)))
        act.wait_ge(*bk.filled(st))
        if name == "us":
            ins = nc.scalar.activation(us[:, i % 2, :].rearrange("p (j b) -> p j b", b=S_B),
                                       b.rearrange("p (b j) -> p j b", j=S_L), ACT.Copy)
        elif name == "mk":
            ins = nc.scalar.activation(mk[:, i, :], b[:, 0:MEM], ACT.Copy)
        elif name == "mv":
            ins = nc.scalar.activation(mv[:, :, i * P:(i + 1) * P], b[:, 0:MEM].rearrange("p (t c) -> p t c", c=P), ACT.Copy)
        elif name == "gd":
            ins = nc.scalar.activation(yT[:, 8 + i, :], b, ACT.Silu)
        elif name == "gx":
            ins = nc.scalar.activation(yT[:, 12 + i, :], b, ACT.Silu)
        elif name == "gs":
            ins = nc.scalar.activation(yT[:, i, :], b, ACT.Silu)
        elif name == "qd":
            ins = nc.scalar.activation(raw[:, 0, :], b, ACT.Copy, scale=DF_D ** -0.5)
        elif name == "kd":
            ins = nc.scalar.activation(raw[:, 1, :], b, ACT.Copy)
        elif name == "vd":
            ins = nc.scalar.activation(v[:, i % 2, :, :], b.rearrange("p (t c) -> p t c", c=P), ACT.Copy)
        elif name == "qx":
            ins = nc.scalar.activation(qr[:, i % 2, :], b, ACT.Copy)
        ins.then_inc(bk.free_sem(st), 1)

    def act_ss_par(act, L, st):
        act.wait_ge(s_tb, n_tb)
        nc.scalar.activation(tm[0], logdt, ACT.Exp).then_inc(s_sa, 1)
        act.wait_ge(s_sv, 1)
        nc.scalar.activation(tm[1], tm[1], ACT.Exp).then_inc(s_sa, 1)
        nc.scalar.activation(lamp, lamp, ACT.Exp).then_inc(s_sa, 1)
        act.wait_ge(s_sv, 2)
        nc.scalar.activation(tm[4], tm[3], ACT.Sin).then_inc(s_sa, 1)
        nc.scalar.activation(tm[5], tm[3], ACT.Sin, scale=0.5).then_inc(s_sa, 1)

    def act_rope_tab(act, L, st):
        act.wait_ge(s_sv, 3)
        nc.scalar.activation(ropeS, ang, ACT.Sin).then_inc(s_sa, 1)
        nc.scalar.activation(half, ang, ACT.Sin, scale=0.5).then_inc(s_sa, 1)

    def act_sp_b(act, L, st):
        c = st[1]
        for j in range(2):
            act.wait_ge(*bk.filled(st, ("i", j)))
            if c >= 1 and j == 0:
                act.wait_ge(*bk.filled(("sp_c", c - 1), 1))
            nc.scalar.activation(inm[:, 4 * j:4 * j + 4, :].rearrange("p g m -> p (g m)"), ps(st, ("i", j)),
                                 ACT.Copy).then_inc(bk.free_sem(st, ("i", j)), 1)
        for j in range(2):
            act.wait_ge(*bk.filled(st, ("k", j)))
            if j == 0:
                act.wait_ge(s_zst, 16 * S_C)
                if c >= 1:
                    act.wait_ge(s_kst, 16 * c)
            nc.scalar.activation(krow[0:S_H, 4 * j:4 * j + 4, :].rearrange("p g m -> p (g m)"), ps(st, ("k", j))[0:S_H, :],
                                 ACT.Copy).then_inc(bk.free_sem(st, ("k", j)), 1)

    def act_sp_c(act, L, st):
        c = st[1]
        if c == 0:
            for i in range(4):
                act.wait_ge(s_u[i], 32 * S_CG)
        act.wait_ge(*bk.filled(st, 0))
        nc.scalar.activation(vst[:, 0, :, c * S_CG:(c + 1) * S_CG].rearrange("p b g -> p g b"),
                             ps(st, 0).rearrange("p (g b) -> p g b", b=S_B), ACT.Copy).then_inc(bk.free_sem(st, 0), 1)

    def act_sp_d(act, L, st):
        c = st[1]
        if c >= 2:
            act.wait_ge(s_yst[c % 2], 16 * S_L * (c // 2))
        act.wait_ge(*bk.filled(st))
        nc.scalar.activation(ybuf[:, c % 2, :], ps(st), ACT.Copy).then_inc(bk.free_sem(st), 1)

    def act_gelu(act, L, st):
        act.wait_ge(s_yb, 16 * S_C)
        for c in range(S_C):
            nc.scalar.activation(ych[:, c, :], ych[:, c, :], ACT.Gelu_apprx_tanh).then_inc(s_gelu, 1)

    def act_at_s(act, L, st):
        u = st[1]
        kind, h, qb = units[u]
        if kind == "d":
            for c in range(2):
                act.wait_ge(s_score, 2 * u + c + 1)
                x = e4[u % 2][c][:, 0:(qb + 1) * P]
                nc.scalar.activation(x, x, ACT.Exp, bias=mx[:, u % 2, c:c + 1],
                                     accum_out=sums[:, u % 4, c:c + 1]).then_inc(s_exp, 1)
        else:
            act.wait_ge(s_score, 32 + u - 15)
            act.wait_ge(*bk.filled(("at_t", u - 2)))
            nc.scalar.activation(e4[u % 2][0][:, 0:MEM], ps(st)[:, 0:MEM], ACT.Exp, bias=mx[:, u % 2, 0:1],
                                 scale=XA_D ** -0.5, accum_out=sums[:, u % 4, 0:1]).then_inc(s_exp, 1)
            act.wait_ge(s_exp, 32 + u - 15)
            act.sem_inc(bk.free_sem(st), 1)

    def act_at_t(act, L, st):
        u = st[1]
        kind, h, qb = units[u]
        n = (qb + 1) * P if kind == "d" else MEM
        if u >= 2:
            act.wait_ge(*bk.filled(("at_v", u - 2)))
        act.wait_ge(*bk.filled(st))
        nc.scalar.activation(pT[:, u % 2, 0:n], ps(st)[:, 0:n], ACT.Copy).then_inc(bk.free_sem(st), 1)

    def act_at_o(act, L, st):
        i = st[1] // TT
        if i < DF_H:
            act.wait_ge(s_oss, i + 1)
            nc.scalar.activation(oss, oss, ACT.Sqrt, scale=1.0 / DF_V, bias=K.eps[:, 0:1]).then_inc(s_ort, 1)

    def act_wo(act, L, st):
        n = st[2]
        for tt in range(TT):
            act.wait_ge(*bk.filled(st, tt))
            nc.scalar.activation(mix[:, tt, n * NC:(n + 1) * NC], ps(st, tt), ACT.Copy).then_inc(bk.free_sem(st, tt), 1)

    def act_final(act, L, st):
        tt = st[2]
        act.wait_ge(*bk.released(("wo", 1, 3), tt))
        K.act_rstd(act, L, st, mix[:, tt, :], junk)
        act.wait_ge(K.s_ss, K.norms[st] + 1)

    def reduce_angle(vec, L, x, turns):
        L(nc.vector.tensor_scalar(turns, x, 1.0 / (2.0 * math.pi), MAGIC, ALU.mult, ALU.add))
        L.settle()
        L(nc.vector.tensor_scalar(turns, turns, MAGIC, None, ALU.subtract))
        L.settle()
        for part in TWO_PI:
            L(nc.vector.scalar_tensor_tensor(x, turns, -part, x, ALU.mult, ALU.add))
            L.settle()
        L(nc.vector.tensor_scalar(x, x, PI_DOWN, -PI_DOWN, ALU.min, ALU.max))
        L.settle()

    def vec_ss_par(vec, L, st):
        def op(fn, *a_):
            L(fn(*a_))
            L.settle()
        tt_ = nc.vector.tensor_tensor
        vec.wait_ge(s_par, K.par_count[1])
        vec.wait_ge(*bk.filled(st))
        lr, li = tm[6], tm[7]
        L(nc.vector.tensor_copy(lr, ps(st)[:, 0:S_G]))
        L(nc.vector.tensor_copy(li, ps(st)[:, S_G:2 * S_G]))
        L.settle()
        vec.sem_inc(bk.free_sem(st), 1)
        for j in range(2):
            L(nc.vector.tensor_tensor_reduce(lqk_j, lqk[:, 2 * j, :], lqk[:, 2 * j + 1, :], 1.0, 0.0, ALU.mult, ALU.add,
                                             lamp[:, j:j + 1]))
            L.settle()
        vec.wait_ge(s_sa, 1)
        op(tt_, tm[3], li, tm[0], ALU.mult)
        nc.vector.tensor_tensor(tm[1], lr, tm[0], ALU.mult).then_inc(s_sv, 1)
        reduce_angle(vec, L, tm[3], tm[8])
        vec.sem_inc(s_sv, 1)
        vec.wait_ge(s_sa, 5)
        op(tt_, nlam, lamp[:, 1:2], lamp[:, 0:1], ALU.subtract)
        op(nc.vector.tensor_scalar, nlam, nlam, LAMBDA_INIT, None, ALU.subtract)
        op(nc.vector.tensor_scalar, subln, subln, 1.0 - LAMBDA_INIT, None, ALU.mult)
        ar, ai, mag = tm[9], tm[10], tm[1]
        op(tt_, tm[5], tm[5], tm[5], ALU.mult)
        op(nc.vector.tensor_scalar, tm[5], tm[5], -2.0, 1.0, ALU.mult, ALU.add)
        op(tt_, ar, mag, tm[5], ALU.mult)
        op(tt_, ai, mag, tm[4], ALU.mult)
        nr, den, x = tm[11], tm[12], tm[13]
        op(nc.vector.tensor_scalar, nr, ar, 1.0, None, ALU.subtract)
        op(tt_, den, lr, lr, ALU.mult)
        op(tt_, x, li, li, ALU.mult)
        op(tt_, den, den, x, ALU.add)
        op(nc.vector.reciprocal, den, den)
        op(tt_, z_re, nr, lr, ALU.mult)
        op(tt_, x, ai, li, ALU.mult)
        op(tt_, z_re, z_re, x, ALU.add)
        op(tt_, z_re, z_re, den, ALU.mult)
        op(tt_, z_im, ai, lr, ALU.mult)
        op(tt_, x, nr, li, ALU.mult)
        op(tt_, z_im, z_im, x, ALU.subtract)
        op(tt_, z_im, z_im, den, ALU.mult)
        op(nc.vector.tensor_scalar, z_im, z_im, sgn[:, 0:1], None, ALU.mult)
        op(nc.vector.memset, pc_re[:, :, 0], 1.0)
        op(nc.vector.memset, pc_im[:, :, 0], 0.0)
        for k in range(1, S_L + 1):
            pr, pi, nr_, ni_ = pc_re[:, :, k - 1], pc_im[:, :, k - 1], pc_re[:, :, k], pc_im[:, :, k]
            op(tt_, nr_, pr, ar, ALU.mult)
            op(tt_, x, pi, ai, ALU.mult)
            op(tt_, nr_, nr_, x, ALU.subtract)
            op(tt_, ni_, pr, ai, ALU.mult)
            op(tt_, x, pi, ar, ALU.mult)
            op(tt_, ni_, ni_, x, ALU.add)
        op(nc.vector.tensor_copy, l_re, pc_re[:, :, S_L])
        op(nc.vector.tensor_scalar, l_im[:, 0, :], pc_im[:, :, S_L], sgn[:, 0:1], None, ALU.mult)
        op(nc.vector.tensor_scalar, l_im[:, 1, :], pc_im[:, :, S_L], sgn[:, 1:2], None, ALU.mult)
        for j in range(S_L):
            op(nc.vector.tensor_copy, pb_re[:, :, j], pc_re[:, :, S_L - 1 - j])
            op(nc.vector.tensor_scalar, pb_im[:, :, j], pc_im[:, :, S_L - 1 - j], sgn[:, 0:1], None, ALU.mult)
        op(nc.vector.tensor_scalar, pc_re, pc_re, sgn[:, 1:2], None, ALU.mult)
        op(nc.vector.tensor_scalar, pc_im, pc_im, -1.0, None, ALU.mult)
        vec.sem_inc(s_pow, 1)

    def vec_rope_tab(vec, L, st):
        vec.wait_ge(s_tab, 48)
        L(nc.vector.tensor_copy(ang, pos_i))
        L.settle()
        L(nc.vector.tensor_scalar(ang, ang, invf[:, 0:1], None, ALU.mult))
        L.settle()
        reduce_angle(vec, L, ang, kk_)
        vec.sem_inc(s_sv, 1)
        vec.wait_ge(s_sa, 7)
        L(nc.vector.tensor_tensor(half, half, half, ALU.mult))
        L.settle()
        L(nc.vector.tensor_scalar(ropeC, half, -2.0, 1.0, ALU.mult, ALU.add))
        L.settle()

    def vec_sp_a(vec, L, st):
        c = st[1]
        g = slice(c * S_CG, (c + 1) * S_CG)
        i = c % 2
        gh = lambda ap: ap[:, g].unsqueeze(2).to_broadcast([P, S_CG, S_H])
        b1, b2 = (braw[:, 2 * i + j, :].rearrange("p (g h) -> p g h", h=S_H) for j in range(2))
        t2 = tmp.rearrange("p a b -> p (a b)")
        x = t2[:, 0:S_CG * S_H].rearrange("p (g h) -> p g h", h=S_H)
        x2 = t2[:, S_CG * S_H:2 * S_CG * S_H].rearrange("p (g h) -> p g h", h=S_H)
        tt_ = nc.vector.tensor_tensor
        vec.wait_ge(s_bc[i], 16 * 7 * (c // 2 + 1))
        if c >= 1:
            vec.wait_ge(*bk.filled(("sp_b", c - 1), ("k", 1)))
        L(tt_(bst, b1, gh(z_re), ALU.mult))
        L(tt_(x, b2, gh(z_im), ALU.mult))
        L(tt_(bsw, b2, gh(z_re), ALU.mult))
        L(tt_(x2, b1, gh(z_im), ALU.mult))
        L.settle()
        L(tt_(bst, bst, x, ALU.add))
        L(tt_(bsw, bsw, x2, ALU.subtract))
        L.settle()
        four = [P, S_CG, S_L, S_H]
        ba4 = ba.rearrange("p (g j) h -> p g j h", j=S_L)
        x4 = t2[:, 0:S_CG * S_L * S_H].rearrange("p (g j h) -> p g j h", j=S_L, h=S_H)
        L(tt_(ba4, pb_re[:, g, :].unsqueeze(3).to_broadcast(four), bst[:, :, :].unsqueeze(2).to_broadcast(four), ALU.mult))
        L(tt_(x4, pb_im[:, g, :].unsqueeze(3).to_broadcast(four), bsw[:, :, :].unsqueeze(2).to_broadcast(four), ALU.mult))
        L.settle()
        nc.vector.tensor_tensor(ba4, ba4, x4, ALU.add).then_inc(s_ba, 1)
        vec.wait_ge(s_ba, c + 1)
        four = [P, S_CG, S_L + 1, S_H]
        ca4 = ca.rearrange("p g (j h) -> p g j h", h=S_H)
        x4 = t2[:, 0:S_CG * (S_L + 1) * S_H].rearrange("p (g j h) -> p g j h", j=S_L + 1, h=S_H)
        cs, cw_ = (ps(("sp_a", c), "c")[:, j * P:(j + 1) * P].rearrange("p (g h) -> p g h", h=S_H) for j in range(2))
        vec.wait_ge(*bk.filled(st, "c"))
        if c >= 1:
            vec.wait_ge(s_cst, 16 * c)
        L(tt_(ca4, pc_re[:, g, :].unsqueeze(3).to_broadcast(four), cs.unsqueeze(2).to_broadcast(four), ALU.mult))
        nc.vector.tensor_tensor(x4, pc_im[:, g, :].unsqueeze(3).to_broadcast(four), cw_.unsqueeze(2).to_broadcast(four),
                                ALU.mult).then_inc(bk.free_sem(st, "c"), 1)
        vec.wait_ge(*bk.released(st, "c"))
        L.settle()
        nc.vector.tensor_tensor(ca4, ca4, x4, ALU.add).then_inc(s_ca, 1)
        vec.wait_ge(s_ca, c + 1)

    def vec_sp_b(vec, L, st):
        c = st[1]
        g = slice(c * S_CG, (c + 1) * S_CG)
        x = tmp.rearrange("p a b -> p (a b)")[0:S_H, 0:S_CG * S_H].rearrange("p (g h) -> p g h", h=S_H)
        three = [S_H, S_CG, S_H]
        L(nc.vector.tensor_tensor(x, d_skip[0:S_H, g].unsqueeze(2).to_broadcast(three),
                                  K.ident[0:S_H, 0:S_H].unsqueeze(1).to_broadcast(three), ALU.mult))
        L.settle()
        for j in range(2):
            vec.wait_ge(*bk.released(st, ("k", j)))
        k0 = krow[0:S_H, :, 0:S_H]
        nc.vector.tensor_tensor(k0, k0, x, ALU.add).then_inc(s_kr, 1)
        vec.wait_ge(s_kr, c + 1)

    def vec_sp_c(vec, L, st):
        c = st[1]
        if c == 0:
            for i in range(4):
                vec.wait_ge(s_u[i], 32 * S_CG)
        vec.wait_ge(*bk.filled(st, 1))
        nc.vector.tensor_copy(vst[:, 1, :, c * S_CG:(c + 1) * S_CG].rearrange("p b g -> p g b"),
                              ps(st, 1).rearrange("p (g b) -> p g b", b=S_B)).then_inc(bk.free_sem(st, 1), 1)

    def vec_scan(vec, L, st):
        vec.wait_ge(*bk.released(("sp_c", S_C - 1), 0))
        vec.wait_ge(*bk.released(("sp_c", S_C - 1), 1))
        t1, t2 = scan_t[:, 0:2, :], scan_t[:, 2:4, :]
        lre2 = l_re.unsqueeze(1).to_broadcast([P, 2, S_G])
        with vec.Fori(0, S_B - 1) as b:
            x0 = vst[:, :, bass.ds(b, 1), :].rearrange("p s o g -> p s (o g)")
            x1 = vst[:, :, bass.ds(b + 1, 1), :].rearrange("p s o g -> p s (o g)")
            nc.vector.tensor_tensor(t1, x0, lre2, ALU.mult).then_inc(s_scan, 1)
            nc.vector.tensor_tensor(t2[:, 0, :], x0[:, 1, :], l_im[:, 0, :], ALU.mult).then_inc(s_scan, 1)
            nc.vector.tensor_tensor(t2[:, 1, :], x0[:, 0, :], l_im[:, 1, :], ALU.mult).then_inc(s_scan, 1)
            vec.wait_ge(s_scan, b * 5 + 3)
            nc.vector.tensor_tensor(t1, t1, t2, ALU.add).then_inc(s_scan, 1)
            vec.wait_ge(s_scan, b * 5 + 4)
            nc.vector.tensor_tensor(x1, x1, t1, ALU.add).then_inc(s_scan, 1)
            vec.wait_ge(s_scan, b * 5 + 5)
        vec.sem_inc(s_scand, 1)

    def vec_rope(vec, L, st):
        h = st[1]
        for j, dst in enumerate((qr, kr)):
            vec.wait_ge(*bk.filled(st, j))
            if h >= 2 and j == 0:
                vec.wait_ge(*bk.filled(("at_s", at["d", h - 2, TT - 1]), 1))
            o, x = dst[:, h % 2, :], rope_t[:, j, :]
            L(nc.vector.tensor_tensor(o, raw[:, j, :], ropeC[:, :], ALU.mult))
            nc.vector.tensor_tensor(x, ps(st, j), ropeS[:, :], ALU.mult).then_inc(bk.free_sem(st, j), 1)
            vec.wait_ge(*bk.released(st, j))
            L.settle()
            L(nc.vector.tensor_tensor(o, o, x, ALU.add))
        L.settle()
        vec.sem_inc(s_rope, 1)

    def vec_tile(vec, L, st):
        _, _, name, i = st
        if name == "glu":
            vec.wait_ge(*bk.released(st))
            s_ = sig[:, i % 2, :]
            L(nc.vector.tensor_tensor(s_, ych[:, i, :], s_, ALU.mult))
            L.settle()
            y = yT[:, i, :].rearrange("p (b j) -> p j b", j=S_L)
            nc.vector.tensor_tensor(y, y, s_.rearrange("p (j b) -> p j b", b=S_B), ALU.mult).then_inc(K.y_done, 1)

    def vec_at_s(vec, L, st):
        u = st[1]
        kind, h, qb = units[u]
        nk = (qb + 1) * P
        if kind == "d":
            if u >= 2:
                vec.wait_ge(*bk.filled(("at_t", u - 2)))
            for c in range(2):
                vec.wait_ge(*bk.filled(st, c))
                m = mx[:, u % 2, c:c + 1]
                nc.vector.tensor_tensor_reduce(e4[u % 2][c][:, 0:nk], ps(st, c)[:, 0:nk], tri[:, SEQ - nk:SEQ], 1.0, -3e38,
                                               ALU.add, ALU.max, m).then_inc(bk.free_sem(st, c), 1)
                vec.wait_ge(*bk.released(st, c))
                nc.vector.tensor_scalar(m, m, -1.0, None, ALU.mult).then_inc(s_score, 1)
        else:
            m = mx[:, u % 2, 0:1]
            vec.wait_ge(s_exp, 32 + u - 17 if u >= 18 else 2 * (u - 1))
            vec.wait_ge(*bk.filled(st))
            nc.vector.tensor_reduce(m, ps(st)[:, 0:MEM], AX.X, ALU.max).then_inc(bk.free_sem(st), 1)
            vec.wait_ge(*bk.read_once(st))
            nc.vector.tensor_scalar(m, m, -XA_D ** -0.5, None, ALU.mult).then_inc(s_score, 1)

    def vec_at_t(vec, L, st):
        u = st[1]
        kind, h, qb = units[u]
        if kind != "d":
            return
        nk = (qb + 1) * P
        vec.wait_ge(s_exp, 2 * u + 2)
        r = rs[:, u % 2, :]
        L(nc.vector.reciprocal(r, sums[:, u % 4, :]))
        L.settle()
        L(nc.vector.tensor_tensor(r[:, 1:2], r[:, 1:2], nlam, ALU.mult))
        e0, e1 = (e4[u % 2][c][:, 0:nk] for c in range(2))
        L(nc.vector.tensor_scalar(e0, e0, r[:, 0:1], None, ALU.mult))
        L.settle()
        nc.vector.scalar_tensor_tensor(e0, e1, r[:, 1:2], e0, ALU.mult, ALU.add).then_inc(s_w, 1)

    def vec_at_v(vec, L, st):
        u = st[1]
        kind, h, qb = units[u]
        if qb == 0 and u >= TT:
            vec.wait_ge(*bk.filled(("at_o", u - 1)))
        vec.wait_ge(*bk.filled(st))
        if kind == "d":
            nc.vector.tensor_copy(obuf[:, qb, :], ps(st)[:, 0:P]).then_inc(bk.free_sem(st), 1)
        else:
            r = rs[:, u % 2, 0:1]
            vec.wait_ge(s_exp, 32 + u - 15)
            L(nc.vector.reciprocal(r, sums[:, u % 4, 0:1]))
            L.settle()
            nc.vector.tensor_scalar(obuf[:, qb, :], ps(st)[:, 0:P], r, None, ALU.mult).then_inc(bk.free_sem(st), 1)
        vec.wait_ge(*bk.released(st))

    def vec_at_o(vec, L, st):
        u = st[1]
        i = u // TT
        if i < DF_H:
            for tt in range(TT):
                L(nc.vector.tensor_tensor_reduce(rope_t[:, 0, 0:P], obuf[:, tt, :], obuf[:, tt, :], 1.0, 0.0, ALU.mult, ALU.add,
                                                 oss[:, tt:tt + 1]))
                L.settle()
            vec.sem_inc(s_oss, 1)
            vec.wait_ge(s_ort, i + 1)
            L(nc.vector.reciprocal(oss, oss))
            L.settle()
            L(nc.vector.tensor_tensor(obuf, obuf, oss.unsqueeze(2).to_broadcast([P, TT, P]), ALU.mult))
            L.settle()
        vec.sem_inc(s_on, 1)
        vec.wait_ge(*bk.filled(st))
        y = yT[:, 8 + i, :]
        gate = ("tile", 1, "gd", i) if i < DF_H else ("tile", 1, "gx", i - DF_H)
        vec.wait_ge(*bk.released(gate))
        if i < DF_H:
            nc.vector.scalar_tensor_tensor(y, ps(st), subln[:, 0:1], y, ALU.mult, ALU.mult).then_inc(bk.free_sem(st), 1)
        else:
            nc.vector.tensor_tensor(y, ps(st), y, ALU.mult).then_inc(bk.free_sem(st), 1)
        vec.wait_ge(*bk.released(st))
        vec.sem_inc(K.y_done, 1)

    def vec_final(vec, L, st):
        tt = st[2]
        m = mix[:, tt, :]
        K.vec_rstd(vec, L, st)
        if tt == 0:
            vec.wait_ge(s_fg, 16)
            vec.wait_ge(s_back, 16 * TT)
        L(nc.vector.scalar_tensor_tensor(m, m, K.rstd[:, tt:tt + 1], gain_post, ALU.mult, ALU.mult))
        L.settle()
        nc.vector.tensor_tensor(X[:, tt, :], X[:, tt, :], m, ALU.add).then_inc(K.x_done, 1)

    K.y_base[1] = K.y_count
    K.y_count += KT
    K.mix_parts[1] = (K.A_parts.rearrange("p (k t) -> p k t", t=SEQ), K.B_parts.rearrange("p (k t) -> p k t", t=SEQ))
    K.wo_src[1] = (T["w_out"][0], yT)
    K.params.append(pool_params)
    K.wait_gain[1] = K.wait_gain["mem"] = lambda vec: vec.wait_ge(s_par, K.par_count[1])
    K.tiles[glu[0]]["wait"] = lambda pe: pe.wait_ge(s_gelu, S_C)
    K.stage("pool", b1_tables=pool_tables, rope_tab=pool_rope_tab, tile1=pool_tile, sp_a=pool_sp_a, sp_b=pool_sp_b,
            scan=pool_scan, sp_d=pool_sp_d, y_back=pool_y_back, wo1=pool_wo)
    K.stage("pe", ss_par=pe_ss_par, sp_a=pe_sp_a, sp_b=pe_sp_b, sp_c=pe_sp_c, sp_d=pe_sp_d, rope=pe_rope,
            at_s=pe_at_s, at_t=pe_at_t, at_v=pe_at_v, at_o=pe_at_o)
    K.stage("act", tile1=act_tile, ss_par=act_ss_par, rope_tab=act_rope_tab, sp_b=act_sp_b, sp_c=act_sp_c, sp_d=act_sp_d,
            gelu=act_gelu, at_s=act_at_s, at_t=act_at_t, at_o=act_at_o, wo1=act_wo, final1=act_final)
    K.stage("vec", tile1=vec_tile, ss_par=vec_ss_par, rope_tab=vec_rope_tab, sp_a=vec_sp_a, sp_b=vec_sp_b, sp_c=vec_sp_c,
            scan=vec_scan, rope=vec_rope, at_s=vec_at_s, at_t=vec_at_t, at_v=vec_at_v, at_o=vec_at_o, final1=vec_final)
    return script


C2_CONV = 1024
C2_DK = 512
C2_V = 1024
GLA_H = 4
GLA_K = C2_DK // GLA_H
GLA_VD = C2_V // GLA_H
GLA_CH = 64
GLA_NC = SEQ // GLA_CH
GLA_TAU = 16.0


def block2(K):
    nc, T, ps, bk = K.nc, K.T, K.ps, K.bk
    yT, X = K.A_kt, K.X
    h_hi = K.B_parts.rearrange("p (k t) -> p k t", t=SEQ)
    h_lo = K.X_parts.rearrange("p t (k c) -> p t k c", c=P)
    x_keep = nc.dram_tensor("x_keep_2", (SEQ, D), F32).ap()
    s_keep = [K.sem(f"x_rows{tt}_kept_2") for tt in range(TT)]
    s_back = K.sem("x_back_2")
    K.norm_parts[2] = (h_hi, h_lo)
    K.norm_parts_wait[2] = lambda vec, tt: vec.wait_ge(s_keep[tt], 16)
    a = K.arena()
    v = a("b2_v", 2, TT, GLA_VD)
    r = a("b2_r", 2, 2, NC)
    ab = a("b2_ab", NC)
    gd = a("b2_gd", NC)
    q = a("b2_q", 2, NC)
    k = a("b2_k", 2, NC)
    mn = a("b2_mn", NC)
    bcum = a("b2_bcum", NC)
    dec = a("b2_dec", GLA_NC)
    kd = a("b2_kd", NC)
    kn = a("b2_kn", TT, P)
    state = a("b2_state", GLA_NC, GLA_VD)
    sq = a("b2_sq", 2, NC)
    rs = a("b2_rs", NC)
    w_up = a("w_up", C2_DK)
    assert a.at[0] <= WORK - (ADA_SLOTS + 1) * ADA_W
    a = K.arena()
    tmp_h = a("b2_ch", 2, NC)
    tmp_u = a("b2_u", 2, NC + 2)
    tmp_y = a("b2_y", 2, NC)
    tmp_z = a("b2_z", 2, NC)
    fg = K.work[:, 2 * D:3 * D]
    prm = K.keep(16 + 24 + 8 + 4 + 8)
    norm_g, conv_w, conv_b = prm[:, 0:16], prm[:, 16:40], prm[:, 40:48]
    b_gate, gla_g = prm[:, 48:52], prm[:, 52:60]
    K.norm_gain[2] = (norm_g, None)

    col, c0 = {}, 0
    for n, w in (("ch", 1024), ("cb", 1024), ("cc", 1024), ("cz", 1024),
                 ("gq", 512), ("gk", 512), ("gv", 1024), ("gr", 1024), ("gd", 16)):
        col[n] = c0
        c0 += w

    def tile(name, i, mode="T", w=P):
        st = ("tile", 2, name, i)
        K.tile(st, [(T["w_in_2"][0], col[name] + i * w, w)], mode, w, h_hi, SEQ, lo=h_lo)
        return st

    script = [("norm", 2, tt) for tt in range(TT)]
    script.append(tile("gd", 0, w=16))
    K.after_norm(script[-1], 2)
    heads = []
    for h in range(GLA_H):
        heads.append([tile("gk", h), tile("gq", h), tile("gv", h, "N", GLA_VD),
                      tile("gr", 2 * h), tile("gr", 2 * h + 1)])
    convs = [[tile(n, i) for n in ("ch", "cc", "cb", "cz")] for i in range(8)]
    for h in range(GLA_H):
        t = heads[h]
        script += [t[0], ("gla_gate", h), t[1], ("gla_kt", h), t[2], ("gla_u", h), t[3], ("gla_o", h), t[4],
                   ("gla_ss", h)]
    for c in convs:
        script += c
    script += [("wo", 2, n) for n in range(4)]
    script += [("final", 2, tt) for tt in range(TT)]
    for st in script:
        if st[0] == "gla_gate":
            K.uses[st] = [("x", "S", 2)]
        elif st[0] == "gla_kt":
            K.uses[st] = [("t", "S", 1)]
        elif st[0] == "gla_u":
            K.uses[st] = [((half, par), "S", 1) for half in range(2) for par in range(2)]
        elif st[0] == "gla_o":
            K.uses[st] = [(0, "S", 2), (1, "S", 2)]
        elif st[0] == "gla_ss":
            K.uses[st] = [("s", "S", 1)]

    s_par = K.sem("b2_params")
    s_fg = K.sem("final_gain_2_loaded")
    s_up = K.sem("gate_weights_loaded")
    s_kd = K.sem("gla_kd_ready")
    s_state = K.sem("gla_state_ready")
    s_sq = K.sem("gla_squares_ready")
    s_act = K.sem("gla_act_ready")
    s_vec = K.sem("gla_vec_ready")
    s_conv = K.sem("conv_vec_done")

    def pool_params(pool):
        n = 0
        with nc.allow_non_contiguous_dma(reason="small per-channel parameters"):
            for dst, src in ((norm_g, T["norm_g_2"].rearrange("o (k p) -> p (o k)", p=P)),
                             (conv_b, T["conv_b_2"].rearrange("o (k p) -> p (o k)", p=P)),
                             (b_gate, T["gla_b_gate_2"].rearrange("o (k p) -> p (o k)", p=P)),
                             (gla_g, T["gla_norm_g_2"].rearrange("o h (j p) -> p (o h j)", p=P)),
                             (conv_w[:, 0:8], T["conv_w_2"][0, 0:1].rearrange("o (k p) -> p (o k)", p=P)),
                             (conv_w[:, 8:16], T["conv_w_2"][0, 1:2].rearrange("o (k p) -> p (o k)", p=P)),
                             (conv_w[:, 16:24], T["conv_w_2"][0, 2:3].rearrange("o (k p) -> p (o k)", p=P))):
                pool.dma_start(dst, src).then_inc(s_par, 16)
                n += 16
        K.par_count[2] = n

    def pool_norm(pool, st):
        _, _, tt = st
        g = K.blocks.index(2)
        if tt == 0:
            if g > 0:
                pool.wait_ge(K.y_done, K.y_base[1] + KT)
            pool.dma_start(w_up[0:16, :], T["gla_w_up_2"][0]).then_inc(s_up, 16)
        if g == 0:
            pool.wait_ge(K.s_x[tt], 16)
        else:
            pool.wait_ge(K.x_done, (g - 1) * TT + tt + 1)
        pool.dma_start(x_keep[tt * P:(tt + 1) * P, :], X[:, tt, :]).then_inc(s_keep[tt], 16)

    def pool_wo(pool, st):
        if st[2] == 0:
            pool.wait_ge(K.y_done, K.y_base[2] + KT)
            for tt in range(TT):
                pool.dma_start(X[:, tt, :], x_keep[tt * P:(tt + 1) * P, :]).then_inc(s_back, 16)
            pool.dma_start(fg, T["final_g_2"].partition_broadcast(P)).then_inc(s_fg, 16)

    def pe_gate(pe, st):
        h = st[1]
        pe.wait_ge(*bk.released(("tile", 2, "gd", 0)))
        if h == 0:
            pe.wait_ge(s_up, 16)
        bk.take(pe, st, "x")
        nc.tensor.matmul(ps(st, "x"), lhsT=w_up[0:16, h * P:(h + 1) * P], rhs=gd[0:16, :], start=True,
                         stop=True).then_inc(bk.full_sem(st, "x"), 1)

    def pe_kt(pe, st):
        h = st[1]
        pe.wait_ge(s_kd, h + 1)
        bk.take(pe, st, "t")
        for tt in range(TT):
            mm = nc.tensor.transpose(ps(st, "t")[:, tt * P:(tt + 1) * P], kd[:, tt * P:(tt + 1) * P], K.ident[:, :])
        mm.then_inc(bk.full_sem(st, "t"), 1)

    def pe_u(pe, st):
        h = st[1]
        pe.wait_ge(*bk.released(("gla_kt", h), "t"))
        for half in range(2):
            pe.wait_ge(*bk.released(("tile", 2, "gv", h), half))
        for half in range(2):
            for par in range(2):
                bk.take(pe, st, (half, par))
                for j in range(2):
                    tt = 2 * half + j
                    rows = slice(par * GLA_CH, (par + 1) * GLA_CH)
                    mm = nc.tensor.matmul(ps(st, (half, par))[:, j * GLA_VD:(j + 1) * GLA_VD], lhsT=kn[rows, tt, :],
                                          rhs=v[rows, h % 2, tt, :], start=True, stop=True)
                mm.then_inc(bk.full_sem(st, (half, par)), 1)

    def pe_o(pe, st):
        h = st[1]
        pe.wait_ge(s_state, h + 1)
        pe.wait_ge(*bk.released(("tile", 2, "gq", h)))
        for vt in range(2):
            bk.take(pe, st, vt)
            for c in range(GLA_NC):
                mm = nc.tensor.matmul(ps(st, vt)[:, c * GLA_CH:(c + 1) * GLA_CH],
                                      lhsT=state[:, c, vt * P:(vt + 1) * P],
                                      rhs=q[:, h % 2, c * GLA_CH:(c + 1) * GLA_CH], start=True, stop=True)
            mm.then_inc(bk.full_sem(st, vt), 1)

    def pe_ss(pe, st):
        h = st[1]
        pe.wait_ge(s_sq, 2 * h + 2)
        bk.take(pe, st, "s")
        for vt in range(2):
            mm = nc.tensor.matmul(ps(st, "s"), lhsT=K.ones[:, :], rhs=sq[:, vt, :], start=(vt == 0), stop=(vt == 1))
        mm.then_inc(bk.full_sem(st, "s"), 1)

    def act_tile(act, L, st):
        _, _, name, i = st
        b = ps(st)
        if name in ("gd", "gq", "gk", "gv", "gr", "ch", "cz"):
            act.wait_ge(*bk.filled(st))
        if name == "gd":
            ins = nc.scalar.activation(gd[0:16, :], b[0:16, :], ACT.Copy)
        elif name == "gq":
            if i >= 2:
                act.wait_ge(*bk.filled(("gla_o", i - 2), 1))
            ins = nc.scalar.activation(q[:, i % 2, :], b, ACT.Copy, scale=GLA_K ** -0.5)
        elif name == "gk":
            if i >= 2:
                act.wait_ge(s_kd, i - 1)
            ins = nc.scalar.activation(k[:, i % 2, :], b, ACT.Copy)
        elif name == "gv":
            if i >= 2:
                act.wait_ge(*bk.filled(("gla_u", i - 2), (1, 1)))
            for half in range(2):
                act.wait_ge(*bk.filled(st, half))
                nc.scalar.activation(v[:, i % 2, 2 * half:2 * half + 2, :], ps(st, half).rearrange("p (t n) -> p t n", n=GLA_VD),
                                     ACT.Copy).then_inc(bk.free_sem(st, half), 1)
            return
        elif name == "gr":
            h, j = i // 2, i % 2
            if h >= 2:
                act.wait_ge(K.y_done, K.y_base[2] + 2 * (h - 2) + 2)
            ins = nc.scalar.activation(r[:, h % 2, j, :], b, ACT.Silu)
        elif name == "ch":
            if i >= 2:
                act.wait_ge(s_conv, 2 * (i - 2) + 1)
            else:
                act.wait_ge(K.y_done, K.y_base[2] + 8)
            ins = nc.scalar.activation(tmp_h[:, i % 2, :], b, ACT.Copy)
        elif name == "cz":
            if i >= 2:
                act.wait_ge(s_conv, 2 * (i - 2) + 2)
            ins = nc.scalar.activation(tmp_z[:, i % 2, :], b, ACT.Silu)
        else:
            return
        ins.then_inc(bk.free_sem(st), 1)

    def act_gate(act, L, st):
        h = st[1]
        if h == 0:
            act.wait_ge(s_par, K.par_count[2])
        act.wait_ge(*bk.filled(st, "x"))
        nc.scalar.activation(ab[:, :], ps(st, "x"), ACT.Abs, bias=b_gate[:, h:h + 1]).then_inc(bk.free_sem(st, "x"), 1)
        act.wait_ge(*bk.read_once(st, "x"))
        L(nc.scalar.activation(ab[:, :], ab[:, :], ACT.Exp, scale=-1.0))
        L.settle()
        nc.scalar.activation(ab[:, :], ab[:, :], ACT.Ln, bias=1.0).then_inc(s_act, 1)
        act.wait_ge(s_vec, h + 1)
        nc.scalar.activation(mn[:, :], mn[:, :], ACT.Exp, scale=1.0 / GLA_TAU).then_inc(s_act, 1)
        nc.scalar.activation(dec[:, :], bcum[:, GLA_CH - 1::GLA_CH], ACT.Exp, scale=1.0 / GLA_TAU).then_inc(s_act, 1)

    def act_kt(act, L, st):
        h = st[1]
        act.wait_ge(*bk.filled(st, "t"))
        if h >= 1:
            act.wait_ge(*bk.filled(("gla_u", h - 1), (1, 1)))
        nc.scalar.activation(kn.rearrange("p t n -> p (t n)"), ps(st, "t"), ACT.Copy).then_inc(bk.free_sem(st, "t"), 1)

    def act_o(act, L, st):
        h = st[1]
        for vt in range(2):
            act.wait_ge(*bk.filled(st, vt))
            if h >= 1 and vt == 0:
                act.wait_ge(*bk.filled(("gla_ss", h - 1), "s"))
                act.wait_ge(K.y_done, K.y_base[2] + 2 * h)
            nc.scalar.activation(sq[:, vt, :], ps(st, vt), ACT.Square).then_inc(s_sq, 1)
            act.wait_ge(s_sq, 2 * h + vt + 1)
            act.sem_inc(bk.free_sem(st, vt), 1)

    def act_ss(act, L, st):
        h = st[1]
        act.wait_ge(*bk.filled(st, "s"))
        if h >= 1:
            act.wait_ge(K.y_done, K.y_base[2] + 2 * h)
        L(nc.scalar.activation(rs[:, :], ps(st, "s"), ACT.Identity, scale=1.0 / GLA_VD, bias=K.eps[:, 0:1]))
        L.settle()
        act.sem_inc(bk.free_sem(st, "s"), 1)
        nc.scalar.activation(rs[:, :], rs[:, :], ACT.Sqrt).then_inc(s_act, 1)

    def vec_tile(vec, L, st):
        _, _, name, i = st
        b = ps(st)
        if name == "cc":
            vec.wait_ge(*bk.filled(st))
            vec.wait_ge(*bk.released(("tile", 2, "ch", i)))
            if i == 0:
                L(nc.vector.memset(tmp_u[:, :, 0:2], 0.0))
                vec.wait_ge(s_par, K.par_count[2])
            u, y = tmp_u[:, i % 2, :], tmp_y[:, i % 2, :]
            nc.vector.tensor_tensor(u[:, 2:NC + 2], b, tmp_h[:, i % 2, :], ALU.mult).then_inc(bk.free_sem(st), 1)
            vec.wait_ge(*bk.released(st))
            L.settle()
            nc.vector.tensor_scalar(y, u[:, 0:NC], conv_w[:, i:i + 1], conv_b[:, i:i + 1], ALU.mult, ALU.add).then_inc(s_conv, 1)
            vec.wait_ge(s_conv, 2 * i + 1)
            for j in (1, 2):
                L(nc.vector.scalar_tensor_tensor(y, u[:, j:NC + j], conv_w[:, 8 * j + i:8 * j + i + 1], y, ALU.mult, ALU.add))
                L.settle()
        elif name == "cb":
            y = tmp_y[:, i % 2, :]
            vec.wait_ge(*bk.filled(st))
            nc.vector.tensor_tensor(y, b, y, ALU.mult).then_inc(bk.free_sem(st), 1)
            vec.wait_ge(*bk.released(st))
        elif name == "cz":
            vec.wait_ge(*bk.released(st))
            y = tmp_y[:, i % 2, :]
            nc.vector.tensor_tensor(yT[:, i, :], y, tmp_z[:, i % 2, :], ALU.mult).then_inc(K.y_done, 1)
            vec.wait_ge(K.y_done, K.y_base[2] + 8 + i + 1)
            vec.sem_inc(s_conv, 1)

    def vec_gate(vec, L, st):
        h = st[1]
        if h == 0:
            vec.wait_ge(s_par, K.par_count[2])
        vec.wait_ge(*bk.read_once(st, "x"))
        L(nc.vector.tensor_scalar(mn[:, :], ps(st, "x"), b_gate[:, h:h + 1], 0.0, ALU.add, ALU.min))
        L.settle()
        vec.sem_inc(bk.free_sem(st, "x"), 1)
        vec.wait_ge(s_act, 4 * h + 1)
        L(nc.vector.tensor_tensor(mn[:, :], mn[:, :], ab[:, :], ALU.subtract))
        L.settle()
        L(nc.vector.tensor_tensor_scan(bcum[:, :], K.reset[:, :], mn[:, :], 0.0, ALU.mult, ALU.add))
        L.settle()
        b3 = bcum.rearrange("p (c l) -> p c l", l=GLA_CH)
        nc.vector.tensor_tensor(mn.rearrange("p (c l) -> p c l", l=GLA_CH),
                                b3[:, :, GLA_CH - 1:GLA_CH].to_broadcast([P, GLA_NC, GLA_CH]), b3,
                                ALU.subtract).then_inc(s_vec, 1)
        vec.wait_ge(s_act, 4 * h + 3)
        vec.wait_ge(*bk.released(("tile", 2, "gk", h)))
        if h >= 1:
            vec.wait_ge(*bk.filled(("gla_kt", h - 1), "t"))
        nc.vector.tensor_tensor(kd[:, :], k[:, h % 2, :], mn[:, :], ALU.mult).then_inc(s_kd, 1)
        vec.wait_ge(s_kd, h + 1)

    def vec_u(vec, L, st):
        h = st[1]
        if h >= 1:
            vec.wait_ge(*bk.filled(("gla_o", h - 1), 1))
        for c in range(GLA_NC):
            tt, par = c // 2, c % 2
            key, j = (tt // 2, par), tt % 2
            u = ps(st, key)[:, j * GLA_VD:(j + 1) * GLA_VD]
            if j == 0:
                vec.wait_ge(*bk.filled(st, key))
            if c == 0:
                L(nc.vector.tensor_copy(state[:, 0, :], u))
            else:
                ins = nc.vector.scalar_tensor_tensor(state[:, c, :], state[:, c - 1, :], dec[:, c:c + 1], u, ALU.mult, ALU.add)
                L(ins)
            L.settle()
            if j == 1:
                vec.sem_inc(bk.free_sem(st, key), 1)
        vec.sem_inc(s_state, 1)

    def vec_ss(vec, L, st):
        h = st[1]
        vec.wait_ge(s_act, 4 * h + 4)
        L(nc.vector.reciprocal(rs[:, :], rs[:, :]))
        L.settle()
        for vt in range(2):
            o = ps(("gla_o", h), vt)
            nc.vector.tensor_tensor(sq[:, vt, :], o, rs[:, :], ALU.mult).then_inc(bk.free_sem(("gla_o", h), vt), 1)
            vec.wait_ge(*bk.released(("gla_o", h), vt))
            vec.wait_ge(*bk.released(("tile", 2, "gr", 2 * h + vt)))
            nc.vector.scalar_tensor_tensor(yT[:, 8 + 2 * h + vt, :], sq[:, vt, :], gla_g[:, 2 * h + vt:2 * h + vt + 1],
                                           r[:, h % 2, vt, :], ALU.mult, ALU.mult).then_inc(K.y_done, 1)

    def vec_wo(vec, L, st):
        n = st[2]
        if n == 0:
            vec.wait_ge(s_back, 16 * TT)
        for tt in range(TT):
            vec.wait_ge(*bk.filled(st, tt))
            xs = X[:, tt, n * NC:(n + 1) * NC]
            nc.vector.tensor_tensor(xs, ps(st, tt), xs, ALU.add).then_inc(bk.free_sem(st, tt), 1)

    def vec_final(vec, L, st):
        tt = st[2]
        K.vec_rstd(vec, L, st)
        vec.wait_ge(s_fg, 16)
        nc.vector.scalar_tensor_tensor(X[:, tt, :], X[:, tt, :], K.rstd[:, tt:tt + 1], fg[:, :], ALU.mult,
                                       ALU.mult).then_inc(K.x_done, 1)

    K.mix_parts[2] = (K.B_parts.rearrange("p (k t) -> p k t", t=SEQ), K.A_parts.rearrange("p (k t) -> p k t", t=SEQ))
    K.y_base[2] = K.y_count
    K.y_count += 16
    K.params.append(pool_params)
    K.stage("pool", norm2=pool_norm, wo2=pool_wo)
    K.wait_gain[2] = lambda vec: vec.wait_ge(s_par, K.par_count[2])
    K.stage("pe", gla_gate=pe_gate, gla_kt=pe_kt, gla_u=pe_u, gla_o=pe_o, gla_ss=pe_ss)
    K.stage("act", tile2=act_tile, gla_gate=act_gate, gla_kt=act_kt, gla_o=act_o, gla_ss=act_ss, final2=K.act_rstd_x)
    K.stage("vec", tile2=vec_tile, gla_gate=vec_gate, gla_u=vec_u, gla_ss=vec_ss, wo2=vec_wo, final2=vec_final)
    K.wo_src[2] = (T["w_out_2"][0], yT)
    return script


M_H, M_HD, M_CH, M_TAPS = 4, 256, 64, 4
M_NC = SEQ // M_CH
M_W = M_H * M_HD
N_H, N_G, N_HD = 16, 4, 64
N_HPG = N_H // N_G
C_LEN, C_STEP, C_HID = 32, 16, 128
N_CMP = (SEQ - C_LEN) // C_STEP + 1
ADA_W = 1024
ADA_SLOTS = 4
ADA_PARTS = 3 * D // ADA_W
ADA_KP = KT


def ada_stages():
    out = []
    for part in range(ADA_PARTS):
        out += [("ada", part, kp) for kp in range(ADA_KP)] + [("ada_sum", part)]
    return out


def modulation(K):
    nc, T, ps, bk = K.nc, K.T, K.ps, K.bk
    cT, sc = K.keep(KT), K.keep(KT)
    b_ada, mod = K.keep(3 * KT), K.keep(3 * KT)
    K.mod = mod
    s_c, s_sc = K.sem("c_loaded"), K.sem("silu_c_ready")
    s_used, s_acc = K.sem("ada_slot_used"), K.sem("ada_part_ready")
    slots = K.work[:, WORK - ADA_SLOTS * ADA_W:].rearrange("p (s c) -> p s c", c=ADA_W)
    acc = K.work[:, WORK - (ADA_SLOTS + 1) * ADA_W:WORK - ADA_SLOTS * ADA_W]
    s_load = [K.sem(f"ada_slot{i}_loaded") for i in range(ADA_SLOTS)]
    K.s_mod = s_mod = K.sem("modulation_ready")

    def pool_params(pool):
        with nc.allow_non_contiguous_dma(reason="small per-channel parameters"):
            pool.dma_start(cT, T["c_3"].rearrange("o (k p) -> p (o k)", p=P)).then_inc(s_c, 16)
            pool.dma_start(b_ada, T["b_ada_3"].rearrange("o (k p) -> p (o k)", p=P)).then_inc(s_c, 16)

    def pool_ada(pool, st):
        _, part, kp = st
        n = ADA_KP * part + kp
        if n == 0 and 1 in K.blocks:
            pool.wait_ge(K.y_done, K.y_base[1] + KT)
        if n >= ADA_SLOTS:
            pool.wait_ge(s_used, n - ADA_SLOTS + 1)
        pool.dma_start(slots[:, n % ADA_SLOTS, :],
                       T["w_ada_3"][0][kp * P:(kp + 1) * P, part * ADA_W:(part + 1) * ADA_W]).then_inc(s_load[n % ADA_SLOTS], 16)

    def act_ada(act, L, st):
        if st[1:] == (0, 0):
            act.wait_ge(s_c, 32)
            nc.scalar.activation(sc, cT, ACT.Silu).then_inc(s_sc, 1)

    def vec_ada(vec, L, st):
        _, part, kp = st
        if (part, kp) == (0, 0):
            vec.wait_ge(s_sc, 1)
        if part >= 1 and kp == 0:
            vec.wait_ge(*bk.filled(("ada_sum", part - 1)))
        n = ADA_KP * part + kp
        w = slots[:, n % ADA_SLOTS, :]
        vec.wait_ge(s_load[n % ADA_SLOTS], 16 * (n // ADA_SLOTS + 1))
        if kp == 0:
            ins = nc.vector.tensor_scalar(acc[:, :], w, sc[:, 0:1], None, ALU.mult)
        else:
            ins = nc.vector.scalar_tensor_tensor(acc[:, :], w, sc[:, kp:kp + 1], acc[:, :], ALU.mult, ALU.add)
        ins.then_inc(s_used, 1)
        vec.wait_ge(s_used, ADA_KP * part + kp + 1)

    def pe_sum(pe, st):
        part = st[1]
        pe.wait_ge(s_used, ADA_KP * (part + 1))
        bk.take(pe, st)
        n = ADA_W // P
        for m in range(n):
            mm = nc.tensor.matmul(ps(st)[:, m:m + 1], lhsT=acc[:, m * P:(m + 1) * P], rhs=K.ones[:, 0:1], start=True, stop=True)
        mm.then_inc(bk.full_sem(st), 1)

    def vec_sum(vec, L, st):
        part, n = st[1], ADA_W // P
        vec.wait_ge(*bk.filled(st))
        if part == 0:
            vec.wait_ge(s_c, 32)
        sl = slice(part * n, (part + 1) * n)
        nc.vector.tensor_tensor(mod[:, sl], ps(st)[:, 0:n], b_ada[:, sl], ALU.add).then_inc(bk.free_sem(st), 1)
        vec.wait_ge(*bk.released(st))

    for st in ada_stages():
        if st[0] == "ada_sum":
            K.uses[st] = [(0, "S", 1)]
    K.params.append(pool_params)
    K.stage("pool", ada=pool_ada)
    K.stage("act", ada=act_ada)
    K.stage("vec", ada=vec_ada, ada_sum=vec_sum)
    K.stage("pe", ada_sum=pe_sum)


def block3(K):
    nc, T, ps, bk = K.nc, K.T, K.ps, K.bk
    yT, X = K.B_kt, K.X
    h_hi = K.A_parts.rearrange("p (k t) -> p k t", t=SEQ)
    lo_at = WORK - D * 2
    h_lo = tuple(r.rearrange("p (k t) -> p k t", t=SEQ) for r in (K.B_parts[:, 0:2 * D], K.work_parts[:, lo_at:]))
    h_lo_f32 = tuple(r.rearrange("p (k t) -> p k t", t=SEQ) for r in (K.B[:, 0:2 * D], K.work[:, lo_at:]))
    K.norm_parts[3] = (h_hi, h_lo_f32, h_lo)
    K.norm_parts_wait[3] = lambda vec, tt: None
    if not K.modulated:
        modulation(K)
    ln_g, gain = K.keep(KT), K.keep(KT)
    cw, cb, nw, skip = K.keep(M_TAPS * 8), K.keep(8), K.keep(8), K.keep(8)
    fb = K.keep(1)
    bias = {n: K.keep(w) for n, w in (("mx", 8), ("mo", 8), ("mz", 8), ("nq", 8), ("nz", 8), ("ksw", 4), ("kvc", 4),
                                    ("mv", 8), ("vv", 4), ("gates", 1))}
    pos = K.keep(C_LEN)
    K.norm_gain[3] = (gain, K.mod[:, 0:KT])
    a = K.arena()
    negM, wst = a("negM", SEQ), a("wst", SEQ)
    maskbd = a("maskbd", P)
    gates = a("gates", TT, 56)
    nat = a("nat", 3, TT, M_H)
    decb = a("decb", M_H, M_NC)
    mp = a("m_prev", M_NC + 1)
    mark = a.at[0]
    ndist, cdist = a("ndist", SEQ), a("cdist", TT, N_CMP)
    slope_tab = a("slope_tab", 2, SEQ)
    slope_cmp = a("slope_cmp", 2, TT, N_CMP)
    ksw, kws = a("ksw", 2, SEQ), a("kws", 2, SEQ)
    vv = a("vv", 2, TT, P)
    q = a("q", 2, 2, SEQ)
    kcmp, vcmp = a("kcmp", N_G * N_CMP), a("vcmp", N_G, N_HD)
    w2 = a("w2", 3, N_HD)
    hid = a("hid", 2, N_G * N_CMP)
    hb1 = a("hid_bias", 2)
    obuf = a("obuf", 2, TT, P)
    mx = a("mx", 2, 3)
    sums = a("sums", 4, 3)
    coef = a("coef", 2, 3)
    kv_mark = a.at[0]
    es = a("es", 2, 2, SEQ)
    ec = a("ec", 2, N_CMP)
    pT = a("pT", 2, 2, SEQ)
    cT = a("cT", 2, P)
    a2 = K.arena(kv_mark)
    kvc = a2("kvc", N_G, SEQ)
    Xf = X.rearrange("p t d -> p (t d)")
    x = K.arena(0, Xf)
    xc = x("xc", 4, SEQ)
    so = x("so", 4, SEQ)
    xp = x("xp", 1, SEQ + M_TAPS - 1)
    vx0, vx1 = x("vx0", TT, M_HD + 1), x("vx1", TT, M_HD + 1)
    vx = [vx0, vx1]
    cv = x("cv", 1, SEQ)
    turned = x("turned", SEQ)
    rows = K.arena(0, Xf)
    rf, ra, rb, rM, re, rt = (rows(n, SEQ) for n in ("rf", "ra", "rb", "rM", "re", "rt"))
    s = K.arena(mark)
    mq, mqt, mk = s("mq", 2, SEQ), s("mqt", 2, SEQ), s("mk", 2, SEQ)
    kn = s("kn", TT, M_HD)
    Cst = s("Cst", 2 * (M_NC - 1), M_HD + 1)
    E, Pm = s("E", SEQ), s("Pm", SEQ)
    hbuf = s("hbuf", TT, M_HD)
    st6, mv2, rden = s("st6", TT, 6), s("mv2", TT, 2), s("rden", TT)
    yt = s("yt", SEQ)
    assert max(a.at[0], a2.at[0], s.at[0]) <= lo_at

    qT, esb, pTb = ([[ap[:, p, i, :] for i in range(2)] for p in range(2)] for ap in (q, es, pT))

    names = (("mx", M_W), ("mv", M_W), ("mo", M_W), ("mz", M_W), ("mi", M_H), ("mf", M_H), ("nq", N_H * N_HD),
             ("kc", 256), ("vc", 256), ("ks", 256), ("vs", 256), ("kw", 256), ("vw", 256), ("ng", 3 * N_H), ("nz", 1024))
    col, c0 = {}, 0
    for n, w in names:
        col[n] = c0
        c0 += w
    W = T["w_in_3"][0]

    def tile(name, i):
        st = ("tile", 3, name, i)
        pair = {"gates": ("mi", 0, 8, "ng", 48), "ksw": ("ks", 64, 64, "kw", 64), "kvc": ("kc", 64, 64, "vc", 64),
                "vv": ("vs", 64, 64, "vw", 64)}
        if name in pair:
            c1, step, w1, c2, w2_ = pair[name]
            srcs = [(W, col[c1] + i * step, w1), (W, col[c2] + i * step, w2_)]
        else:
            srcs = [(W, col[name] + i * P, P)]
        late = name == "mz" or name in ("mx", "mo", "mv") and i >= M_H
        K.tile(st, srcs, "T", sum(w for _, _, w in srcs), h_hi, SEQ, lo=h_lo, lo_from=8 if late else 0,
               full=K.A_kt if late else None)
        return st

    script = ([] if K.modulated else ada_stages()) + [("norm", 3, tt) for tt in range(TT)]
    script.append(tile("gates", 0))
    K.after_norm(script[-1], 3)
    script += [tile("kvc", 0), ("turn", "gates", 0), ("mg_rows", 0), tile("kvc", 1), tile("kvc", 2), ("mg_nat", 0), tile("kvc", 3),
               ("cmp", 0), ("cmp2", 0)]
    G = [[tile("ksw", g), tile("vv", g), tile("nq", 2 * g), ("turn", "vv", g), tile("nq", 2 * g + 1)] for g in range(N_G)]
    M = [[tile("mx", 2 * h), tile("mx", 2 * h + 1), tile("mv", 2 * h), tile("mo", 2 * h), ("turn", "mv", 2 * h),
          tile("mv", 2 * h + 1), tile("mo", 2 * h + 1), ("turn", "mv", 2 * h + 1)] for h in range(M_H)]
    NZ, MZ = [tile("nz", i) for i in range(8)], [tile("mz", i) for i in range(8)]
    units = [(g, j, qb, hh) for g in range(N_G) for j in range(2) for qb in range(TT) for hh in range(2)]
    at = {u: n for n, u in enumerate(units)}

    def attention_steps(n):
        out = []
        if n < len(units):
            out.append(("nsa_s", n))
        if 0 <= n - 1 < len(units):
            out.append(("nsa_t", n - 1))
        if 0 <= n - 2 < len(units):
            out.append(("nsa_v", n - 2))
            if units[n - 2][2:] == (TT - 1, 1):
                out.append(("nsa_o", n - 2))
        return out

    script += G[0]
    between = [NZ[0:2] + G[1] + M[0][0:2], NZ[2:4] + G[2] + M[0][2:5], NZ[4:6] + G[3] + M[0][5:8] + M[1][0:2], NZ[6:8] + M[1][2:8]]
    per_group = len(units) // N_G
    n = 0
    for g, tiles in enumerate(between):
        for i, t in enumerate(tiles):
            script.append(t)
            while n < per_group * g + per_group * (i + 1) // len(tiles):
                script += attention_steps(n)
                n += 1
    script.append(("h_whole", 0))
    script += attention_steps(n) + attention_steps(n + 1)

    head = lambda h: [("ml_qk", h), ("ml_s", h), ("ml_u", h), ("ml_n", h), ("ml_t", h)]
    script += spread_steps(MZ[0:6], head(0)) + spread_steps(M[2], head(1)) + spread_steps(M[3], head(2)) + \
        spread_steps(MZ[6:8], head(3))
    turns = [st for st in script if st[0] == "turn"]
    script += [("wo", 3, n) for n in range(4)] + [("final", 3, tt) for tt in range(TT)]

    for st in script:
        kind = st[0]
        if kind == "mg_rows":
            K.uses[st] = [("i", "S", 1), ("f", "S", 2)]
        elif kind == "mg_nat":
            K.uses[st] = [("n", "S", 1), ("d", "S", 1)]
        elif kind == "cmp":
            K.uses[st] = [(0, "S", 1), (1, "S", 1)]
        elif kind == "cmp2":
            K.uses[st] = [("k", "S", 1), ("v", "S", 1)]
        elif kind in ("nsa_s", "nsa_t"):
            K.uses[st] = [(b, "S", 1) for b in range(3)]
        elif kind in ("nsa_v", "nsa_o", "turn"):
            K.uses[st] = [(0, "S", 1)]
        elif kind == "ml_qk":
            K.uses[st] = [(("q", e), "S", 1) for e in range(2)] + [(("k", e), "S", 1) for e in range(2)] + \
                         [(("n", e), "S", 1) for e in range(2)]
        elif kind == "ml_s":
            K.uses[st] = [("m", "S", 1), ("w", "S", 1), ("s", "S", 1)]
        elif kind == "ml_u":
            K.uses[st] = [((c, d), "S", 1) for c in range(M_NC - 1) for d in range(2)]
        elif kind == "ml_n":
            K.uses[st] = [(tt, "S", 1) for tt in range(TT)]
        elif kind == "ml_t":
            K.uses[st] = [(j, "S", 1) for j in range(2)]

    s_par = K.sem("b3_params")
    s_tab = K.sem("b3_tables")
    s_keep, s_back = K.sem("x_kept"), K.sem("x_back")
    s_gain = K.sem("gain_ready")
    s_fg = K.sem("final_gain_3_loaded")
    s_gate = K.sem("gate_rows_act")
    s_gatev = K.sem("gate_rows_vec")
    s_bq = K.sem("scaled_bias_ready")
    s_swap = [K.sem(f"keys_swapped{i}") for i in range(2)]
    s_hid = K.sem("hidden_ready")
    s_hbias = K.sem("hidden_bias_ready")
    s_slope = K.sem("slope_tables_ready")
    s_score = K.sem("scores_ready")
    s_exp = K.sem("exps_ready")
    s_comb = K.sem("unit_combined")
    s_conv = K.sem("mconv_ready")
    s_xc = K.sem("xc_ready")
    s_E = K.sem("decay_logits_ready")
    s_Ee = K.sem("decay_weights_ready")
    s_Pm = K.sem("weighted_scores_ready")
    s_qt = K.sem("decayed_q_ready")
    s_C = K.sem("cell_state_ready")
    s_var = K.sem("head_variance_ready")
    s_std = K.sem("head_std_ready")
    s_hn = K.sem("head_normed")
    s_y = K.sem("ungated_tile_ready")
    s_whole = K.sem("input_whole_again")
    x_keep = nc.dram_tensor("x_keep", (SEQ, D), F32).ap()

    def pool_params(pool):
        n = 0
        t = lambda name: T[name + "_3"]
        vec_of = lambda ap: ap.rearrange("o (k p) -> p (o k)", p=P)
        b_in = t("b_in")
        loads = [(ln_g, vec_of(t("ln_g"))), (cb, vec_of(t("m_conv_b"))), (nw, vec_of(t("m_norm_w"))),
                 (skip, vec_of(t("m_skip"))), (fb[0:M_H, :], t("m_f_bias").rearrange("o h -> h o")),
                 (pos[0:64, :], t("n_pos_k")[0].rearrange("l d -> d l")),
                 (pos[64:128, :], t("n_pos_v")[0].rearrange("l d -> d l"))]
        loads += [(cw[:, 8 * j:8 * j + 8], vec_of(t("m_conv_w")[0, j:j + 1])) for j in range(M_TAPS)]
        loads += [(bias[n], vec_of(b_in[:, col[n]:col[n] + 1024])) for n in ("mx", "mo", "mv", "mz", "nq", "nz")]
        for name, lo, hi in (("ksw", "ks", "kw"), ("kvc", "kc", "vc"), ("vv", "vs", "vw")):
            for r, c in ((0, lo), (64, hi)):
                loads.append((bias[name][r:r + 64, :], b_in[:, col[c]:col[c] + 256].rearrange("o (g d) -> d (o g)", d=64)))
        for r, c, w in ((0, "mi", 8), (8, "ng", 48)):
            loads.append((bias["gates"][r:r + w, :], b_in[:, col[c]:col[c] + w].rearrange("o k -> k o")))
        with nc.allow_non_contiguous_dma(reason="small per-channel parameters"):
            for dst, src in loads:
                pool.dma_start(dst, src).then_inc(s_par, 16)
                n += 16
        K.par_count[3] = n

    def pool_norm(pool, st):
        _, blk, tt = st
        if blk != 3:
            return
        g = K.blocks.index(3)
        if g == 0:
            for s in K.s_x:
                pool.wait_ge(s, 16)
        else:
            pool.wait_ge(K.x_done, g * TT + (tt - TT + 1))
        pool.dma_start(x_keep[tt * P:(tt + 1) * P, :], X[:, tt, :]).then_inc(s_keep, 16)

    def pool_tile(pool, st):
        _, _, name, i = st
        if name == "ksw":
            pool.wait_ge(*bk.released(st))
            if i >= 2:
                pool.wait_ge(*bk.filled(("nsa_s", at[(i - 2, 1, TT - 1, 1)]), 2))
            pool.dma_start(kws[0:64, i % 2, :], ksw[64:128, i % 2, :]).then_inc(s_swap[i % 2], 16)
            pool.dma_start(kws[64:128, i % 2, :], ksw[0:64, i % 2, :]).then_inc(s_swap[i % 2], 16)

    tables = [(maskbd, T["c_maskbd"]), (ndist, T["c_ndist"]), (cdist, T["c_cdist"]),
              (w2[:, 0, :], T["n_w2_k_3"][0]), (w2[:, 1, :], T["n_w2_k_3"][0]), (w2[:, 2, :], T["n_w2_v_3"][0])]

    def pool_tables(pool, st):
        pool.wait_ge(*bk.filled(("norm", 3, TT - 1), KT // 4 - 1))
        for dst, src in tables:
            pool.dma_start(dst, src).then_inc(s_tab, 16)
    n_tab = 16 * len(tables)

    def pool_wo(pool, st):
        if st[2] == 0:
            pool.wait_ge(K.y_done, K.y_base[3] + KT)
            pool.wait_ge(s_keep, 16 * TT)
            for tt in range(TT):
                pool.dma_start(X[:, tt, :], x_keep[tt * P:(tt + 1) * P, :]).then_inc(s_back, 16)
            pool.dma_start(K.work[:, 2 * D:3 * D], T["final_g_3"].partition_broadcast(P)).then_inc(s_fg, 16)

    def pe_turn(pe, st):
        _, name, i = st
        pe.wait_ge(*bk.released(("tile", 3, name, i)))
        bk.take(pe, st)
        w = K.tiles["tile", 3, name, i]["w"]
        for tt in range(TT):
            mm = nc.tensor.transpose(ps(st)[:, tt * P:tt * P + w], turned[0:w, tt * P:(tt + 1) * P], K.ident[0:w, 0:w])
        mm.then_inc(bk.full_sem(st), 1)

    def pe_mg_rows(pe, st):
        pe.wait_ge(*bk.released(("turn", "gates", 0)))
        for key, c in (("i", 0), ("f", M_H)):
            bk.take(pe, st, key)
            for tt in range(TT):
                mm = nc.tensor.transpose(ps(st, key)[0:M_H, tt * P:(tt + 1) * P], gates[:, tt, c:c + M_H], K.ident[:, :])
            mm.then_inc(bk.full_sem(st, key), 1)

    def pe_mg_nat(pe, st):
        pe.wait_ge(s_gate, 5)
        pe.wait_ge(s_gatev, 1)
        bk.take(pe, st, "n")
        for i, r in enumerate((ra, rt, re)):
            for tt in range(TT):
                mm = nc.tensor.transpose(ps(st, "n")[:, (i * TT + tt) * M_H:(i * TT + tt + 1) * M_H],
                                         r[0:M_H, tt * P:(tt + 1) * P], K.ident[0:M_H, 0:M_H])
        mm.then_inc(bk.full_sem(st, "n"), 1)
        bk.take(pe, st, "d")
        for h in range(M_H):
            mm = nc.tensor.matmul(ps(st, "d")[:, h * M_NC:(h + 1) * M_NC], lhsT=K.ident[0:M_H, h:h + 1].to_broadcast([M_H, P]),
                                  rhs=wst[0:M_H, M_CH - 1::M_CH], start=True, stop=True)
        mm.then_inc(bk.full_sem(st, "d"), 1)

    def pe_cmp(pe, st):
        for i in range(N_G):
            pe.wait_ge(*bk.released(("tile", 3, "kvc", i)))
        pe.wait_ge(s_par, K.par_count[3])
        n = N_G * N_CMP
        for b in range(2):
            bk.take(pe, st, b)
        w1 = [K.slot_ap(st, s_).rearrange("p (l h) -> p l h", h=C_HID) for s_ in range(4)]
        for s_ in range(4):
            pe.wait_ge(*K.slot_loaded(st, s_))
        for b in range(2):
            r = slice(64 * b, 64 * b + 64)
            for l in range(C_LEN):
                rhs = kvc[r, :, l:l + C_STEP * (N_CMP - 1) + 1:C_STEP]
                nc.tensor.matmul(ps(st, b)[:, 0:n].rearrange("p (g j) -> p g j", j=N_CMP), lhsT=w1[l // 8][r, l % 8, :], rhs=rhs, start=(l == 0),
                                 stop=(l == C_LEN - 1))
            for l in range(C_LEN):
                mm = nc.tensor.matmul(ps(st, b)[:, n:n + 1], lhsT=w1[l // 8][r, l % 8, :], rhs=pos[r, l:l + 1],
                                      start=(l == 0), stop=(l == C_LEN - 1))
            mm.then_inc(bk.full_sem(st, b), 1)

    def pe_cmp2(pe, st):
        pe.wait_ge(s_hid, 2)
        pe.wait_ge(s_tab, n_tab)
        bk.take(pe, st, "k")
        nc.tensor.matmul(ps(st, "k")[:, 0:N_G * N_CMP], lhsT=w2[:, 0:2, :], rhs=hid[:, 0, :],
                         start=True, stop=True).then_inc(bk.full_sem(st, "k"), 1)
        bk.take(pe, st, "v")
        for g in range(N_G):
            mm = nc.tensor.matmul(ps(st, "v")[0:N_CMP, g * N_HD:(g + 1) * N_HD], lhsT=hid[:, 1, g * N_CMP:(g + 1) * N_CMP],
                                  rhs=w2[:, 2, :], start=True, stop=True)
        mm.then_inc(bk.full_sem(st, "v"), 1)

    def pe_nsa_s(pe, st):
        g, j, qb, hh = units[st[1]]
        r = slice(64 * hh, 64 * hh + 64)
        nk = (qb + 1) * P
        if (j, qb, hh) == (0, 0, 0):
            pe.wait_ge(s_swap[g % 2], 32 * (g // 2 + 1))
            pe.wait_ge(*bk.released(("tile", 3, "ksw", g)))
            pe.wait_ge(*bk.released(("tile", 3, "nq", 2 * g)))
            pe.wait_ge(*bk.released(("tile", 3, "nq", 2 * g + 1)))
            if g == 0:
                pe.wait_ge(*bk.released(("cmp2", 0), "k"))
        lhsT = qT[g % 2][j][r, qb * P:(qb + 1) * P]
        keys = (kcmp[r, g * N_CMP:(g + 1) * N_CMP], (ksw, kws)[hh][r, g % 2, 0:nk], (kws, ksw)[hh][r, g % 2, 0:nk])
        for b, rhs in enumerate(keys):
            bk.take(pe, st, b)
            nc.tensor.matmul(ps(st, b)[:, 0:rhs.shape[1]], lhsT=lhsT, rhs=rhs, start=True,
                             stop=True).then_inc(bk.full_sem(st, b), 1)

    def pe_nsa_t(pe, st):
        u = st[1]
        g, j, qb, hh = units[u]
        for b in range(3):
            pe.wait_ge(s_exp, 3 * u + b + 1)
            bk.take(pe, st, b)
            if b == 0:
                mm = nc.tensor.transpose(ps(st, b)[0:N_CMP, 0:P], ec[:, u % 2, :], K.ident[:, :])
            else:
                for kt in range(qb + 1):
                    mm = nc.tensor.transpose(ps(st, b)[:, kt * P:(kt + 1) * P], esb[u % 2][b - 1][:, kt * P:(kt + 1) * P],
                                             K.ident[:, :])
            mm.then_inc(bk.full_sem(st, b), 1)

    def pe_nsa_v(pe, st):
        u = st[1]
        g, j, qb, hh = units[u]
        if u == 0:
            pe.wait_ge(*bk.released(("cmp2", 0), "v"))
        if (j, qb, hh) == (0, 0, 0):
            pe.wait_ge(*bk.released(("turn", "vv", g)))
        for b in range(3):
            pe.wait_ge(*bk.released(("nsa_t", u), b))
        bk.take(pe, st)
        o = ps(st)
        nc.tensor.matmul(o[:, 0:N_HD], lhsT=cT[0:N_CMP, u % 2, :], rhs=vcmp[0:N_CMP, g, :], start=True, stop=True)
        for b in (1, 2):
            for kt in range(qb + 1):
                mm = nc.tensor.matmul(o[:, b * N_HD:(b + 1) * N_HD], lhsT=pTb[u % 2][b - 1][:, kt * P:(kt + 1) * P],
                                      rhs=vv[:, g % 2, kt, (b - 1) * N_HD:b * N_HD], start=(kt == 0), stop=(kt == qb))
        mm.then_inc(bk.full_sem(st), 1)

    def pe_nsa_o(pe, st):
        u = st[1]
        pe.wait_ge(s_comb, u + 1)
        bk.take(pe, st)
        par = (u // 8) % 2
        for tt in range(TT):
            mm = nc.tensor.transpose(ps(st)[:, tt * P:(tt + 1) * P], obuf[:, par, tt, :], K.ident[:, :])
        mm.then_inc(bk.full_sem(st), 1)

    def pe_ml_qk(pe, st):
        h = st[1]
        pe.wait_ge(s_xc, 2 * h + 2)
        pe.wait_ge(*K.slot_loaded(st))
        if h == 0:
            pe.wait_ge(s_comb, len(units))
        w = K.slot_ap(st).rearrange("p (m k e) -> p m k e", m=2, k=2)
        for m, key in ((0, "q"), (1, "k")):
            for e in range(2):
                bk.take(pe, st, (key, e))
                for d in range(2):
                    mm = nc.tensor.matmul(ps(st, (key, e)), lhsT=w[:, m, d, e * P:(e + 1) * P], rhs=xc[:, 2 * (h % 2) + d, :],
                                          start=(d == 0), stop=(d == 1))
                mm.then_inc(bk.full_sem(st, (key, e)), 1)
        for half in range(2):
            bk.take(pe, st, ("n", half))
            for i in range(2):
                tt = 2 * half + i
                for d in range(2):
                    mm = nc.tensor.matmul(ps(st, ("n", half))[:, i * M_HD:(i + 1) * M_HD],
                                          lhsT=xc[:, 2 * (h % 2) + d, tt * P:(tt + 1) * P], rhs=w[:, 1, d, :],
                                          start=(d == 0), stop=(d == 1))
            mm.then_inc(bk.full_sem(st, ("n", half)), 1)

    def pe_ml_s(pe, st):
        h = st[1]
        for key, r in (("m", negM), ("w", wst)):
            bk.take(pe, st, key)
            nc.tensor.matmul(ps(st, key), lhsT=K.ident[0:M_H, h:h + 1].to_broadcast([M_H, P]), rhs=r[0:M_H, :], start=True,
                             stop=True).then_inc(bk.full_sem(st, key), 1)
        for key in ("q", "k"):
            for e in range(2):
                pe.wait_ge(*bk.released(("ml_qk", h), (key, e)))
        bk.take(pe, st, "s")
        for tt in range(TT):
            t = slice(tt * P, (tt + 1) * P)
            for d in range(2):
                mm = nc.tensor.matmul(ps(st, "s")[:, t], lhsT=mk[:, d, t], rhs=mq[:, d, t], start=(d == 0), stop=(d == 1))
        mm.then_inc(bk.full_sem(st, "s"), 1)

    def pe_ml_u(pe, st):
        h = st[1]
        for half in range(2):
            pe.wait_ge(*bk.released(("ml_qk", h), ("n", half)))
        for j in range(2):
            pe.wait_ge(*bk.released(("turn", "mv", 2 * h + j)))
        for c in range(M_NC - 1):
            r = slice((c % 2) * M_CH, (c % 2 + 1) * M_CH)
            for d in range(2):
                bk.take(pe, st, (c, d))
                nc.tensor.matmul(ps(st, (c, d))[:, 0:M_HD + 1], lhsT=kn[r, c // 2, d * P:(d + 1) * P],
                                 rhs=vx[h % 2][r, c // 2, :], start=True, stop=True).then_inc(bk.full_sem(st, (c, d)), 1)

    def pe_ml_n(pe, st):
        h = st[1]
        pe.wait_ge(s_Pm, h + 1)
        pe.wait_ge(s_qt, h + 1)
        for tt in range(TT):
            bk.take(pe, st, tt)
            o = ps(st, tt)[:, 0:M_HD + 1]
            mm = nc.tensor.matmul(o, lhsT=Pm[:, tt * P:(tt + 1) * P], rhs=vx[h % 2][:, tt, :], start=True, stop=False,
                                  skip_group_check=True)
            for c in (2 * tt, 2 * tt + 1):
                if c == 0:
                    continue
                pe.wait_ge(s_C, 14 * h + 2 * c)
                r = slice((c % 2) * M_CH, (c % 2 + 1) * M_CH)
                for d in range(2):
                    mm = nc.tensor.matmul(o[r, :], lhsT=mqt[:, d, c * M_CH:(c + 1) * M_CH], rhs=Cst[:, 2 * (c - 1) + d, :],
                                          start=False, stop=(d == 1), skip_group_check=True)
            mm.then_inc(bk.full_sem(st, tt), 1)

    def pe_ml_t(pe, st):
        h = st[1]
        pe.wait_ge(s_hn, TT * (h + 1))
        for j in range(2):
            bk.take(pe, st, j)
            for tt in range(TT):
                mm = nc.tensor.transpose(ps(st, j)[:, tt * P:(tt + 1) * P], hbuf[:, tt, j * P:(j + 1) * P], K.ident[:, :])
            mm.then_inc(bk.full_sem(st, j), 1)

    def act_tile(act, L, st):
        _, _, name, i = st
        b = ps(st)
        if name == "mx":
            act.wait_ge(s_conv, i + 1)
            nc.scalar.activation(xc[:, i % 4, :], cv[:, 0, :], ACT.Silu).then_inc(s_xc, 1)
            return
        if name == "nq" and i >= 4:
            act.wait_ge(*bk.filled(("nsa_s", at[(i // 2 - 2, 1, TT - 1, 1)]), 2))
        if name == "ksw" and i >= 2:
            act.wait_ge(*bk.filled(("nsa_s", at[(i - 2, 1, TT - 1, 1)]), 2))
            act.wait_ge(s_swap[i % 2], 32 * (i // 2))
        if name == "mo" and i >= 4:
            act.wait_ge(s_y, 2 * (i // 2 - 2) + 2)
        if name in ("vv", "mv", "gates"):
            n = turns.index(("turn", name, i))
            if n == 0:
                act.wait_ge(s_keep, 16 * TT)
            else:
                act.wait_ge(*bk.filled(turns[n - 1]))
        if name in ("gates", "kvc") and i == 0:
            act.wait_ge(s_par, K.par_count[3])
            act.wait_ge(s_bq, 1)
        act.wait_ge(*bk.filled(st))
        if name in ("gates", "vv", "mv"):
            w = K.tiles[st]["w"]
            ins = nc.scalar.activation(turned[0:w, :], b[0:w, :], ACT.Identity, bias=bias[name][0:w, i:i + 1])
        elif name == "kvc":
            ins = nc.scalar.activation(kvc[:, i, :], b, ACT.Identity, bias=bias["kvc"][:, i:i + 1])
        elif name == "ksw":
            ins = nc.scalar.activation(ksw[:, i % 2, :], b, ACT.Identity, bias=bias["ksw"][:, i:i + 1])
        elif name == "nq":
            ins = nc.scalar.activation(qT[(i // 2) % 2][i % 2], b, ACT.Identity, bias=bias["nq"][:, i:i + 1],
                                       scale=N_HD ** -0.5)
        elif name == "mo":
            ins = nc.scalar.activation(so[:, i % 4, :], b, ACT.Sigmoid, bias=bias["mo"][:, i:i + 1])
        else:
            ins = nc.scalar.activation(yT[:, 8 + i if name == "nz" else i, :], b, ACT.Silu, bias=bias[name][:, i:i + 1])
        ins.then_inc(bk.free_sem(st), 1)

    def act_turn(act, L, st):
        _, name, i = st
        if name == "vv" and i >= 2:
            act.wait_ge(*bk.filled(("nsa_v", at[(i - 2, 1, TT - 1, 1)])))
        if name == "mv" and i >= 4:
            act.wait_ge(*bk.filled(("ml_n", i // 2 - 2), TT - 1))
        act.wait_ge(*bk.filled(st))
        rows = ps(st).rearrange("p (t c) -> p t c", c=P)
        if name == "gates":
            L(nc.scalar.activation(gates[:, :, 0:8], rows[:, :, 0:8], ACT.Copy))
            ins = nc.scalar.activation(gates[:, :, 8:56], rows[:, :, 8:56], ACT.Sigmoid)
        elif name == "vv":
            ins = nc.scalar.activation(vv[:, i % 2, :, :], rows, ACT.Copy)
        else:
            ins = nc.scalar.activation(vx[(i // 2) % 2][:, :, (i % 2) * P:(i % 2 + 1) * P], rows, ACT.Copy)
        ins.then_inc(bk.free_sem(st), 1)

    def act_mg_rows(act, L, st):
        act.wait_ge(*bk.filled(st, "f"))
        act.wait_ge(s_keep, 16 * TT)
        act.wait_ge(s_hn_done, hn_done)
        r = slice(0, M_H)
        nc.scalar.activation(rf[r, :], ps(st, "f")[r, :], ACT.Abs, bias=fb[r, 0:1]).then_inc(bk.free_sem(st, "f"), 1)
        act.wait_ge(*bk.read_once(st, "f"))
        L(nc.scalar.activation(rf[r, :], rf[r, :], ACT.Exp, scale=-1.0))
        L.settle()
        nc.scalar.activation(rf[r, :], rf[r, :], ACT.Ln, bias=1.0).then_inc(s_gate, 1)
        act.wait_ge(s_gatev, 1)
        nc.scalar.activation(wst[r, :], wst[r, :], ACT.Exp).then_inc(s_gate, 1)
        nc.scalar.activation(re[r, :], re[r, :], ACT.Exp, scale=-1.0).then_inc(s_gate, 1)
        nc.scalar.activation(rt[r, :], rt[r, :], ACT.Exp).then_inc(s_gate, 1)
        nc.scalar.activation(negM[r, :], rM[r, :], ACT.Copy, scale=-1.0).then_inc(s_gate, 1)

    def act_cmp(act, L, st):
        n = N_G * N_CMP
        act.wait_ge(s_hbias, 1)
        for b in range(2):
            act.wait_ge(*bk.filled(st, b))
            nc.scalar.activation(hid[:, b, :], ps(st, b)[:, 0:n], ACT.Gelu_apprx_tanh,
                                 bias=hb1[:, b:b + 1]).then_inc(s_hid, 1)
            act.wait_ge(s_hid, b + 1)
            act.sem_inc(bk.free_sem(st, b), 1)

    def act_cmp2(act, L, st):
        act.wait_ge(*bk.filled(st, "k"))
        nc.scalar.activation(kcmp[:, :], ps(st, "k")[:, 0:N_G * N_CMP], ACT.Copy).then_inc(bk.free_sem(st, "k"), 1)
        act.wait_ge(*bk.filled(st, "v"))
        nc.scalar.activation(vcmp[0:N_CMP, :, :], ps(st, "v")[0:N_CMP, 0:N_G * N_HD].rearrange("p (g d) -> p g d", d=N_HD),
                             ACT.Copy).then_inc(bk.free_sem(st, "v"), 1)

    def act_nsa_s(act, L, st):
        u = st[1]
        g, j, qb, hh = units[u]
        nk = (qb + 1) * P
        n = g * N_HPG + 2 * j + hh
        if qb == 0:
            act.wait_ge(s_tab, n_tab)
            if n >= 2:
                act.wait_ge(s_score, 3 * (u - 1))
            slope = 2.0 ** (-8.0 * (n + 1) / N_H)
            nc.scalar.activation(slope_tab[:, hh, :], ndist, ACT.Copy, scale=slope).then_inc(s_slope, 1)
            nc.scalar.activation(slope_cmp[:, hh, :, :], cdist, ACT.Copy, scale=slope).then_inc(s_slope, 1)
        for b in range(3):
            act.wait_ge(s_score, 3 * u + b + 1)
            e = ec[:, u % 2, :] if b == 0 else esb[u % 2][b - 1][:, 0:nk]
            nc.scalar.activation(e, e, ACT.Exp, bias=mx[:, u % 2, b:b + 1],
                                 accum_out=sums[:, u % 4, b:b + 1]).then_inc(s_exp, 1)

    def act_nsa_t(act, L, st):
        u = st[1]
        qb = units[u][2]
        nk = (qb + 1) * P
        if u >= 2:
            act.wait_ge(*bk.filled(("nsa_v", u - 2)))
        act.wait_ge(*bk.filled(st, 1))
        nc.scalar.activation(pTb[u % 2][0][:, 0:nk], ps(st, 1)[:, 0:nk], ACT.Copy).then_inc(bk.free_sem(st, 1), 1)

    def act_ml_qk(act, L, st):
        h = st[1]
        for key, dst, sc in (("q", mq, 1.0), ("k", mk, M_HD ** -0.5)):
            for e in range(2):
                act.wait_ge(*bk.filled(st, (key, e)))
                if h >= 1 and e == 0:
                    act.wait_ge(*bk.filled(("ml_s", h - 1), "s"))
                    act.wait_ge(s_qt, h)
                nc.scalar.activation(dst[:, e, :], ps(st, (key, e)), ACT.Copy, scale=sc).then_inc(bk.free_sem(st, (key, e)), 1)

    def act_ml_s(act, L, st):
        h = st[1]
        act.wait_ge(s_E, h + 1)
        for tt in range(TT):
            t = slice(tt * P, (tt + 1) * P)
            nc.scalar.activation(E[:, t], E[:, t], ACT.Exp, bias=natc(0, tt, h)).then_inc(s_Ee, 1)

    def natc(i, tt, h):
        c = (i * TT + tt) * M_H + h
        return nat2[:, c:c + 1]
    nat2 = nat.rearrange("p a b c -> p (a b c)")

    def act_ml_n(act, L, st):
        h = st[1]
        for tt in range(TT):
            act.wait_ge(s_var, TT * h + tt + 1)
            nc.scalar.activation(mv2[:, tt, 1:2], mv2[:, tt, 1:2], ACT.Sqrt, bias=K.eps[:, 0:1]).then_inc(s_std, 1)

    def wait_gain(vec):
        vec.wait_ge(s_par, K.par_count[3])
        L = K.vlane[0]
        L(nc.vector.scalar_tensor_tensor(gain, K.mod[:, KT:2 * KT], 1.0, ln_g, ALU.add, ALU.mult))
        L.settle()
        nc.vector.tensor_scalar(bias["nq"], bias["nq"], N_HD ** -0.5, None, ALU.mult).then_inc(s_bq, 1)

    def vec_tile(vec, L, st):
        _, _, name, i = st
        b = ps(st)
        if name == "mx":
            vec.wait_ge(*bk.filled(st))
            if i == 0:
                vec.wait_ge(s_gate, 5)
                vec.wait_ge(*bk.filled(("mg_nat", 0), "d"))
                L(nc.vector.memset(xp[:, :, 0:M_TAPS - 1], 0.0))
                for v in vx:
                    L(nc.vector.memset(v[:, :, M_HD:M_HD + 1], 1.0))
            u = xp[:, 0, :]
            if i >= 4:
                vec.wait_ge(s_y, 2 * (i // 2 - 2) + 2)
            nc.vector.tensor_scalar(u[:, M_TAPS - 1:], b, bias["mx"][:, i:i + 1], None, ALU.add).then_inc(bk.free_sem(st), 1)
            vec.wait_ge(*bk.released(st))
            L.settle()
            if i >= 1:
                vec.wait_ge(s_xc, i)
            for k in range(M_TAPS):
                w = cw[:, 8 * k + i:8 * k + i + 1]
                if k == 0:
                    ins = nc.vector.tensor_scalar(cv[:, 0, :], u[:, 0:SEQ], w, cb[:, i:i + 1], ALU.mult, ALU.add)
                else:
                    ins = nc.vector.scalar_tensor_tensor(cv[:, 0, :], u[:, k:k + SEQ], w, cv[:, 0, :], ALU.mult, ALU.add)
                if k < M_TAPS - 1:
                    L(ins)
                    L.settle()
            ins.then_inc(s_conv, 1)
            vec.wait_ge(s_conv, i + 1)

    def vec_h_whole(vec, L, st):
        vec.wait_ge(*bk.filled(M[1][6]))
        k8 = slice(0, 2 * D)
        nc.vector.tensor_tensor(K.A[:, k8], K.A_parts[:, k8], K.B_parts[:, k8], ALU.add).then_inc(s_whole, 1)
        vec.wait_ge(s_whole, 1)

    def vec_mg_rows(vec, L, st):
        r = slice(0, M_H)
        vec.wait_ge(*bk.read_once(st, "f"))
        vec.wait_ge(s_keep, 16 * TT)
        vec.wait_ge(s_hn_done, hn_done)
        L(nc.vector.tensor_scalar(rb[r, :], ps(st, "f")[r, :], fb[r, 0:1], 0.0, ALU.add, ALU.min))
        L(nc.vector.memset(mp[r, 0:1], 0.0))
        L.settle()
        vec.sem_inc(bk.free_sem(st, "f"), 1)
        vec.wait_ge(s_gate, 1)
        L(nc.vector.tensor_tensor(ra[r, :], rb[r, :], rf[r, :], ALU.subtract))
        L.settle()
        L(nc.vector.tensor_tensor_scan(rb[r, :], K.reset[r, :], ra[r, :], 0.0, ALU.mult, ALU.add))
        L.settle()
        vec.wait_ge(*bk.filled(st, "i"))
        nc.vector.tensor_tensor(ra[r, :], ps(st, "i")[r, :], rb[r, :], ALU.subtract).then_inc(bk.free_sem(st, "i"), 1)
        vec.wait_ge(*bk.released(st, "i"))
        for c in range(M_NC):
            t, e = slice(c * M_CH, (c + 1) * M_CH), slice((c + 1) * M_CH - 1, (c + 1) * M_CH)
            L(nc.vector.tensor_tensor_scan(rM[r, t], ra[r, t], ra[r, t], mp[r, c:c + 1], ALU.max, ALU.max))
            L.settle()
            L(nc.vector.tensor_tensor(mp[r, c + 1:c + 2], rb[r, e], rM[r, e], ALU.add))
            L.settle()
        c3 = lambda ap: ap[r, :].rearrange("p (c l) -> p c l", l=M_CH)
        whole = [M_H, M_NC, M_CH]
        L(nc.vector.tensor_tensor(c3(wst), mp[r, 0:M_NC].unsqueeze(2).to_broadcast(whole), c3(rM), ALU.subtract))
        L(nc.vector.tensor_tensor(re[r, :], rb[r, :], rM[r, :], ALU.add))
        L(nc.vector.tensor_tensor(c3(rt), c3(ra), c3(rM)[:, :, M_CH - 1:M_CH].to_broadcast(whole), ALU.subtract))
        L.settle()
        vec.sem_inc(s_gatev, 1)

    def vec_mg_nat(vec, L, st):
        vec.wait_ge(*bk.filled(st, "n"))
        nc.vector.tensor_copy(nat2, ps(st, "n")[:, 0:3 * TT * M_H]).then_inc(bk.free_sem(st, "n"), 1)
        vec.wait_ge(*bk.filled(st, "d"))
        nc.vector.tensor_copy(decb.rearrange("p h c -> p (h c)"), ps(st, "d")[:, 0:M_H * M_NC]).then_inc(bk.free_sem(st, "d"), 1)

    def vec_cmp(vec, L, st):
        n = N_G * N_CMP
        for b in range(2):
            vec.wait_ge(*bk.filled(st, b))
            L(nc.vector.tensor_copy(hb1[:, b:b + 1], ps(st, b)[:, n:n + 1]))
        L.settle()
        vec.sem_inc(s_hbias, 1)

    def vec_nsa_s(vec, L, st):
        u = st[1]
        g, j, qb, hh = units[u]
        nk = (qb + 1) * P
        n = g * N_HPG + 2 * j + hh
        if u >= 2:
            for b in range(3):
                vec.wait_ge(*bk.filled(("nsa_t", u - 2), b))
        vec.wait_ge(s_slope, 2 * (n + 1))
        for b in range(3):
            vec.wait_ge(*bk.filled(st, b))
            width = N_CMP if b == 0 else nk
            e = ec[:, u % 2, :] if b == 0 else esb[u % 2][b - 1][:, 0:nk]
            table = slope_cmp[:, hh, qb, :] if b == 0 else slope_tab[:, hh, SEQ - nk:SEQ]
            m = mx[:, u % 2, b:b + 1]
            nc.vector.tensor_tensor_reduce(e, ps(st, b)[:, 0:width], table, 1.0, -3e38, ALU.add, ALU.max,
                                           m).then_inc(bk.free_sem(st, b), 1)
            vec.wait_ge(*bk.released(st, b))
            if b == 0:
                nc.vector.tensor_scalar(m, m, -1.0, 1e20, ALU.mult, ALU.min).then_inc(s_score, 1)
            else:
                nc.vector.tensor_scalar(m, m, -1.0, None, ALU.mult).then_inc(s_score, 1)

    def vec_nsa_t(vec, L, st):
        u = st[1]
        nk = (units[u][2] + 1) * P
        if u >= 2:
            vec.wait_ge(*bk.filled(("nsa_v", u - 2)))
        vec.wait_ge(*bk.filled(st, 0))
        nc.vector.tensor_copy(cT[0:N_CMP, u % 2, :], ps(st, 0)[0:N_CMP, 0:P]).then_inc(bk.free_sem(st, 0), 1)
        vec.wait_ge(*bk.filled(st, 2))
        nc.vector.tensor_copy(pTb[u % 2][1][:, 0:nk], ps(st, 2)[:, 0:nk]).then_inc(bk.free_sem(st, 2), 1)

    def vec_nsa_v(vec, L, st):
        u = st[1]
        g, j, qb, hh = units[u]
        n = g * N_HPG + 2 * j + hh
        par = (u // 8) % 2
        if u >= 16 and u % 8 == 0:
            vec.wait_ge(*bk.filled(("nsa_o", u - 9)))
        vec.wait_ge(s_exp, 3 * u + 3)
        c = coef[:, u % 2, :]
        L(nc.vector.tensor_scalar(c, sums[:, u % 4, :], 1e-30, None, ALU.max))
        L.settle()
        L(nc.vector.reciprocal(c, c))
        L.settle()
        L(nc.vector.tensor_tensor(c, c, gates[:, qb, 8 + 3 * n:8 + 3 * n + 3], ALU.mult))
        L.settle()
        vec.wait_ge(*bk.filled(st))
        o = obuf[:, par, qb, hh * N_HD:(hh + 1) * N_HD]
        p = ps(st)
        L(nc.vector.tensor_scalar(o, p[:, 0:N_HD], c[:, 0:1], None, ALU.mult))
        L.settle()
        L(nc.vector.scalar_tensor_tensor(o, p[:, N_HD:2 * N_HD], c[:, 1:2], o, ALU.mult, ALU.add))
        L.settle()
        nc.vector.scalar_tensor_tensor(o, p[:, 2 * N_HD:3 * N_HD], c[:, 2:3], o, ALU.mult, ALU.add).then_inc(bk.free_sem(st), 1)
        vec.wait_ge(*bk.released(st))
        vec.sem_inc(s_comb, 1)

    def vec_nsa_o(vec, L, st):
        u = st[1]
        vec.wait_ge(*bk.filled(st))
        vec.wait_ge(*bk.released(("tile", 3, "nz", u // 8)))
        y = yT[:, 8 + u // 8, :]
        nc.vector.tensor_tensor(y, ps(st), y, ALU.mult).then_inc(bk.free_sem(st), 1)
        vec.wait_ge(*bk.released(st))
        vec.sem_inc(K.y_done, 1)

    def vec_ml_qk(vec, L, st):
        h = st[1]
        if h >= 1:
            vec.wait_ge(*bk.filled(("ml_u", h - 1), (M_NC - 2, 1)))
        for half in range(2):
            vec.wait_ge(*bk.filled(st, ("n", half)))
            for i in range(2):
                tt = 2 * half + i
                ins = nc.vector.tensor_scalar(kn[:, tt, :], ps(st, ("n", half))[:, i * M_HD:(i + 1) * M_HD], natc(1, tt, h),
                                              M_HD ** -0.5, ALU.mult, ALU.mult)
                if i == 0:
                    L(ins)
            ins.then_inc(bk.free_sem(st, ("n", half)), 1)

    def vec_ml_s(vec, L, st):
        h = st[1]
        vec.wait_ge(*bk.filled(st, "m"))
        if h == 0:
            vec.wait_ge(s_tab, n_tab)
        L(nc.vector.tensor_tensor(E[:, :].rearrange("p (t l) -> p t l", l=P), ps(st, "m").rearrange("p (t l) -> p t l", l=P),
                                  maskbd[:, :].unsqueeze(1).to_broadcast([P, TT, P]), ALU.add))
        L.settle()
        vec.sem_inc(bk.free_sem(st, "m"), 1)
        vec.sem_inc(s_E, 1)
        vec.wait_ge(*bk.filled(st, "w"))
        for e in range(2):
            vec.wait_ge(*bk.released(("ml_qk", h), ("q", e)))
        if h >= 1:
            vec.wait_ge(*bk.filled(("ml_n", h - 1), TT - 1))
        for e in range(2):
            L(nc.vector.tensor_tensor(mqt[:, e, :], mq[:, e, :], ps(st, "w"), ALU.mult))
        L.settle()
        vec.sem_inc(bk.free_sem(st, "w"), 1)
        vec.sem_inc(s_qt, 1)
        vec.wait_ge(s_Ee, TT * (h + 1))
        vec.wait_ge(*bk.filled(st, "s"))
        nc.vector.tensor_tensor(Pm[:, :], ps(st, "s"), E[:, :], ALU.mult).then_inc(bk.free_sem(st, "s"), 1)
        vec.wait_ge(*bk.released(st, "s"))
        vec.sem_inc(s_Pm, 1)

    def vec_ml_u(vec, L, st):
        h = st[1]
        if h >= 1:
            vec.wait_ge(*bk.filled(("ml_n", h - 1), TT - 1))
        for c in range(M_NC - 1):
            for d in range(2):
                vec.wait_ge(*bk.filled(st, (c, d)))
                u = ps(st, (c, d))[:, 0:M_HD + 1]
                if c == 0:
                    ins = nc.vector.tensor_copy(Cst[:, d, :], u)
                else:
                    vec.wait_ge(s_C, 14 * h + 2 * (c - 1) + d + 1)
                    ins = nc.vector.scalar_tensor_tensor(Cst[:, 2 * c + d, :], Cst[:, 2 * (c - 1) + d, :], decb[:, h, c:c + 1], u,
                                                         ALU.mult, ALU.add)
                ins.then_inc(s_C, 1)
                vec.wait_ge(s_C, 14 * h + 2 * c + d + 1)
                vec.sem_inc(bk.free_sem(st, (c, d)), 1)

    def vec_ml_n(vec, L, st):
        h = st[1]
        if h >= 1:
            vec.wait_ge(*bk.filled(("ml_t", h - 1), 1))
        for tt in range(TT):
            vec.wait_ge(*bk.filled(st, tt))
            o = ps(st, tt)
            r1 = rden[:, tt:tt + 1]
            L(nc.vector.tensor_scalar(r1, o[:, M_HD:M_HD + 1], -1.0, natc(2, tt, h), ALU.mult, ALU.max))
            L.settle()
            L(nc.vector.tensor_tensor(r1, o[:, M_HD:M_HD + 1], r1, ALU.max))
            L.settle()
            L(nc.vector.reciprocal(r1, r1))
            L.settle()
            nc.vector.tensor_scalar(hbuf[:, tt, :], o[:, 0:M_HD], r1, None, ALU.mult).then_inc(bk.free_sem(st, tt), 1)
            vec.wait_ge(*bk.released(st, tt))
            L(nc.vector.bn_stats(st6[:, tt, :], hbuf[:, tt, :]))
            L.settle()
            nc.vector.bn_aggr(mv2[:, tt, :], st6[:, tt, :]).then_inc(s_var, 1)
            vec.wait_ge(s_var, TT * h + tt + 1)
        for tt in range(TT):
            vec.wait_ge(s_std, TT * h + tt + 1)
            L(nc.vector.reciprocal(mv2[:, tt, 1:2], mv2[:, tt, 1:2]))
            L.settle()
            nc.vector.tensor_scalar(hbuf[:, tt, :], hbuf[:, tt, :], mv2[:, tt, 0:1], mv2[:, tt, 1:2], ALU.subtract,
                                    ALU.mult).then_inc(s_hn, 1)
        vec.wait_ge(s_hn, TT * (h + 1))

    def vec_ml_t(vec, L, st):
        h = st[1]
        for j in range(2):
            i = 2 * h + j
            vec.wait_ge(*bk.filled(st, j))
            vec.wait_ge(*bk.released(("tile", 3, "mo", i)))
            y = yt[:, :]
            nc.vector.scalar_tensor_tensor(y, ps(st, j), nw[:, i:i + 1], so[:, i % 4, :], ALU.mult, ALU.mult).then_inc(bk.free_sem(st, j), 1)
            vec.wait_ge(*bk.released(st, j))
            nc.vector.scalar_tensor_tensor(y, xc[:, i % 4, :], skip[:, i:i + 1], y, ALU.mult, ALU.add).then_inc(s_y, 1)
            vec.wait_ge(s_y, i + 1)
            vec.wait_ge(*bk.released(("tile", 3, "mz", i)))
            nc.vector.tensor_tensor(yT[:, i, :], y, yT[:, i, :], ALU.mult).then_inc(K.y_done, 1)
            vec.wait_ge(K.y_done, K.y_base[3] + 8 + i + 1)

    def pe_wo_gate(pe, st):
        n = st[2]
        bk.take(pe, st, "g")
        for j in range(4):
            c = 2 * KT + 4 * n + j
            mm = nc.tensor.matmul(ps(st, "g")[:, j * P:(j + 1) * P], lhsT=K.mod[:, c:c + 1].to_broadcast([P, P]),
                                  rhs=K.ident[:, :], start=True, stop=True)
        mm.then_inc(bk.full_sem(st, "g"), 1)

    gate_sb = K.work[:, 3 * D:4 * D]
    s_gsb = K.sem("gate_row_ready")

    def act_wo_gate(act, L, st):
        n = st[2]
        act.wait_ge(*bk.filled(st, "g"))
        if n == 0:
            act.wait_ge(K.y_done, K.y_base[3] + KT)
        nc.scalar.activation(gate_sb[:, n * NC:(n + 1) * NC], ps(st, "g"), ACT.Copy).then_inc(bk.free_sem(st, "g"), 1)

    def vec_wo(vec, L, st):
        n = st[2]
        if n == 0:
            vec.wait_ge(s_back, 16 * TT)
        vec.wait_ge(*bk.released(("wo_gate", 3, n), "g"))
        for tt in range(TT):
            vec.wait_ge(*bk.filled(st, tt))
            xs = X[:, tt, n * NC:(n + 1) * NC]
            t = K.work[:, tt * NC:(tt + 1) * NC]
            L(nc.vector.tensor_tensor(t, ps(st, tt), gate_sb[:, n * NC:(n + 1) * NC], ALU.mult))
            L.settle()
            nc.vector.tensor_tensor(xs, xs, t, ALU.add).then_inc(bk.free_sem(st, tt), 1)

    def vec_final(vec, L, st):
        tt = st[2]
        K.vec_rstd(vec, L, st)
        vec.wait_ge(s_fg, 16)
        nc.vector.scalar_tensor_tensor(X[:, tt, :], X[:, tt, :], K.rstd[:, tt:tt + 1], K.work[:, 2 * D:3 * D], ALU.mult,
                                       ALU.mult).then_inc(K.x_done, 1)

    s_hn_done, hn_done = K.s_hn, TT * (K.blocks.index(3) + 1) + (MEM // P if 1 in K.blocks else 0)
    gi = [n for n, st in enumerate(script) if st[0] == "wo"][0]
    for n in range(4):
        script.insert(gi, ("wo_gate", 3, 3 - n))
    for n in range(4):
        K.uses[("wo_gate", 3, n)] = [("g", "S", 1)]
    script.insert(script.index(("norm", 3, TT - 1)) + 1, ("b3_tables", 0))
    w1 = [T[f"n_w1_{c}_3"][0].rearrange("(l d) h -> d l h", d=N_HD) for c in "kv"]
    K.slot_src["cmp"] = lambda st, sub, ap: [
        (ap[64 * b:64 * b + 64, :].rearrange("p (l h) -> p l h", h=C_HID), w1[b][:, 8 * sub:8 * sub + 8, :]) for b in range(2)]
    K.slot_src["ml_qk"] = lambda st, sub, ap: [
        (ap[:, 512 * m:512 * m + 512].rearrange("p (k e) -> p k e", e=M_HD),
         T[n][0, st[1]].rearrange("(k p) e -> p k e", p=P)) for m, n in enumerate(("m_wq_3", "m_wk_3"))]
    K.slot_count["cmp"], K.slot_count["ml_qk"] = 4, 1
    K.slot_used["cmp"] = lambda st, sub: bk.filled(st, 1)
    K.slot_used["ml_qk"] = lambda st, sub: bk.filled(st, ("n", 1))
    K.mix_parts[3] = (K.A_parts.rearrange("p (k t) -> p k t", t=SEQ), K.B_parts.rearrange("p (k t) -> p k t", t=SEQ))
    K.wo_src[3] = (T["w_out_3"][0], yT)
    K.y_base[3] = K.y_count
    K.y_count += KT
    K.params.append(pool_params)
    K.wait_gain[3] = wait_gain
    K.tiles[MZ[0]]["wait"] = lambda pe: pe.wait_ge(s_whole, 1)
    K.stage("pool", norm3=pool_norm, tile3=pool_tile, b3_tables=pool_tables, wo3=pool_wo)
    K.stage("pe", turn=pe_turn, mg_rows=pe_mg_rows, mg_nat=pe_mg_nat, cmp=pe_cmp, cmp2=pe_cmp2, nsa_s=pe_nsa_s, nsa_t=pe_nsa_t,
            nsa_v=pe_nsa_v, nsa_o=pe_nsa_o, ml_qk=pe_ml_qk, ml_s=pe_ml_s, ml_u=pe_ml_u, ml_n=pe_ml_n, ml_t=pe_ml_t,
            wo_gate=pe_wo_gate)
    K.stage("act", tile3=act_tile, turn=act_turn, mg_rows=act_mg_rows, cmp=act_cmp, cmp2=act_cmp2, nsa_s=act_nsa_s, nsa_t=act_nsa_t,
            ml_qk=act_ml_qk, ml_s=act_ml_s, ml_n=act_ml_n, wo_gate=act_wo_gate, final3=K.act_rstd_x)
    K.stage("vec", tile3=vec_tile, h_whole=vec_h_whole, mg_rows=vec_mg_rows, mg_nat=vec_mg_nat, cmp=vec_cmp, nsa_s=vec_nsa_s, nsa_t=vec_nsa_t,
            nsa_v=vec_nsa_v, nsa_o=vec_nsa_o, ml_qk=vec_ml_qk, ml_s=vec_ml_s, ml_u=vec_ml_u, ml_n=vec_ml_n, ml_t=vec_ml_t,
            wo3=vec_wo, final3=vec_final)
    return script


BLOCKS = {1: block1, 2: block2, 3: block3}
WORK = 19000
PAR = 656


class Kit:

    def __init__(self, nc, ctx, T):
        self.nc, self.ctx, self.T = nc, ctx, T
        self.at = {"pe": {}, "act": {}, "vec": {}, "pool": {}}
        self.uses, self.tiles, self.params = {}, {}, []
        self.norm_gain, self.par_count, self.wo_src = {}, {}, {}
        self.y_base, self.y_count = {}, 0
        self.slot_src, self.slot_count, self.slot_used = {}, {"wo": 8}, {}
        self.const_loads, self.wait_gain, self.par_at = [], {}, 0
        self.sp_start, self.mix_parts, self.norm_parts, self.norm_parts_wait = [], {}, {}, {}

    def keep(self, *dims):
        n = math.prod(dims)
        ap = self.par[:, self.par_at:self.par_at + n]
        self.par_at += n
        assert self.par_at <= PAR
        return ap.rearrange("p (a b) -> p a b", b=dims[1]) if len(dims) == 2 else ap

    def sb(self, name, *dims, dt=F32):
        return self.ctx.enter_context(self.nc.sbuf_tensor(name, [P, *dims], dt))

    def sem(self, name):
        return self.ctx.enter_context(self.nc.semaphore(name))

    def arena(self, start=0, base=None):
        at = [start]
        region = self.work if base is None else base

        def take(name, *dims):
            n = math.prod(dims)
            ap = region[:, at[0]:at[0] + n]
            at[0] += n
            assert at[0] <= region.shape[1], (name, at[0])
            if len(dims) == 2:
                ap = ap.rearrange("p (a b) -> p a b", b=dims[1])
            elif len(dims) == 3:
                ap = ap.rearrange("p (a b c) -> p a b c", b=dims[1], c=dims[2])
            return ap
        take.at = at
        return take

    def stage(self, eng, **fns):
        self.at[eng].update(fns)

    def tile(self, st, srcs, mode, w, act, n, kt=KT, bias=None, after=(), readers=1, lo=None,
             lo_from=0, full=None):
        self.tiles[st] = dict(srcs=srcs, mode=mode, w=w, act=act, n=n, kt=kt, bias=bias, after=list(after),
                              readers=readers, lo=lo, per=SLOT // max(w, P), lo_from=lo_from, full=full)

    def rounded(self, name, *dims):
        with self.nc.sbuf_tensor(name, [P, *dims], F32) as t:
            pass
        return t, self.sb(name + "_parts", *dims, dt=F32R)

    def after_norm(self, st, blk, rows=TT):
        self.tiles[st]["after"] += [(("norm", blk, tt), k4) for tt in range(rows) for k4 in range(KT // 4)]


def build(nc, T, out, blocks):
    with ExitStack() as ctx:
        K = Kit(nc, ctx, T)
        A, K.A_parts = K.rounded("A", KT * SEQ)
        B, K.B_parts = K.rounded("B", KT * SEQ)
        K.A, K.B = A, B
        K.A_kt = A.rearrange("p (k t) -> p k t", t=SEQ)
        K.B_kt = B.rearrange("p (k t) -> p k t", t=SEQ)
        K.memT = None
        X, K.X_parts = K.rounded("X", TT, D)
        K.X = X
        ring, ring_lo = K.rounded("ring", RING, SLOT)
        ring_hi = K.sb("ring_hi", RING, SLOT, dt=F32R)
        K.work, K.work_parts = K.rounded("work", WORK)
        K.ident = K.sb("ident", P)
        K.ones = K.sb("ones", P)
        K.reset = K.sb("reset", SEQ)
        K.eps = K.sb("eps", 1)
        K.rstd = K.sb("rstd", TT)
        K.blocks, K.modulated = list(blocks), False
        K.par = K.sb("par", PAR)
        K.hn = K.work[:, 0:2 * D].rearrange("p (a d) -> p a d", d=D)
        K.hn_junk = K.hn[:, 1, :]
        banks = [ctx.enter_context(nc.psum_tensor(f"bank{i}", [P, NC], F32)) for i in range(8)]

        full = [K.sem(f"bank{i}_full") for i in range(8)]
        free = [K.sem(f"bank{i}_free") for i in range(8)]
        K.bk = bk = Banks(full, free)
        loaded = [K.sem(f"slot{i}_loaded") for i in range(RING)]
        part_used = K.sem("part_of_stage_used")
        s_hi, s_lo = K.sem("weight_upper_ready"), K.sem("weight_lower_ready")
        s_yhi, s_ylo = K.sem("mix_upper_ready"), K.sem("mix_lower_ready")
        K.s_const = K.sem("constants_ready")
        s_made = K.sem("constants_made")
        K.s_x = s_x = [K.sem(f"x_rows{tt}_loaded") for tt in range(TT)]
        K.s_hn = s_hn = K.sem("normed_rows_ready")
        K.s_ss = s_ss = K.sem("square_sums_ready")
        K.s_ms = s_ms = K.sem("mean_squares_ready")
        K.s_rt = s_rt = K.sem("root_ready")
        K.s_rstd = s_rstd = K.sem("rstd_ready")
        K.y_done = K.sem("mixed_tile_done")
        K.x_done = K.sem("x_rows_done")
        s_out = K.sem("rows_stored")
        act_step, vec_step = K.sem("act_step"), K.sem("vec_step")
        K.act_step, K.vec_step = act_step, vec_step
        K.ps = lambda st, key=0: banks[bk.bank(st, key)][:, :]

        norms = {}
        K.norms = norms

        def act_rstd(act, L, st, src, junk):
            i = norms[st]
            nc.scalar.activation(junk, src, ACT.Square, accum_out=K.rstd[:, st[2]:st[2] + 1]).then_inc(s_ss, 1)
            act.wait_ge(s_ms, i + 1)
            tt = st[2]
            nc.scalar.activation(K.rstd[:, tt:tt + 1], K.rstd[:, tt:tt + 1], ACT.Sqrt).then_inc(s_rt, 1)

        def vec_rstd(vec, L, st):
            i, tt = norms[st], st[2]
            vec.wait_ge(s_ss, i + 1)
            r1 = K.rstd[:, tt:tt + 1]
            nc.vector.tensor_scalar(r1, r1, 1.0 / D, EPS, ALU.mult, ALU.add).then_inc(s_ms, 1)
            vec.wait_ge(s_rt, i + 1)
            nc.vector.reciprocal(r1, r1).then_inc(s_rstd, 1)
            vec.wait_ge(s_rstd, i + 1)
        K.vec_rstd = vec_rstd

        def act_rstd_x(act, L, st):
            _, blk, tt = st
            if tt == 0:
                act.wait_ge(*bk.filled(("wo", blk, 3), 3))
            act.wait_ge(*bk.released(("wo", blk, 3), tt))
            act_rstd(act, L, st, X[:, tt, :], K.hn_junk)
            act.wait_ge(s_ss, norms[st] + 1)
        K.act_rstd, K.act_rstd_x = act_rstd, act_rstd_x

        block_of = BLOCKS
        script = []
        for b in blocks:
            part = block_of[b](K)
            if b == 2 and 3 in blocks:
                modulation(K)
                K.modulated = True
                part = deal(part, ada_stages())
            script += part
        for st in script:
            if st[0] in ("norm", "final"):
                norms[st] = len(norms)
        normed = [st for st in script if st[0] == "norm"]
        hn_at = {st: n for n, st in enumerate(normed)}
        for blk in blocks:
            i = script.index(("wo", blk, 0))
            script[i:i] = [("mix_parts", blk, g) for g in range(KT // 2)]

        def slot_subs(st):
            return K.tiles[st]["kt"] // K.tiles[st]["per"] if st[0] == "tile" else K.slot_count.get(st[0], 0)

        def is_split(st, sub):
            if st[0] != "tile":
                return st[0] == "wo"
            t = K.tiles[st]
            return t["lo"] is not None and sub * t["per"] >= t["lo_from"]

        before, ahead, stage_at, slots = script[0], {}, {script[0]: 0}, []
        for n, st in enumerate(script):
            subs = slot_subs(st)
            for sub in range(subs):
                slots.append((st, sub))
                stage_at[st] = n
                if is_split(st, sub):
                    target = st if sub >= 2 else before
                    assert len(slots) <= RING or stage_at[slots[-1 - RING][0]] <= stage_at[target]
                    ahead.setdefault(target, []).append(("split", st, sub))
            if subs:
                before = st
        script = [s_ for st in script for s_ in ahead.get(st, []) + [st]]
        split_no = {st[1:]: n for n, st in enumerate([st for st in script if st[0] == "split"])}

        for st in script:
            if st[0] == "norm":
                for k4 in range(KT // 4):
                    bk.plan(st, k4, "S")
            elif st[0] == "tile":
                t = K.tiles[st]
                for half in range(2 if t["mode"] == "N" and t["w"] > P else 1):
                    bk.plan(st, half, "P", t["readers"])
            elif st[0] == "wo":
                for tt in range(TT):
                    bk.plan(st, tt, (st[2] % 2) * 4 + tt)
            for key, pool, readers in K.uses.get(st, []):
                bk.plan(st, key, pool, readers)
        slot_of, slot_value, slot_view, count, loads = {}, {}, {}, [0] * RING, []
        parts = 0
        for n, (st, sub) in enumerate(slots):
            i = n % RING
            if st[0] == "tile":
                t = K.tiles[st]
                view = lambda r, i=i, t=t: r[:, i, :].rearrange("p (k c) -> p k c", c=max(t["w"], P))[:, :, 0:t["w"]]
                dmas, at = [], 0
                for w, c0, width in t["srcs"]:
                    k0 = sub * t["per"]
                    dmas.append((view(ring)[:, :, at:at + width],
                                 w[k0 * P:(k0 + t["per"]) * P, c0:c0 + width].rearrange("(k p) c -> p k c", p=P)))
                    at += width
                last = bk.filled(st, 1 if t["mode"] == "N" and t["w"] > P else 0)
                subs = slot_subs(st)
            elif st[0] in K.slot_src:
                view = lambda r, i=i: r[:, i, :]
                dmas = K.slot_src[st[0]](st, sub, ring[:, i, :])
                last, subs = K.slot_used[st[0]](st, sub), 1
            else:
                w = K.wo_src[st[1]][0]
                view = lambda r, i=i: r[:, i, :].rearrange("p (k c) -> p k c", c=NC)
                dmas = [(view(ring), w[sub * 2 * P:(sub + 1) * 2 * P, st[2] * NC:(st[2] + 1) * NC].rearrange("(k p) c -> p k c", p=P))]
                last, subs = bk.filled(st, 3), 8
            if sub < subs - 1 and st[0] not in K.slot_src:
                parts += 1
                used = (part_used, parts)
            else:
                used = last
            count[i] += 16 * len(dmas)
            slot_of[st, sub], slot_value[st, sub], slot_view[st, sub] = i, count[i], view
            loads.append((i, dmas, used))
        K.slot_ap = lambda st, sub=0: slot_view[st, sub](ring)
        mix_no = {st: n for n, st in enumerate([st for st in script if st[0] == "mix_parts"])}
        K.slot_loaded = lambda st, sub=0: (loaded[slot_of[st, sub]], slot_value[st, sub])
        x_after = {blk: (g + 1) * TT for g, blk in enumerate(blocks)}
        x_total = TT * len(blocks)

        def by_block(st):
            return st[0] + str(st[1]) if st[0] in ("norm", "tile", "final", "wo") else st[0]

        def columns(ap, kk, tt=None):
            if isinstance(ap, tuple):
                ap, kk = ap[kk // 8], kk % 8
            if len(ap.shape) == 4:
                return ap[:, :, kk, :] if tt is None else ap[:, tt, kk, :]
            return ap[:, kk, :] if tt is None else ap[:, kk, tt * P:(tt + 1) * P]

        block = ctx.enter_context(nc.Block())

        @block.sync
        def _(sp):
            for tt in range(TT):
                sp.dma_start(X[:, tt, :], T["x"][0, tt * P:(tt + 1) * P, :]).then_inc(s_x[tt], 16)
            for fn in K.sp_start:
                fn(sp)
            for n, (i, dmas, _) in enumerate(loads):
                if n >= RING:
                    sp.wait_ge(*loads[n - RING][2])
                for dst, src in dmas:
                    sp.dma_start(dst, src).then_inc(loaded[i], 16)
            for tt in range(TT):
                sp.wait_ge(K.x_done, x_total - TT + tt + 1)
                sp.dma_start(out[0, tt * P:(tt + 1) * P, :], X[:, tt, :]).then_inc(s_out, 16)
            sp.wait_ge(s_out, 16 * TT)

        @block.gpsimd
        def _(pool):
            pool.dma_start(K.ident[:, :], T["c_ident"]).then_inc(K.s_const, 16)
            pool.dma_start(K.reset[:, :], T["c_reset"].partition_broadcast(P)).then_inc(K.s_const, 16)
            for extra in K.const_loads:
                pool.dma_start(*extra).then_inc(K.s_const, 16)
            nc.gpsimd.memset(K.ones[:, :], 1.0).then_inc(s_made, 1)
            nc.gpsimd.memset(K.eps[:, :], EPS).then_inc(s_made, 1)
            for fn in K.params:
                fn(pool)
            for st in script:
                if by_block(st) in K.at["pool"]:
                    K.at["pool"][by_block(st)](pool, st)

        const_total = 16 * (2 + len(K.const_loads))

        @block.tensor
        def _(pe):
            pe.wait_ge(K.s_const, const_total)
            pe.wait_ge(s_made, 2)
            for st in script:
                if st[0] == "norm":
                    pe.wait_ge(s_hn, hn_at[st] + 1)
                    for k4 in range(KT // 4):
                        bk.take(pe, st, k4)
                        for j in range(4):
                            kk = 4 * k4 + j
                            mm = nc.tensor.transpose(K.ps(st, k4)[:, j * P:(j + 1) * P],
                                                     K.hn[:, hn_at[st] % 2, kk * P:(kk + 1) * P], K.ident[:, :])
                        mm.then_inc(bk.full_sem(st, k4), 1)
                elif st[0] == "tile":
                    t = K.tiles[st]
                    if t.get("wait"):
                        t["wait"](pe)
                    for dep in t["after"]:
                        pe.wait_ge(*bk.released(*dep))
                    for half in range(2 if t["mode"] == "N" and t["w"] > P else 1):
                        bk.take(pe, st, half)
                    subs, w, per = slot_subs(st), t["w"], t["per"]
                    if t["bias"] is not None:
                        for tt in range(t["n"] // P):
                            nc.tensor.matmul(K.ps(st)[:, tt * P:tt * P + w], lhsT=K.ones[0:1, :], rhs=t["bias"],
                                             start=(tt == 0), stop=False, skip_group_check=True)
                    for sub in range(subs):
                        split = is_split(st, sub)
                        if split:
                            pe.wait_ge(s_lo, split_no[st, sub] + 1)
                            hi, lo = slot_view[st, sub](ring_hi), slot_view[st, sub](ring_lo)
                        else:
                            pe.wait_ge(*K.slot_loaded(st, sub))
                            hi = slot_view[st, sub](ring)
                        for j in range(per):
                            kk = sub * per + j
                            passes = [(hi, t["act"]), (hi, t["lo"]), (lo, t["act"])] if split else \
                                [(hi, t["act"] if t["full"] is None else t["full"])]
                            for n, (wp, ap) in enumerate(passes):
                                first = kk == 0 and n == 0
                                end = kk == t["kt"] - 1 and n == len(passes) - 1
                                if t["mode"] == "T":
                                    mm = nc.tensor.matmul(K.ps(st)[0:w, 0:t["n"]], lhsT=wp[:, j, :], rhs=columns(ap, kk),
                                                          start=first, stop=end)
                                else:
                                    for tt in range(t["n"] // P):
                                        if w > P:
                                            o = K.ps(st, tt // 2)[:, (tt % 2) * w:(tt % 2 + 1) * w]
                                        else:
                                            o = K.ps(st)[:, tt * P:tt * P + w]
                                        opens = tt % 2 == 0 if w > P else tt == 0
                                        mm = nc.tensor.matmul(o, lhsT=columns(ap, kk, tt), rhs=wp[:, j, :],
                                                              start=first and opens and t["bias"] is None, stop=end, skip_group_check=True)
                                        if end and w > P and tt == 1:
                                            mm.then_inc(bk.full_sem(st, 0), 1)
                        if sub < subs - 1:
                            mm.then_inc(part_used, 1)
                    mm.then_inc(bk.full_sem(st, 1 if t["mode"] == "N" and w > P else 0), 1)
                elif st[0] == "wo":
                    _, blk, n = st
                    yhi, ylo = K.mix_parts[blk]
                    for tt in range(TT):
                        bk.take(pe, st, tt)
                    for sub in range(8):
                        pe.wait_ge(s_ylo, mix_no["mix_parts", blk, sub] + 1)
                        pe.wait_ge(s_lo, split_no[st, sub] + 1)
                        hi, lo = slot_view[st, sub](ring_hi), slot_view[st, sub](ring_lo)
                        for j in range(2):
                            kk = 2 * sub + j
                            for tt in range(TT):
                                rows = slice(tt * P, (tt + 1) * P)
                                for m, (y, w) in enumerate(((yhi, hi), (yhi, lo), (ylo, hi))):
                                    mm = nc.tensor.matmul(K.ps(st, tt), lhsT=y[:, kk, rows], rhs=w[:, j, :],
                                                          start=(kk == 0 and m == 0), stop=(kk == KT - 1 and m == 2),
                                                          skip_group_check=True)
                                if kk == KT - 1:
                                    mm.then_inc(bk.full_sem(st, tt), 1)
                        if sub < 7:
                            mm.then_inc(part_used, 1)
                elif st[0] in K.at["pe"]:
                    K.at["pe"][st[0]](pe, st)

        @block.scalar
        def _(act):
            L = Lane(act, act_step)
            act.wait_ge(K.s_const, const_total)
            act.wait_ge(s_made, 2)
            for st in script:
                if st[0] == "norm":
                    _, blk, tt = st
                    rows = K.mem_rows[:, tt, :] if blk == "mem" else X[:, tt, :]
                    if blk == "mem":
                        act.wait_ge(K.s_mem, 16 * (MEM // P))
                    elif blk == blocks[0]:
                        act.wait_ge(s_x[tt], 16)
                    else:
                        act.wait_ge(K.x_done, x_after[blk - 1] - TT + tt + 1)
                    n = hn_at[st]
                    if n >= 2:
                        act.wait_ge(*bk.filled(normed[n - 2], KT // 4 - 1))
                    act_rstd(act, L, st, rows, K.hn[:, n % 2, :])
                    act.wait_ge(s_rstd, norms[st] + 1)
                    nc.scalar.activation(K.hn[:, n % 2, :], rows, ACT.Copy, scale=K.rstd[:, tt:tt + 1]).then_inc(s_hn, 1)
                elif st[0] == "split":
                    key = st[1:]
                    act.wait_ge(*K.slot_loaded(*key))
                    nc.scalar.activation(slot_view[key](ring_hi), slot_view[key](ring), ACT.Copy).then_inc(s_hi, 1)
                elif st[0] == "mix_parts":
                    _, blk, g = st
                    act.wait_ge(K.y_done, K.y_base[blk] + KT)
                    yT = K.wo_src[blk][1]
                    nc.scalar.activation(K.mix_parts[blk][0][:, 2 * g:2 * g + 2, :], yT[:, 2 * g:2 * g + 2, :],
                                         ACT.Copy).then_inc(s_yhi, 1)
                elif by_block(st) in K.at["act"]:
                    K.at["act"][by_block(st)](act, L, st)

        @block.vector
        def _(vec):
            L = Lane(vec, vec_step)
            K.vlane = [L]
            vec.wait_ge(K.s_const, const_total)
            vec.wait_ge(s_made, 2)
            for st in script:
                if st[0] == "norm":
                    _, blk, tt = st
                    vec_rstd(vec, L, st)
                    gain, shift = K.norm_gain[blk]
                    dst = {"mem": K.memT, 2: K.B_kt}.get(blk, K.A_kt)
                    if tt == 0:
                        K.wait_gain[blk](vec)
                    parts = K.norm_parts.get(blk)
                    if parts:
                        K.norm_parts_wait[blk](vec, tt)
                    for k4 in range(KT // 4):
                        vec.wait_ge(*bk.filled(st, k4))
                        if parts and shift is not None:
                            four, cols = slice(4 * k4, 4 * k4 + 4), slice(tt * P, (tt + 1) * P)
                            hi, (whole, lo) = parts[0][:, four, cols], (v[k4 // 2][:, 4 * (k4 % 2):4 * (k4 % 2) + 4, cols] for v in parts[1:])
                            b = K.ps(st, k4).rearrange("p (k t) -> p k t", t=P)
                            L(nc.vector.tensor_tensor(whole, b, gain[:, four].unsqueeze(2).to_broadcast([P, 4, P]), ALU.mult))
                            L.settle()
                            L(nc.vector.tensor_tensor(whole, whole, shift[:, four].unsqueeze(2).to_broadcast([P, 4, P]), ALU.add))
                            L.settle()
                            L(nc.vector.tensor_copy(hi, whole))
                            L.settle()
                            nc.vector.tensor_tensor(lo, whole, hi, ALU.subtract).then_inc(bk.free_sem(st, k4), 1)
                            continue
                        if parts:
                            hi, lo = parts[0][:, 4 * k4:4 * k4 + 4, tt * P:(tt + 1) * P], parts[1]
                            b = K.ps(st, k4).rearrange("p (k t) -> p k t", t=P)
                            L(nc.vector.tensor_tensor(hi, b, gain[:, 4 * k4:4 * k4 + 4].unsqueeze(2).to_broadcast([P, 4, P]),
                                                      ALU.mult))
                            L.settle()
                            for j in range(4):
                                kk = 4 * k4 + j
                                ins = nc.vector.scalar_tensor_tensor(lo[:, tt, kk, :], b[:, j, :], gain[:, kk:kk + 1],
                                                                     hi[:, j, :], ALU.mult, ALU.subtract)
                                if j < 3:
                                    L(ins)
                            ins.then_inc(bk.free_sem(st, k4), 1)
                            continue
                        o = dst[:, 4 * k4:4 * k4 + 4, tt * P:(tt + 1) * P]
                        g4 = gain[:, 4 * k4:4 * k4 + 4].unsqueeze(2).to_broadcast([P, 4, P])
                        b = K.ps(st, k4).rearrange("p (k t) -> p k t", t=P)
                        if shift is None:
                            nc.vector.tensor_tensor(o, b, g4, ALU.mult).then_inc(bk.free_sem(st, k4), 1)
                        else:
                            L(nc.vector.tensor_tensor(o, b, g4, ALU.mult))
                            L.settle()
                            s4 = shift[:, 4 * k4:4 * k4 + 4].unsqueeze(2).to_broadcast([P, 4, P])
                            nc.vector.tensor_tensor(o, o, s4, ALU.add).then_inc(bk.free_sem(st, k4), 1)
                elif st[0] == "split":
                    key = st[1:]
                    vec.wait_ge(s_hi, split_no[key] + 1)
                    nc.vector.tensor_tensor(slot_view[key](ring_lo), slot_view[key](ring), slot_view[key](ring_hi),
                                            ALU.subtract).then_inc(s_lo, 1)
                elif st[0] == "mix_parts":
                    _, blk, g = st
                    vec.wait_ge(s_yhi, mix_no[st] + 1)
                    yhi, ylo = K.mix_parts[blk]
                    two = slice(2 * g, 2 * g + 2)
                    nc.vector.tensor_tensor(ylo[:, two, :], K.wo_src[blk][1][:, two, :], yhi[:, two, :],
                                            ALU.subtract).then_inc(s_ylo, 1)
                elif by_block(st) in K.at["vec"]:
                    K.at["vec"][by_block(st)](vec, L, st)


def constants():
    import numpy as np
    c = {"c_ident": np.eye(P, dtype=np.float32)}
    q, j = np.arange(P)[:, None], np.arange(SEQ)[None, :]
    c["c_ndist"] = np.where(j - (SEQ - P) <= q, j - (SEQ - P) - q, NEG).astype(np.float32)
    s, l = np.arange(P)[:, None], np.arange(P)[None, :]
    c["c_maskbd"] = np.where((s // 64 == l // 64) & (s <= l), 0.0, NEG).astype(np.float32)
    n = np.arange((SEQ - 32) // 16 + 1)
    t = np.arange(TT)[None, :, None] * P + np.arange(P)[:, None, None]
    mid, end = n * 16 + 15.5, n * 16 + 31
    c["c_cdist"] = np.where(end <= t, -(t.astype(np.float32) - mid.astype(np.float32)), NEG).astype(np.float32)
    p = np.arange(P)
    c["c_invf"] = (np.float32(10000.0) ** (-(2 * (p % 32)).astype(np.float32) / np.float32(64)))[:, None].astype(np.float32)
    perm = np.zeros((P, P), np.float32)
    for m in p:
        perm[m + 32 if m % 64 < 32 else m - 32, m] = -1.0 if m % 64 < 32 else 1.0
    c["c_perm"] = perm
    c["c_sgn"] = np.where((p < 64)[:, None], [[-1.0, 1.0]], [[1.0, -1.0]]).astype(np.float32)
    c["c_tri"] = np.where(np.arange(SEQ)[None, :] - (SEQ - P) <= p[:, None], 0.0, NEG).astype(np.float32)
    c["c_reset"] = (np.arange(SEQ) % 64 != 0).astype(np.float32)
    return c


def kernel(**inputs):
    import numpy as np
    import concourse.bacc as bacc
    from concourse.bass_utils import run_bass_kernel_spmd as run

    nc = bacc.Bacc("TRN2", target_bir_lowering=False, num_devices=1)
    arrays, T = {}, {}
    for name, a in {**inputs, **constants()}.items():
        a = np.ascontiguousarray(a)
        arrays[f"in_{name}"] = a
        T[name] = nc.dram_tensor(f"in_{name}", a.shape, mybir.dt.from_np(a.dtype), kind="ExternalInput").ap()
    out = nc.dram_tensor("out_x", (1, SEQ, D), F32, kind="ExternalOutput").ap()
    build(nc, T, out, [b for b, name in ((1, "w_in"), (2, "w_in_2"), (3, "w_in_3")) if name in inputs])
    return run(nc, [arrays], core_ids=[0]).results[0]["out_x"]
```
